# Optimizing a Trainium2 kernel written in Bass

```python
import math
import jax, jax.numpy as jnp
from jax import lax
import numpy as np

D_MODEL = 1024
BATCH = 1
SEQ = 512
DEPTH = 2

DA_HEADS = 8
DA_HEAD_DIM = 64
DA_WIDTH = DA_HEADS * 2 * DA_HEAD_DIM
SSD_WIDTH = D_MODEL
SSD_HEAD_DIM = 64
SSD_HEADS = SSD_WIDTH // SSD_HEAD_DIM
SSD_GROUPS = 2
SSD_STATE = 128
SSD_CONV = 4
SSD_CHUNK = 128
SSD_CONV_DIM = SSD_WIDTH + 2 * SSD_GROUPS * SSD_STATE
SW_HEADS = 16
SW_KV_HEADS = 2
SW_GQ = SW_HEADS // SW_KV_HEADS
SW_HEAD_DIM = 64
SW_WIDTH = SW_HEADS * SW_HEAD_DIM
SW_KV_WIDTH = SW_KV_HEADS * SW_HEAD_DIM
WINDOW = 128
Q_BLOCK = 128
EPS = 1e-5

N_EVEN = (DEPTH + 1) // 2
N_ODD = DEPTH // 2
EVEN_IN = 4 * DA_WIDTH + SSD_WIDTH + SSD_CONV_DIM + SSD_HEADS
EVEN_SPLITS = [DA_WIDTH, 2 * DA_WIDTH, 3 * DA_WIDTH, 4 * DA_WIDTH,
               4 * DA_WIDTH + SSD_WIDTH, 4 * DA_WIDTH + SSD_WIDTH + SSD_CONV_DIM]
ODD_IN = 2 * SW_WIDTH + 2 * SW_KV_WIDTH
ODD_SPLITS = [SW_WIDTH, SW_WIDTH + SW_KV_WIDTH, SW_WIDTH + 2 * SW_KV_WIDTH]


def rmsnorm(x, w):
    xf = x.astype(jnp.float32)
    y = xf * lax.rsqrt(jnp.mean(xf * xf, axis=-1, keepdims=True) + EPS)
    return (y * w.astype(jnp.float32)).astype(x.dtype)

def alibi_slopes(n):
    return jnp.exp2(-8.0 * jnp.arange(1, n + 1, dtype=jnp.float32) / n)

def diff_attention(q, k, v, lam, slopes):
    b, s = q.shape[:2]
    nb = s // Q_BLOCK
    scale = DA_HEAD_DIM ** -0.5
    qb = q.reshape(b, nb, Q_BLOCK, DA_HEADS, 2, DA_HEAD_DIM).transpose(1, 0, 2, 3, 4, 5)
    kpos = jnp.arange(s)

    def block(args):
        qi, n = args
        qpos = n * Q_BLOCK + jnp.arange(Q_BLOCK)
        dist = qpos[:, None] - kpos[None, :]
        logits = jnp.einsum('bqhmd,bshmd->bhmqs', qi, k).astype(jnp.float32) * scale
        logits = logits - slopes[None, :, None, None, None] * dist.astype(jnp.float32)[None, None, None]
        logits = jnp.where((dist >= 0)[None, None, None], logits, -jnp.inf)
        p = jax.nn.softmax(logits, axis=-1)
        attn = p[:, :, 0] - lam * p[:, :, 1]
        return jnp.einsum('bhqs,bshe->bqhe', attn.astype(v.dtype), v)

    out = lax.map(block, (qb, jnp.arange(nb)))
    return out.transpose(1, 0, 2, 3, 4).reshape(b, s, DA_HEADS, 2 * DA_HEAD_DIM)

def causal_dwconv(x, w, bias):
    c = x.shape[-1]
    y = lax.conv_general_dilated(x, w[:, None, :].astype(x.dtype), window_strides=(1,),
                                 padding=[(SSD_CONV - 1, 0)],
                                 dimension_numbers=('NWC', 'WIO', 'NWC'),
                                 feature_group_count=c)
    return y + bias.astype(x.dtype)

def segsum(a):
    cs = jnp.cumsum(a, axis=-1)
    diff = cs[..., :, None] - cs[..., None, :]
    n = a.shape[-1]
    mask = jnp.tril(jnp.ones((n, n), dtype=bool))
    return jnp.where(mask, diff, -jnp.inf)

def ssd_scan(xh, dt, A, bm, cm):
    b, s = xh.shape[:2]
    nc = s // SSD_CHUNK
    hpg = SSD_HEADS // SSD_GROUPS
    dtype = xh.dtype
    xdt = (xh * dt[..., None].astype(dtype)).reshape(b, nc, SSD_CHUNK, SSD_GROUPS, hpg, SSD_HEAD_DIM)
    bc = bm.reshape(b, nc, SSD_CHUNK, SSD_GROUPS, SSD_STATE)
    cc = cm.reshape(b, nc, SSD_CHUNK, SSD_GROUPS, SSD_STATE)
    dA = (dt * A).reshape(b, nc, SSD_CHUNK, SSD_GROUPS, hpg).transpose(0, 1, 3, 4, 2)
    cs = jnp.cumsum(dA, axis=-1)
    lmat = jnp.exp(segsum(dA)).astype(dtype)
    cb = jnp.einsum('bclgn,bcsgn->bcgls', cc, bc)
    y_diag = jnp.einsum('bcgjls,bcsgjp->bclgjp', cb[:, :, :, None] * lmat, xdt)
    decay_states = jnp.exp(cs[..., -1:] - cs).astype(dtype)
    states = jnp.einsum('bclgn,bcgjl,bclgjp->bcgjpn', bc, decay_states, xdt)
    chunk_decay = jnp.exp(cs[..., -1]).astype(dtype)

    def step(h, inp):
        st, dec = inp
        return h * dec[..., None, None] + st, h

    h0 = jnp.zeros((b, SSD_GROUPS, hpg, SSD_HEAD_DIM, SSD_STATE), dtype)
    _, prev = lax.scan(step, h0, (states.transpose(1, 0, 2, 3, 4, 5), chunk_decay.transpose(1, 0, 2, 3)))
    prev = prev.transpose(1, 0, 2, 3, 4, 5)
    y_off = jnp.einsum('bclgn,bcgjpn,bcgjl->bclgjp', cc, prev, jnp.exp(cs).astype(dtype))
    return (y_diag + y_off).reshape(b, s, SSD_HEADS, SSD_HEAD_DIM)

def sliding_window_attention(q, k, v, sinks, slopes):
    b, s = q.shape[:2]
    nb = s // WINDOW
    scale = SW_HEAD_DIM ** -0.5
    qb = q.reshape(b, nb, WINDOW, SW_KV_HEADS, SW_GQ, SW_HEAD_DIM)
    kb = k.reshape(b, nb, WINDOW, SW_KV_HEADS, SW_HEAD_DIM)
    vb = v.reshape(b, nb, WINDOW, SW_KV_HEADS, SW_HEAD_DIM)
    pad = ((0, 0), (1, 0), (0, 0), (0, 0), (0, 0))
    kk = jnp.concatenate([jnp.pad(kb, pad)[:, :-1], kb], axis=2)
    vv = jnp.concatenate([jnp.pad(vb, pad)[:, :-1], vb], axis=2)
    logits = jnp.einsum('bnqkgd,bnskd->bnkgqs', qb, kk).astype(jnp.float32) * scale
    qrel = jnp.arange(WINDOW) + WINDOW
    krel = jnp.arange(2 * WINDOW)
    dist = qrel[:, None] - krel[None, :]
    key_abs = (jnp.arange(nb) * WINDOW - WINDOW)[:, None] + krel[None, :]
    valid = ((dist >= 0) & (dist < WINDOW))[None] & (key_abs >= 0)[:, None, :]
    sl = slopes.reshape(SW_KV_HEADS, SW_GQ)[None, None, :, :, None, None]
    logits = logits - sl * dist.astype(jnp.float32)
    logits = jnp.where(valid[None, :, None, None], logits, -jnp.inf)
    sink = jnp.broadcast_to(sinks.astype(jnp.float32).reshape(SW_KV_HEADS, SW_GQ)[None, None, :, :, None, None],
                            logits.shape[:-1] + (1,))
    p = jax.nn.softmax(jnp.concatenate([logits, sink], axis=-1), axis=-1)[..., :-1]
    out = jnp.einsum('bnkgqs,bnskd->bnqkgd', p.astype(v.dtype), vv)
    return out.reshape(b, s, SW_WIDTH)

def even_layer(h, w_in, conv_w, conv_b, dt_bias, a_log, d_skip, ssd_norm_w,
               lq1, lk1, lq2, lk2, subln_w, w_out, lambda_init):
    b, s, _ = h.shape
    proj = h @ w_in
    q, k, v, g_a, z, xbc, dt_raw = jnp.split(proj, EVEN_SPLITS, axis=-1)
    q = q.reshape(b, s, DA_HEADS, 2, DA_HEAD_DIM)
    k = k.reshape(b, s, DA_HEADS, 2, DA_HEAD_DIM)
    v = v.reshape(b, s, DA_HEADS, 2 * DA_HEAD_DIM)
    f32 = jnp.float32
    lam = (jnp.exp(jnp.sum(lq1.astype(f32) * lk1.astype(f32)))
           - jnp.exp(jnp.sum(lq2.astype(f32) * lk2.astype(f32))) + lambda_init)
    attn = diff_attention(q, k, v, lam, alibi_slopes(DA_HEADS))
    attn = rmsnorm(attn, subln_w) * (1.0 - lambda_init)
    y_a = attn.reshape(b, s, DA_WIDTH) * jax.nn.silu(g_a)
    xbc = jax.nn.silu(causal_dwconv(xbc, conv_w, conv_b))
    xs, bm, cm = jnp.split(xbc, [SSD_WIDTH, SSD_WIDTH + SSD_GROUPS * SSD_STATE], axis=-1)
    xh = xs.reshape(b, s, SSD_HEADS, SSD_HEAD_DIM)
    dt = jax.nn.softplus(dt_raw.astype(f32) + dt_bias.astype(f32))
    A = -jnp.exp(a_log.astype(f32))
    y = ssd_scan(xh, dt, A, bm.reshape(b, s, SSD_GROUPS, SSD_STATE), cm.reshape(b, s, SSD_GROUPS, SSD_STATE))
    y = y + xh * d_skip[:, None].astype(xh.dtype)
    y = y.reshape(b, s, SSD_WIDTH) * jax.nn.silu(z)
    y_b = rmsnorm(y.reshape(b, s, SSD_GROUPS, SSD_WIDTH // SSD_GROUPS),
                  ssd_norm_w.reshape(SSD_GROUPS, SSD_WIDTH // SSD_GROUPS)).reshape(b, s, SSD_WIDTH)
    return jnp.concatenate([y_a, y_b], axis=-1) @ w_out

def odd_layer(h, w_in, b_in, sinks, w_out):
    b, s, _ = h.shape
    proj = h @ w_in + b_in
    q, k, v, g = jnp.split(proj, ODD_SPLITS, axis=-1)
    q = q.reshape(b, s, SW_KV_HEADS, SW_GQ, SW_HEAD_DIM)
    k = k.reshape(b, s, SW_KV_HEADS, SW_HEAD_DIM)
    v = v.reshape(b, s, SW_KV_HEADS, SW_HEAD_DIM)
    o = sliding_window_attention(q, k, v, sinks, alibi_slopes(SW_HEADS))
    return (o * jax.nn.silu(g)) @ w_out

def first_inputs(seed: int = 0) -> dict:
    key = jax.random.key(seed)
    ks = jax.random.split(key, 24)
    f32 = jnp.float32

    def nrm(k, shape, scale):
        return jax.random.normal(k, shape, f32) * scale

    dt0 = jnp.exp(jax.random.uniform(ks[5], (N_EVEN, SSD_HEADS), f32, math.log(1e-3), math.log(1e-1)))
    return {
        "x": nrm(ks[0], (BATCH, SEQ, D_MODEL), 1.0),
        "norm_a": 1.0 + nrm(ks[1], (N_EVEN, D_MODEL), 0.02),
        "w_in_a": nrm(ks[2], (N_EVEN, D_MODEL, EVEN_IN), D_MODEL ** -0.5),
        "conv_w_a": nrm(ks[3], (N_EVEN, SSD_CONV, SSD_CONV_DIM), SSD_CONV ** -0.5),
        "conv_b_a": nrm(ks[4], (N_EVEN, SSD_CONV_DIM), 0.02),
        "dt_bias_a": dt0 + jnp.log(-jnp.expm1(-dt0)),
        "a_log_a": jnp.log(jax.random.uniform(ks[6], (N_EVEN, SSD_HEADS), f32, 1.0, 16.0)),
        "d_skip_a": 1.0 + nrm(ks[7], (N_EVEN, SSD_HEADS), 0.1),
        "ssd_norm_a": 1.0 + nrm(ks[8], (N_EVEN, SSD_WIDTH), 0.02),
        "lambda_q1_a": nrm(ks[9], (N_EVEN, DA_HEAD_DIM), 0.1),
        "lambda_k1_a": nrm(ks[10], (N_EVEN, DA_HEAD_DIM), 0.1),
        "lambda_q2_a": nrm(ks[11], (N_EVEN, DA_HEAD_DIM), 0.1),
        "lambda_k2_a": nrm(ks[12], (N_EVEN, DA_HEAD_DIM), 0.1),
        "subln_a": 1.0 + nrm(ks[13], (N_EVEN, 2 * DA_HEAD_DIM), 0.02),
        "w_out_a": nrm(ks[14], (N_EVEN, DA_WIDTH + SSD_WIDTH, D_MODEL), (DA_WIDTH + SSD_WIDTH) ** -0.5),
        "norm_c": 1.0 + nrm(ks[15], (N_ODD, D_MODEL), 0.02),
        "w_in_c": nrm(ks[16], (N_ODD, D_MODEL, ODD_IN), D_MODEL ** -0.5),
        "b_in_c": nrm(ks[17], (N_ODD, ODD_IN), 0.02),
        "sinks_c": nrm(ks[18], (N_ODD, SW_HEADS), 1.0),
        "w_out_c": nrm(ks[19], (N_ODD, SW_WIDTH, D_MODEL), SW_WIDTH ** -0.5),
        "final_norm": 1.0 + nrm(ks[20], (D_MODEL,), 0.02),
    }

def first_block(x, norm_a, w_in_a, conv_w_a, conv_b_a, dt_bias_a, a_log_a, d_skip_a, ssd_norm_a,
              lambda_q1_a, lambda_k1_a, lambda_q2_a, lambda_k2_a, subln_a, w_out_a,
              norm_c, w_in_c, b_in_c, sinks_c, w_out_c, final_norm):
    for i in range(DEPTH):
        j = i // 2
        if i % 2 == 0:
            lambda_init = 0.8 - 0.6 * math.exp(-0.3 * i)
            x = x + even_layer(rmsnorm(x, norm_a[j]), w_in_a[j], conv_w_a[j], conv_b_a[j],
                               dt_bias_a[j], a_log_a[j], d_skip_a[j], ssd_norm_a[j],
                               lambda_q1_a[j], lambda_k1_a[j], lambda_q2_a[j], lambda_k2_a[j],
                               subln_a[j], w_out_a[j], lambda_init)
        else:
            x = x + odd_layer(rmsnorm(x, norm_c[j]), w_in_c[j], b_in_c[j], sinks_c[j], w_out_c[j])
    return rmsnorm(x, final_norm)


DEPTH_2 = 1

HEAD_DIM = 64
SB_HEADS = 4
DSA_HEADS = 4
NSA_HEADS = 4
BRANCH_WIDTH = 4 * HEAD_DIM
IDX_HEADS = 4
IDX_DIM = 64
DSA_TOPK = 256
CMP_LEN = 32
CMP_STRIDE = 16
CMP_HIDDEN = 128
SEL_LEN = 64
SEL_TOPN = 16
WINDOW_2 = 512
N_MEM = 256
MEM_HEADS = 4
MEM_HEAD_DIM = 64
D_FF = ((8 * D_MODEL + 3 * 256 - 1) // (3 * 256)) * 256
ROPE_THETA = 10000.0
RMS_EPS = 1e-6
FORCED_SCORE = 1e4

IN_SPLITS = (
    ('q_a', SB_HEADS * HEAD_DIM), ('k_a', SB_HEADS * HEAD_DIM), ('v_a', SB_HEADS * HEAD_DIM),
    ('q_b', DSA_HEADS * HEAD_DIM), ('k_b', HEAD_DIM), ('v_b', HEAD_DIM),
    ('q_idx', IDX_HEADS * IDX_DIM), ('k_idx', IDX_DIM), ('w_idx', IDX_HEADS),
    ('q_c', NSA_HEADS * HEAD_DIM), ('k_cmp', HEAD_DIM), ('v_cmp', HEAD_DIM),
    ('k_sel', HEAD_DIM), ('v_sel', HEAD_DIM), ('k_win', HEAD_DIM), ('v_win', HEAD_DIM),
    ('g_c', NSA_HEADS * 3),
    ('g_merge', 3 * D_MODEL),
)
D_IN = sum(w for _, w in IN_SPLITS)


def _rmsnorm(x, g):
    xf = x.astype(jnp.float32)
    y = xf * lax.rsqrt(jnp.mean(xf * xf, axis=-1, keepdims=True) + RMS_EPS)
    return (y * g.astype(jnp.float32)).astype(x.dtype)

def _rope(x):
    S, hd = x.shape[1], x.shape[-1]
    inv = ROPE_THETA ** (-jnp.arange(0, hd, 2, dtype=jnp.float32) / hd)
    ang = jnp.arange(S, dtype=jnp.float32)[:, None] * inv[None, :]
    cos = jnp.cos(ang)[None, :, None, :]
    sin = jnp.sin(ang)[None, :, None, :]
    xf = x.astype(jnp.float32)
    x1, x2 = xf[..., : hd // 2], xf[..., hd // 2:]
    return jnp.concatenate([x1 * cos - x2 * sin, x2 * cos + x1 * sin], axis=-1).astype(x.dtype)

def _masked_softmax(s, mask):
    s = jnp.where(mask, s.astype(jnp.float32), -jnp.inf)
    m = jnp.max(s, axis=-1, keepdims=True)
    m = jnp.where(jnp.isfinite(m), m, 0.0)
    e = jnp.where(mask, jnp.exp(s - m), 0.0)
    den = jnp.sum(e, axis=-1, keepdims=True)
    return e / jnp.maximum(den, 1e-30)

def _sweep(block_fn, S):
    out = lax.map(block_fn, jnp.arange(S // Q_BLOCK))
    out = jnp.moveaxis(out, 0, 1)
    return out.reshape((out.shape[0], S) + out.shape[3:])

def _split_columns(p):
    parts, off = {}, 0
    for name, w in IN_SPLITS:
        parts[name] = p[..., off:off + w]
        off += w
    return parts

def _stick_breaking(q, k, v):
    B, S, H, hd = q.shape
    scale = hd ** -0.5
    kpos = jnp.arange(S)

    def block(i):
        q0 = i * Q_BLOCK
        qpos = q0 + jnp.arange(Q_BLOCK)
        qb = lax.dynamic_slice_in_dim(q, q0, Q_BLOCK, axis=1)
        z = jnp.einsum('bqhd,bkhd->bhqk', qb, k).astype(jnp.float32) * scale
        strict = kpos[None, :] < qpos[:, None]
        log_1m = jnp.where(strict, jax.nn.log_sigmoid(-z), 0.0)
        suffix = lax.cumsum(log_1m, axis=3, reverse=True) - log_1m
        w = jnp.where(strict, jnp.exp(jax.nn.log_sigmoid(z) + suffix), 0.0)
        return jnp.einsum('bhqk,bkhd->bqhd', w.astype(v.dtype), v)

    return _sweep(block, S)

def _dsa_attention(q, k, v, q_idx, k_idx, w_idx):
    B, S, H, hd = q.shape
    topk = min(DSA_TOPK, S // 4)
    kpos = jnp.arange(S)
    bidx = jnp.arange(B)[:, None, None]
    w_scale = (IDX_HEADS * IDX_DIM) ** -0.5
    scale = hd ** -0.5

    def block(i):
        q0 = i * Q_BLOCK
        qpos = q0 + jnp.arange(Q_BLOCK)
        qi = lax.dynamic_slice_in_dim(q_idx, q0, Q_BLOCK, axis=1)
        wi = lax.dynamic_slice_in_dim(w_idx, q0, Q_BLOCK, axis=1).astype(jnp.float32) * w_scale
        rel = jax.nn.relu(jnp.einsum('bqhd,bkd->bqhk', qi, k_idx).astype(jnp.float32))
        score = jnp.einsum('bqh,bqhk->bqk', wi, rel)
        score = jnp.where(kpos[None, None, :] <= qpos[None, :, None], score, -jnp.inf)
        _, sel = lax.top_k(score, topk)
        kg = k[bidx, sel]
        vg = v[bidx, sel]
        qb = lax.dynamic_slice_in_dim(q, q0, Q_BLOCK, axis=1)
        s = jnp.einsum('bqhd,bqkd->bhqk', qb, kg).astype(jnp.float32) * scale
        valid = (sel <= qpos[None, :, None])[:, None]
        p = _masked_softmax(s, valid)
        return jnp.einsum('bhqk,bqkd->bqhd', p.astype(v.dtype), vg)

    return _sweep(block, S)

def _compress(tok, pos_emb, w1, w2):
    B, S, hd = tok.shape
    n_cmp = (S - CMP_LEN) // CMP_STRIDE + 1
    idx = np.arange(n_cmp)[:, None] * CMP_STRIDE + np.arange(CMP_LEN)[None, :]
    blocks = tok[:, idx] + pos_emb
    hid = jax.nn.gelu(blocks.reshape(B, n_cmp, CMP_LEN * hd) @ w1)
    return hid @ w2

def _nsa_attention(q, k_cmp, v_cmp, k_sel, v_sel, k_win, v_win, gates,
                   cmp_pos_k, cmp_w1_k, cmp_w2_k, cmp_pos_v, cmp_w1_v, cmp_w2_v):
    B, S, H, hd = q.shape
    scale = hd ** -0.5
    kc = _compress(k_cmp, cmp_pos_k, cmp_w1_k, cmp_w2_k)
    vc = _compress(v_cmp, cmp_pos_v, cmp_w1_v, cmp_w2_v)
    n_cmp = kc.shape[1]
    cmp_end = jnp.arange(n_cmp) * CMP_STRIDE + CMP_LEN - 1
    n_sel = S // SEL_LEN
    topn = min(SEL_TOPN, n_sel)
    cs = np.arange(n_cmp) * CMP_STRIDE
    ss = np.arange(n_sel) * SEL_LEN
    overlap = jnp.asarray(((cs[:, None] < ss[None, :] + SEL_LEN) &
                           (cs[:, None] + CMP_LEN > ss[None, :])).astype(np.float32))
    k_blocks = k_sel.reshape(B, n_sel, SEL_LEN, hd)
    v_blocks = v_sel.reshape(B, n_sel, SEL_LEN, hd)
    k_pad = jnp.pad(k_win, ((0, 0), (WINDOW_2, 0), (0, 0)))
    v_pad = jnp.pad(v_win, ((0, 0), (WINDOW_2, 0), (0, 0)))
    sel_ids = jnp.arange(n_sel)
    offs = jnp.arange(SEL_LEN)
    band_offs = jnp.arange(WINDOW_2 + Q_BLOCK)
    bidx = jnp.arange(B)[:, None, None]

    def block(i):
        q0 = i * Q_BLOCK
        qpos = q0 + jnp.arange(Q_BLOCK)
        qb = lax.dynamic_slice_in_dim(q, q0, Q_BLOCK, axis=1)
        gb = lax.dynamic_slice_in_dim(gates, q0, Q_BLOCK, axis=1)
        s_c = jnp.einsum('bqhd,bnd->bhqn', qb, kc).astype(jnp.float32) * scale
        p_c = _masked_softmax(s_c, (cmp_end[None, :] <= qpos[:, None])[None, None])
        o_cmp = jnp.einsum('bhqn,bnd->bqhd', p_c.astype(vc.dtype), vc)
        imp = jnp.einsum('bhqn,nj->bqj', p_c, overlap)
        cur = qpos // SEL_LEN
        forced = ((sel_ids[None, :] == 0) | (sel_ids[None, :] == cur[:, None]) |
                  (sel_ids[None, :] == cur[:, None] - 1))
        admissible = sel_ids[None, :] * SEL_LEN <= qpos[:, None]
        imp = jnp.where(forced[None], FORCED_SCORE, imp)
        imp = jnp.where(admissible[None], imp, -jnp.inf)
        _, sel = lax.top_k(imp, topn)
        kg = k_blocks[bidx, sel].reshape(B, Q_BLOCK, topn * SEL_LEN, hd)
        vg = v_blocks[bidx, sel].reshape(B, Q_BLOCK, topn * SEL_LEN, hd)
        tok = (sel[..., None] * SEL_LEN + offs).reshape(B, Q_BLOCK, topn * SEL_LEN)
        s_s = jnp.einsum('bqhd,bqkd->bhqk', qb, kg).astype(jnp.float32) * scale
        p_s = _masked_softmax(s_s, (tok <= qpos[None, :, None])[:, None])
        o_sel = jnp.einsum('bhqk,bqkd->bqhd', p_s.astype(vg.dtype), vg)
        kw = lax.dynamic_slice_in_dim(k_pad, q0, WINDOW_2 + Q_BLOCK, axis=1)
        vw = lax.dynamic_slice_in_dim(v_pad, q0, WINDOW_2 + Q_BLOCK, axis=1)
        wpos = q0 - WINDOW_2 + band_offs
        diff = qpos[:, None] - wpos[None, :]
        wmask = (diff >= 0) & (diff < WINDOW_2) & (wpos[None, :] >= 0)
        s_w = jnp.einsum('bqhd,bkd->bhqk', qb, kw).astype(jnp.float32) * scale
        p_w = _masked_softmax(s_w, wmask[None, None])
        o_win = jnp.einsum('bhqk,bkd->bqhd', p_w.astype(vw.dtype), vw)
        return gb[..., 0:1] * o_cmp + gb[..., 1:2] * o_sel + gb[..., 2:3] * o_win

    return _sweep(block, S)

def _hybrid_mixer(u, w_in, cmp_pos_k, cmp_w1_k, cmp_w2_k, cmp_pos_v, cmp_w1_v, cmp_w2_v, w_up, w_out):
    B, S, _ = u.shape
    p = _split_columns(u @ w_in)

    def heads(t, h, d=HEAD_DIM):
        return t.reshape(B, S, h, d)

    def rope1(t):
        return _rope(t[:, :, None, :])[:, :, 0]

    o_a = _stick_breaking(heads(p['q_a'], SB_HEADS), heads(p['k_a'], SB_HEADS), heads(p['v_a'], SB_HEADS))
    o_b = _dsa_attention(_rope(heads(p['q_b'], DSA_HEADS)), rope1(p['k_b']), p['v_b'],
                         _rope(heads(p['q_idx'], IDX_HEADS, IDX_DIM)), rope1(p['k_idx']), p['w_idx'])
    gates_c = jax.nn.sigmoid(p['g_c'].reshape(B, S, NSA_HEADS, 3))
    o_c = _nsa_attention(_rope(heads(p['q_c'], NSA_HEADS)), rope1(p['k_cmp']), p['v_cmp'],
                         rope1(p['k_sel']), p['v_sel'], rope1(p['k_win']), p['v_win'], gates_c,
                         cmp_pos_k, cmp_w1_k, cmp_w2_k, cmp_pos_v, cmp_w1_v, cmp_w2_v)
    g = jax.nn.sigmoid(p['g_merge'].reshape(B, S, 3, D_MODEL))
    merged = (g[:, :, 0] * (o_a.reshape(B, S, BRANCH_WIDTH) @ w_up[0]) +
              g[:, :, 1] * (o_b.reshape(B, S, BRANCH_WIDTH) @ w_up[1]) +
              g[:, :, 2] * (o_c.reshape(B, S, BRANCH_WIDTH) @ w_up[2]))
    return merged @ w_out

def _memory_attention(h, mem, g_q, g_kv, w_q, w_kv, w_o):
    B, S, _ = h.shape
    M = mem.shape[1]
    q = (_rmsnorm(h, g_q) @ w_q).reshape(B, S, MEM_HEADS, MEM_HEAD_DIM)
    kv = (_rmsnorm(mem, g_kv) @ w_kv).reshape(B, M, 2, MEM_HEADS, MEM_HEAD_DIM)
    s = jnp.einsum('bshd,bmhd->bhsm', q, kv[:, :, 0]).astype(jnp.float32) * MEM_HEAD_DIM ** -0.5
    pr = jax.nn.softmax(s, axis=-1)
    o = jnp.einsum('bhsm,bmhd->bshd', pr.astype(h.dtype), kv[:, :, 1])
    return o.reshape(B, S, MEM_HEADS * MEM_HEAD_DIM) @ w_o

def _swiglu(u, w_in, w_out):
    a = u @ w_in
    return (jax.nn.silu(a[..., :D_FF]) * a[..., D_FF:]) @ w_out

def second_inputs(seed: int = 0) -> dict:
    key = jax.random.key(seed)
    ks = jax.random.split(key, 21)

    def nrm(k, shape, fan_in):
        return jax.random.normal(k, shape, jnp.float32) * fan_in ** -0.5

    def gain(k, shape):
        return 1.0 + 0.05 * jax.random.normal(k, shape, jnp.float32)

    L = DEPTH_2
    mem_w = MEM_HEADS * MEM_HEAD_DIM
    return {
        'x': jax.random.normal(ks[0], (BATCH, SEQ, D_MODEL), jnp.float32),
        'mem': jax.random.normal(ks[1], (BATCH, N_MEM, D_MODEL), jnp.float32),
        'norm_mix': gain(ks[2], (L, D_MODEL)),
        'w_in': nrm(ks[3], (L, D_MODEL, D_IN), D_MODEL),
        'cmp_pos_k': 0.1 * jax.random.normal(ks[4], (L, CMP_LEN, HEAD_DIM), jnp.float32),
        'cmp_w1_k': nrm(ks[5], (L, CMP_LEN * HEAD_DIM, CMP_HIDDEN), CMP_LEN * HEAD_DIM),
        'cmp_w2_k': nrm(ks[6], (L, CMP_HIDDEN, HEAD_DIM), CMP_HIDDEN),
        'cmp_pos_v': 0.1 * jax.random.normal(ks[7], (L, CMP_LEN, HEAD_DIM), jnp.float32),
        'cmp_w1_v': nrm(ks[8], (L, CMP_LEN * HEAD_DIM, CMP_HIDDEN), CMP_LEN * HEAD_DIM),
        'cmp_w2_v': nrm(ks[9], (L, CMP_HIDDEN, HEAD_DIM), CMP_HIDDEN),
        'w_up': nrm(ks[10], (L, 3, BRANCH_WIDTH, D_MODEL), BRANCH_WIDTH),
        'w_out': nrm(ks[11], (L, D_MODEL, D_MODEL), D_MODEL),
        'norm_mem_q': gain(ks[12], (L, D_MODEL)),
        'norm_mem_kv': gain(ks[13], (L, D_MODEL)),
        'w_mem_q': nrm(ks[14], (L, D_MODEL, mem_w), D_MODEL),
        'w_mem_kv': nrm(ks[15], (L, D_MODEL, 2 * mem_w), D_MODEL),
        'w_mem_o': nrm(ks[16], (L, mem_w, D_MODEL), mem_w),
        'norm_ffn': gain(ks[17], (L, D_MODEL)),
        'w_ffn_in': nrm(ks[18], (L, D_MODEL, 2 * D_FF), D_MODEL),
        'w_ffn_out': nrm(ks[19], (L, D_FF, D_MODEL), D_FF),
        'norm_final': gain(ks[20], (D_MODEL,)),
    }

def second_block(x, mem, norm_mix, w_in, cmp_pos_k, cmp_w1_k, cmp_w2_k, cmp_pos_v, cmp_w1_v, cmp_w2_v,
              w_up, w_out, norm_mem_q, norm_mem_kv, w_mem_q, w_mem_kv, w_mem_o,
              norm_ffn, w_ffn_in, w_ffn_out, norm_final):
    h = x
    for l in range(DEPTH_2):
        h = h + _hybrid_mixer(_rmsnorm(h, norm_mix[l]), w_in[l],
                              cmp_pos_k[l], cmp_w1_k[l], cmp_w2_k[l],
                              cmp_pos_v[l], cmp_w1_v[l], cmp_w2_v[l], w_up[l], w_out[l])
        h = h + _memory_attention(h, mem, norm_mem_q[l], norm_mem_kv[l], w_mem_q[l], w_mem_kv[l], w_mem_o[l])
        h = h + _swiglu(_rmsnorm(h, norm_ffn[l]), w_ffn_in[l], w_ffn_out[l])
    return _rmsnorm(h, norm_final)


def setup_inputs(seed=0):
    out = dict(first_inputs(seed))
    for name, value in second_inputs(seed + 1).items():
        if name != "x":
            out[name + "_2"] = value
    return out


def reference(
    x, norm_a, w_in_a, conv_w_a, conv_b_a, dt_bias_a, a_log_a, d_skip_a, ssd_norm_a,
    lambda_q1_a, lambda_k1_a, lambda_q2_a, lambda_k2_a, subln_a, w_out_a, norm_c, w_in_c,
    b_in_c, sinks_c, w_out_c, final_norm, mem_2, norm_mix_2, w_in_2, cmp_pos_k_2, cmp_w1_k_2,
    cmp_w2_k_2, cmp_pos_v_2, cmp_w1_v_2, cmp_w2_v_2, w_up_2, w_out_2, norm_mem_q_2,
    norm_mem_kv_2, w_mem_q_2, w_mem_kv_2, w_mem_o_2, norm_ffn_2, w_ffn_in_2, w_ffn_out_2,
    norm_final_2,
):
    x = first_block(
        x, norm_a, w_in_a, conv_w_a, conv_b_a, dt_bias_a, a_log_a, d_skip_a, ssd_norm_a,
        lambda_q1_a, lambda_k1_a, lambda_q2_a, lambda_k2_a, subln_a, w_out_a, norm_c, w_in_c,
        b_in_c, sinks_c, w_out_c, final_norm,
    )
    return second_block(
        x, mem_2, norm_mix_2, w_in_2, cmp_pos_k_2, cmp_w1_k_2, cmp_w2_k_2, cmp_pos_v_2,
        cmp_w1_v_2, cmp_w2_v_2, w_up_2, w_out_2, norm_mem_q_2, norm_mem_kv_2, w_mem_q_2,
        w_mem_kv_2, w_mem_o_2, norm_ffn_2, w_ffn_in_2, w_ffn_out_2, norm_final_2,
    )


_drawn_inputs = setup_inputs


def setup_inputs(seed=0):
    import zlib

    import numpy as np

    out = dict(_drawn_inputs(seed))
    spreads = {}
    factors = {'conv_b_a': 2.788,
     'ssd_norm_a': 3.955,
     'lambda_q1_a': 8.0,
     'lambda_k1_a': 8.0,
     'lambda_k2_a': 2.8,
     'subln_a': 6.812,
     'norm_c': 7.126,
     'b_in_c': 4.336,
     'cmp_pos_k_2': 8.0,
     'cmp_pos_v_2': 3.475,
     'norm_mem_q_2': 8.0,
     'norm_mem_kv_2': 6.816,
     'sinks_c': 4.913,
     'norm_ffn_2': 8.0}
    for name, (base, spread) in spreads.items():
        noise = np.random.default_rng([zlib.crc32(name.encode()), seed]).standard_normal(out[name].shape)
        drawn = base * np.exp(spread * noise) if base else spread * noise
        out[name] = __import__('jax').numpy.asarray(drawn.astype(out[name].dtype))
    for name, factor in factors.items():
        out[name] = (out[name] * factor).astype(out[name].dtype)
    return out
```

```python
import math
from contextlib import ExitStack

import concourse.bass as bass
import numpy as np
from concourse import mybir

F32 = mybir.dt.float32
ALU = mybir.AluOpType
ACT = mybir.ActivationFunctionType
AXX = mybir.AxisListType.X

P = 128
D = 1024
S = 512
NT = S // P
KD = D // P
UNIT = 1024
NEG = -1.0e30
DA_H = 8
SSD_H = 16
SSD_P = 64
SW_H = 16
FF = 2816
NFF = FF // P
N_CMP = 31
EPS_A = 1e-5
EPS_B = 1e-6
LAMBDA_INIT = 0.8 - 0.6 * math.exp(-0.3 * 0)
RING = 8

CONSTS = {}
_at = 0
for _n, _w in [("ident", P), ("tri_le", P), ("tri_gt", P), ("neg_ge", P), ("neg_ones", P), ("strict_neg", P),
               ("strict01", P), ("ones", P), ("alibi", S), ("sw", 2 * P), ("causal", S), ("cos", S), ("sin", S),
               ("perm", P), ("cmp_neg", NT * 32), ("cmp01", NT * 32)]:
    CONSTS[_n] = (_at, _w)
    _at += _w
N_CONST = _at

COLS = {}
_at = 0
for _n, _w in [("norm_a", 8), ("norm_c", 8), ("norm_mix", 8), ("norm_mem_q", 8), ("norm_mem_kv", 8),
               ("norm_ffn", 8), ("ssd_norm", 8), ("subln", 1), ("conv_w", 48), ("conv_b", 12), ("bq", 8), ("bk", 2),
               ("pos", 32)]:
    COLS[_n] = (_at, _w)
    _at += _w
N_COLS = _at

ROWS = {}
_at = 0
for _n, _w in [("dt_bias", 16), ("a_log", 16), ("d_skip", 16), ("sinks", 16), ("lq1", 64), ("lk1", 64),
               ("lq2", 64), ("lk2", 64), ("bv", 128)]:
    ROWS[_n] = (_at, _w)
    _at += _w
N_ROWS = _at

STAGES = [("in_a", 53), ("out_a", 16), ("in_c", 19), ("out_c", 8), ("in_m", 15 + 4 + 24), ("cmp", 5), ("up", 6),
          ("out_m", 8), ("mem_kv", 4), ("mem_q", 2), ("mem_out", 2), ("ffn_in", 2 * NFF), ("ffn_out", NFF)]
START = {}
_at = 0
for _n, _c in STAGES:
    START[_n] = _at
    _at += _c
N_UNITS = _at


def build(nc, w_dram, x_dram, mem_dram, const_dram, cols_dram, rows_dram, big_dram, out_dram):
    ctx = ExitStack()
    with ctx:
        def sb(name, shape):
            return ctx.enter_context(nc.sbuf_tensor(name, shape, F32))

        stage_sems = []

        def sem(name):
            stage_sems.append(nc.alloc_semaphore(name))
            return stage_sems[-1]

        def lasting_sem(name):
            return ctx.enter_context(nc.semaphore(name))

        def recycle():
            with nc.Block() as block:
                @block.sync
                def _(sp):
                    for s in stage_sems:
                        sp.sem_clear(s)
            for s in stage_sems:
                nc.release_semaphore(s)
            stage_sems.clear()

        ring = sb("ring", [P, RING, UNIT])
        x = sb("x", [P, NT, D])
        hT = sb("hT", [P, KD * S])
        consts = sb("consts", [P, N_CONST])
        cols = sb("cols", [P, N_COLS])
        rows = sb("rows", [P, N_ROWS])
        big_row = sb("big_row", [P, D])
        arena = sb("arena", [P, 27136])
        scr = sb("scr", [P, 4096])
        small = sb("small", [P, 1024])
        ps = ctx.enter_context(nc.psum_tensor("ps", [P, 8, 512], F32))

        hT3 = hT[:, :].rearrange("p (k s) -> p k s", k=KD)

        def const(name):
            a, w = CONSTS[name]
            return consts[:, a:a + w]

        def col(name, i=0, n=1):
            a = COLS[name][0] + i
            return cols[:, a:a + n]

        def row(name):
            a, w = ROWS[name]
            return rows[:, a:a + w]

        def part(a, shape):
            n = 1
            for d in shape:
                n *= d
            v = arena[:, a:a + n]
            if len(shape) == 2:
                return v.rearrange("p (a b) -> p a b", a=shape[0])
            return v

        ident = const("ident")
        ss = small[:, 0:64]
        ms = small[:, 64:128]
        rs = small[:, 128:192]
        neg_half = small[:, 192:256]
        lam = small[:, 256:257]
        subln8 = small[:, 257:258]
        neg_a = small[:, 258:274]
        neg_sink = small[:, 274:290]
        neg_max = small[:, 300:308]
        den = small[:, 308:316]
        rden = small[:, 316:324]
        esink = small[:, 324:332]

        weights_used = lasting_sem("weights_used")
        weights_loaded = [lasting_sem(f"weights_loaded{i}") for i in range(RING)]
        stored = lasting_sem("stored")
        issued = [0]

        def stream(sp, stage):
            count = dict(STAGES)[stage] if stage else 0
            end = START[stage] + count if stage else 0
            for u in range(issued[0], min(end + RING - 1, N_UNITS)):
                if u >= RING:
                    sp.wait_ge(weights_used, u - RING + 1)
                sp.dma_start(ring[:, u % RING, :], w_dram[u]).then_inc(weights_loaded[u % RING], 16)
            issued[0] = max(issued[0], min(end + RING - 1, N_UNITS))

        def unit(pe, u):
            pe.wait_ge(weights_loaded[u % RING], 16 * (u // RING + 1))
            return ring[:, u % RING, :]


        const_loaded, x_loaded, small_loaded, big_loaded = (
            sem("const_loaded"), sem("x_loaded"), sem("small_loaded"), lasting_sem("big_loaded"))
        setup_chain, lam_dots, lam_exps, sub_ready = sem("setup_chain"), sem("lam_dots"), sem("lam_exps"), sem("sub_ready")
        with nc.Block() as block:
            @block.sync
            def _(sp):
                sp.dma_start(x[:, :, :], x_dram.rearrange("(t p) d -> p t d", p=P)).then_inc(x_loaded, 16)
                stream(sp, None)

            @block.scalar
            def _(act):
                act.dma_start(consts[:, :], const_dram).then_inc(const_loaded, 16)
                act.dma_start(cols[:, :], cols_dram).then_inc(small_loaded, 16)
                act.dma_start(rows[:, :], rows_dram.partition_broadcast(P)).then_inc(small_loaded, 16)
                act.dma_start(big_row[:, :], big_dram[0, :].partition_broadcast(P)).then_inc(big_loaded, 16)
                act.wait_ge(lam_dots, 2)
                act.activation(small[:, 334:336], small[:, 332:334], ACT.Exp).then_inc(lam_exps, 1)
                act.activation(small[:, 336:352], row("a_log"), ACT.Exp).then_inc(lam_exps, 1)

            @block.vector
            def _(dve):
                dve.memset(neg_half, -0.5).then_inc(setup_chain, 1)
                dve.wait_ge(small_loaded, 32)
                dve.tensor_tensor(scr[:, 0:64], row("lq1"), row("lk1"), ALU.mult).then_inc(setup_chain, 1)
                dve.tensor_tensor(scr[:, 64:128], row("lq2"), row("lk2"), ALU.mult).then_inc(setup_chain, 1)
                dve.wait_ge(setup_chain, 3)
                dve.tensor_reduce(small[:, 332:333], scr[:, 0:64], AXX, ALU.add).then_inc(lam_dots, 1)
                dve.tensor_reduce(small[:, 333:334], scr[:, 64:128], AXX, ALU.add).then_inc(lam_dots, 1)
                dve.tensor_scalar(subln8, col("subln"), 1.0 - LAMBDA_INIT, None, ALU.mult).then_inc(sub_ready, 1)
                dve.tensor_scalar(neg_sink, row("sinks"), -1.0, None, ALU.mult).then_inc(sub_ready, 1)
                dve.wait_ge(lam_exps, 2)
                dve.tensor_scalar(neg_a, small[:, 336:352], -1.0, None, ALU.mult).then_inc(sub_ready, 1)
                dve.tensor_tensor(small[:, 352:353], small[:, 334:335], small[:, 335:336], ALU.subtract)\
                   .then_inc(setup_chain, 1)
                dve.wait_ge(setup_chain, 4)
                dve.tensor_scalar(lam, small[:, 352:353], LAMBDA_INIT, None, ALU.add).then_inc(sub_ready, 1)
                dve.wait_ge(const_loaded, 16)
                dve.wait_ge(x_loaded, 16)
                dve.wait_ge(big_loaded, 16)

        def norm(tag, src, nt, eps, gain, xs):
            squared, mean, rooted, scaled, turned, out_act, out_dve = (
                sem(tag + n) for n in ("_squared", "_mean", "_rooted", "_scaled", "_turned", "_out_act", "_out_dve"))
            dst = hT[:, 0:KD * nt * P].rearrange("p (k s) -> p k s", k=KD)
            with nc.Block() as block:
                @block.scalar
                def _(act):
                    for t in range(nt):
                        act.activation(xs[:, t, :], src[:, t, :], ACT.Square, accum_out=ss[:, t:t + 1]).then_inc(squared, 1)
                    for k in range(0, KD, 2):
                        act.wait_ge(turned, k + 1)
                        act.activation(dst[:, k, :], ps[:, k, 0:nt * P], ACT.Copy, scale=col(gain, k))\
                           .then_inc(out_act, 1)

                @block.vector
                def _(dve):
                    for t in range(nt):
                        dve.wait_ge(squared, t + 1)
                        dve.tensor_scalar(ms[:, t:t + 1], ss[:, t:t + 1], 1.0 / D, eps, ALU.mult, ALU.add)\
                           .then_inc(mean, 1)
                    for t in range(nt):
                        dve.wait_ge(rooted, t + 1)
                        dve.tensor_scalar(xs[:, t, :], src[:, t, :], rs[:, t:t + 1], None, ALU.mult)\
                           .then_inc(scaled, 1)
                    for k in range(1, KD, 2):
                        dve.wait_ge(turned, k + 1)
                        dve.tensor_scalar(dst[:, k, :], ps[:, k, 0:nt * P], col(gain, k), None, ALU.mult)\
                           .then_inc(out_dve, 1)

                @block.gpsimd
                def _(pool):
                    for t in range(nt):
                        pool.wait_ge(mean, t + 1)
                        pool.tensor_tensor(rs[:, t:t + 1], ms[:, t:t + 1], neg_half[:, 0:1], ALU.pow)\
                            .then_inc(rooted, 1)

                @block.tensor
                def _(pe):
                    for t in range(nt):
                        pe.wait_ge(scaled, t + 1)
                        for k in range(KD):
                            last = pe.transpose(ps[:, k, t * P:(t + 1) * P], xs[:, t, k * P:(k + 1) * P], ident)
                            if t == nt - 1:
                                last.then_inc(turned, 1)

        def project(tag, stage, jobs, outs, nt=NT):
            done, out_act, out_dve = sem(tag + "_done"), sem(tag + "_out_act"), sem(tag + "_out_dve")
            src = hT[:, 0:KD * nt * P].rearrange("p (k s) -> p k s", k=KD)

            def width(i):
                b = 0
                for job in jobs:
                    n = 1 if job[0] == "F" else nt
                    if i < b + n:
                        return nt * P if job[0] == "F" else job[1]
                    b += n

            def emptied(pe, i):
                if i >= 8:
                    who = outs[i - 8][0]
                    n = sum(o[0] == who for o in outs[:i - 7])
                    pe.wait_ge(out_act if who == "act" else out_dve, n)

            with nc.Block() as block:
                @block.sync
                def _(sp):
                    stream(sp, stage)

                @block.tensor
                def _(pe):
                    u, i = START[stage], 0
                    for job in jobs:
                        if job[0] == "F":
                            emptied(pe, i)
                            w = unit(pe, u)
                            for k in range(KD):
                                mm = pe.matmul(ps[:, i % 8, 0:nt * P], w[:, k * P:(k + 1) * P], src[:, k, :],
                                               start=k == 0, stop=k == KD - 1)
                                if k == 0 and u:
                                    mm.then_inc(weights_used, 1)
                            mm.then_inc(done, 1)
                            u += 1
                            i += 1
                        else:
                            n, bk = job[1:]
                            for t in range(nt):
                                emptied(pe, i + t)
                            for k in range(KD):
                                if k % bk == 0:
                                    w = unit(pe, u)
                                    u += 1
                                for t in range(nt):
                                    mm = pe.matmul(ps[:, (i + t) % 8, 0:n], src[:, k, t * P:(t + 1) * P],
                                                   w[:, (k % bk) * n:(k % bk + 1) * n],
                                                   start=k == 0, stop=k == KD - 1)
                                    if k % bk == 0 and t == 0 and u > 1:
                                        mm.then_inc(weights_used, 1)
                                    if k == KD - 1:
                                        mm.then_inc(done, 1)
                            i += nt

                @block.scalar
                def _(act):
                    for i, (who, what, dst, arg) in enumerate(outs):
                        if who != "act":
                            continue
                        act.wait_ge(done, i + 1)
                        bank = ps[:, i % 8, 0:width(i)]
                        if what == "copy":
                            act.activation(dst, bank, ACT.Copy, scale=arg).then_inc(out_act, 1)
                        elif what == "silu":
                            act.activation(dst, bank, ACT.Silu).then_inc(out_act, 1)
                        elif what == "sigmoid":
                            act.activation(dst, bank, ACT.Sigmoid).then_inc(out_act, 1)

                @block.vector
                def _(dve):
                    for i, (who, what, dst, arg) in enumerate(outs):
                        if who != "dve":
                            continue
                        dve.wait_ge(done, i + 1)
                        bank = ps[:, i % 8, 0:width(i)]
                        if what == "copy":
                            dve.tensor_scalar(dst, bank, arg, None, ALU.mult).then_inc(out_dve, 1)
                        elif what == "bias":
                            dve.tensor_scalar(dst, bank, arg[0], arg[1], ALU.add, ALU.mult).then_inc(out_dve, 1)
                        elif what == "add_row":
                            dve.tensor_tensor(dst, bank, arg, ALU.add).then_inc(out_dve, 1)
                        elif what == "times":
                            dve.wait_ge(out_act, arg)
                            dve.tensor_tensor(dst, bank, dst, ALU.mult).then_inc(out_dve, 1)

        def combine(tag, stage, yT, nk):
            done, out_dve = sem(tag + "_done"), sem(tag + "_out_dve")
            with nc.Block() as block:
                @block.sync
                def _(sp):
                    stream(sp, stage)

                @block.tensor
                def _(pe):
                    for k in range(nk):
                        w = unit(pe, START[stage] + k)
                        for b in range(8):
                            t, half = b // 2, b % 2
                            mm = pe.matmul(ps[:, b, :], yT(k)[:, t * P:(t + 1) * P],
                                           w[:, half * 512:(half + 1) * 512], start=k == 0, stop=k == nk - 1)
                            if b == 0:
                                mm.then_inc(weights_used, 1)
                            elif k == nk - 1:
                                mm.then_inc(done, 1)

                @block.vector
                def _(dve):
                    for b in range(8):
                        t, half = b // 2, b % 2
                        xv = x[:, t, half * 512:(half + 1) * 512]
                        dve.wait_ge(done, max(b, 1))
                        dve.tensor_tensor(xv, ps[:, b, :], xv, ALU.add).then_inc(out_dve, 1)

        def turn(tag, src, dst, nk, gain=None):
            turned, out_act, out_dve = sem(tag + "_turned"), sem(tag + "_out_act"), sem(tag + "_out_dve")
            with nc.Block() as block:
                @block.tensor
                def _(pe):
                    for k in range(nk):
                        if k >= 8:
                            pe.wait_ge(out_act if k % 2 == 0 else out_dve, (k - 8) // 2 + 1)
                        for t in range(NT):
                            last = pe.transpose(ps[:, k % 8, t * P:(t + 1) * P], src(t, k), ident)
                        last.then_inc(turned, 1)

                @block.scalar
                def _(act):
                    for k in range(0, nk, 2):
                        act.wait_ge(turned, k + 1)
                        act.activation(dst(k), ps[:, k % 8, :], ACT.Copy, scale=gain(k) if gain else 1.0)\
                           .then_inc(out_act, 1)

                @block.vector
                def _(dve):
                    for k in range(1, nk, 2):
                        dve.wait_ge(turned, k + 1)
                        dve.tensor_scalar(dst(k), ps[:, k % 8, :], gain(k) if gain else 1.0, None, ALU.mult)\
                           .then_inc(out_dve, 1)

        def attend(tag, units, maps=1, keep=False):
            n = len(units)
            nb_s, t_bank, o_bank, nb_o = (3, 3, 5, 3) if maps == 1 else (2, 4, 6, 2)
            NP = 3
            mixing = maps == 2 or keep
            names = ["scored", "lifted", "maxed", "expd", "mixed", "turned", "pT_out", "valued", "out", "chain", "esink"]
            scored, lifted, maxed, expd, mixed, turned, pT_out, valued, out_done, dve_chain, esunk = (
                sem(tag + "_" + m) for m in names)

            def score(i, m):
                return ps[:, (i % nb_s) * maps + m, 0:units[i]["w"]]

            def prob(i, m):
                a = ((i % NP) * maps + m) * 512
                return scr[:, a:a + units[i]["w"]]

            def pT(i):
                a = NP * maps * 512 + (i % 2) * 512
                return scr[:, a:a + 512]

            def stat(first, i, m=None):
                a = first + 2 * (i % 4)
                return small[:, a:a + maps] if m is None else small[:, a + m:a + m + 1]

            NMAX, DEN, RDEN, ESINK = 300, 308, 316, 324

            with nc.Block() as block:
                @block.tensor
                def _(pe):
                    for step in range(n + 2):
                        if step < n:
                            i, u = step, units[step]
                            if i >= nb_s:
                                pe.wait_ge(lifted, i - nb_s + 1)
                            for m in range(maps):
                                last = pe.matmul(score(i, m), u["q"][m], u["k"][m], start=True, stop=True)
                            last.then_inc(scored, 1)
                        if 1 <= step <= n:
                            i, u = step - 1, units[step - 1]
                            nb = len(u["v"])
                            kp = u["w"] // nb
                            pe.wait_ge(mixed if mixing else expd, i + 1)
                            if i >= 2:
                                pe.wait_ge(pT_out, i - 1)
                            for b in range(nb):
                                last = pe.transpose(ps[0:kp, t_bank + i % 2, b * P:(b + 1) * P],
                                                    prob(i, 0)[:, b * kp:(b + 1) * kp], ident)
                            last.then_inc(turned, 1)
                        if step >= 2:
                            i, u = step - 2, units[step - 2]
                            nb = len(u["v"])
                            kp = u["w"] // nb
                            pe.wait_ge(pT_out, i + 1)
                            if i >= nb_o:
                                pe.wait_ge(out_done, i - nb_o + 1)
                            for b in range(nb):
                                last = pe.matmul(ps[:, o_bank + i % nb_o, 0:u["dv"]], pT(i)[0:kp, b * P:(b + 1) * P],
                                                 u["v"][b], start=b == 0, stop=b == nb - 1)
                            last.then_inc(valued, 1)

                @block.scalar
                def _(act):
                    for step in range(n + 1):
                        if step < n:
                            i, u = step, units[step]
                            act.wait_ge(maxed, i + 1)
                            if "sink" in u:
                                act.activation(stat(ESINK, i), u["sink"], ACT.Exp, bias=stat(NMAX, i))\
                                   .then_inc(esunk, 1)
                            for m in range(maps):
                                last = act.activation(prob(i, m), prob(i, m), ACT.Exp, bias=stat(NMAX, i, m),
                                                      accum_out=stat(DEN, i, m))
                            last.then_inc(expd, 1)
                        if step >= 1:
                            i, u = step - 1, units[step - 1]
                            nb = len(u["v"])
                            kp = u["w"] // nb
                            act.wait_ge(turned, i + 1)
                            if i >= 2:
                                act.wait_ge(valued, i - 1)
                            act.activation(pT(i)[0:kp, 0:nb * P], ps[0:kp, t_bank + i % 2, 0:nb * P], ACT.Copy)\
                               .then_inc(pT_out, 1)

                @block.vector
                def _(dve):
                    links = [0]

                    def link(ins):
                        links[0] += 1
                        ins.then_inc(dve_chain, 1)
                        dve.wait_ge(dve_chain, links[0])

                    for step in range(n + 3):
                        if step < n:
                            i, u = step, units[step]
                            dve.wait_ge(scored, i + 1)
                            if i >= NP:
                                dve.wait_ge(turned, i - NP + 1)
                            for m in range(maps):
                                if u["mask"] is None:
                                    last = dve.tensor_copy(prob(i, m), score(i, m))
                                else:
                                    last = dve.scalar_tensor_tensor(prob(i, m), u["mask"], u["slope"], score(i, m),
                                                                    ALU.mult, ALU.add)
                            last.then_inc(lifted, 1)
                            dve.wait_ge(lifted, i + 1)
                            for m in range(maps):
                                last = dve.tensor_reduce(stat(NMAX, i, m), prob(i, m), AXX, ALU.max, negate=True)
                            if "sink" in u:
                                link(last)
                                last = dve.tensor_tensor(stat(NMAX, i), stat(NMAX, i), u["neg_sink"], ALU.min)
                            last.then_inc(maxed, 1)
                        if mixing and 1 <= step <= n:
                            i, u = step - 1, units[step - 1]
                            dve.wait_ge(expd, i + 1)
                            if maps == 2:
                                link(dve.reciprocal(stat(RDEN, i), stat(DEN, i)))
                                link(dve.tensor_tensor(stat(RDEN, i, 1), stat(RDEN, i, 1), lam, ALU.mult))
                                link(dve.tensor_scalar(prob(i, 1), prob(i, 1), stat(RDEN, i, 1), None, ALU.mult))
                                dve.scalar_tensor_tensor(prob(i, 0), prob(i, 0), stat(RDEN, i, 0), prob(i, 1),
                                                         ALU.mult, ALU.subtract).then_inc(mixed, 1)
                            else:
                                dve.scalar_tensor_tensor(prob(i, 0), prob(i, 0), 1.0, u["keep01"], ALU.mult, ALU.mult,
                                                         accum_out=stat(DEN, i)).then_inc(mixed, 1)
                                dve.wait_ge(mixed, i + 1)
                                link(dve.tensor_scalar(stat(DEN, i), stat(DEN, i), 1e-30, None, ALU.max))
                        if step >= 3:
                            i, u = step - 3, units[step - 3]
                            bank = ps[:, o_bank + i % nb_o, 0:u["dv"]]
                            if maps == 1:
                                dve.wait_ge(expd, i + 1)
                                if "sink" in u:
                                    dve.wait_ge(esunk, i + 1)
                                    link(dve.tensor_tensor(stat(DEN, i), stat(DEN, i), stat(ESINK, i), ALU.add))
                                link(dve.reciprocal(stat(RDEN, i), stat(DEN, i)))
                                if "gate" in u:
                                    link(dve.tensor_tensor(stat(RDEN, i), stat(RDEN, i), u["gate"], ALU.mult))
                            dve.wait_ge(valued, i + 1)
                            if maps == 2:
                                last = dve.tensor_copy(u["out"], bank)
                            elif u.get("add"):
                                last = dve.scalar_tensor_tensor(u["out"], bank, stat(RDEN, i), u["out"],
                                                                ALU.mult, ALU.add)
                            else:
                                last = dve.tensor_scalar(u["out"], bank, stat(RDEN, i), None, ALU.mult)
                            last.then_inc(out_done, 1)

        def token(ap, t):
            return ap[:, t * P:(t + 1) * P]

        Q, K, V, G, Z, XBC, DT = 0, 4096, 8192, 12288, 16384, 20480, 26624
        norm("norm_a", x, NT, EPS_A, "norm_a", part(0, [NT, D]))
        qT, kT = part(Q, [8, S]), part(K, [8, S])
        v_tok, g_tok, z_tok = part(V, [NT, D]), part(G, [NT, D]), part(Z, [NT, D])
        xbc = part(XBC, [12, S])
        dt = part(DT, [NT, 16])
        jobs = [("F",)] * 28 + [("T", 512, 2)] * 6 + [("T", 16, 8)]
        outs = [("act" if j % 2 == 0 else "dve", "copy", qT[:, j, :], 0.125) for j in range(8)]
        outs += [("act" if j % 2 == 0 else "dve", "copy", kT[:, j, :], 1.0) for j in range(8)]
        outs += [("act" if j % 2 == 0 else "dve", "copy", xbc[:, j, :], 1.0) for j in range(12)]
        for tok, what in ((v_tok, "copy"), (g_tok, "silu"), (z_tok, "silu")):
            for c in range(2):
                for t in range(NT):
                    who = "act" if what == "silu" or t % 2 == 0 else "dve"
                    outs.append((who, what, tok[:, t, c * 512:(c + 1) * 512], 1.0))
        outs += [("dve", "copy", dt[:, t, :], 1.0) for t in range(NT)]
        project("in_a", "in_a", jobs, outs)

        y_a = hT[:, :].rearrange("p (t d) -> p t d", t=NT)
        units = []
        for h in range(DA_H):
            for t in range(NT):
                w = (t + 1) * P
                units.append(dict(q=[token(qT[m * 64:m * 64 + 64, h, :], t) for m in range(2)],
                                  k=[kT[m * 64:m * 64 + 64, h, 0:w] for m in range(2)], w=w,
                                  mask=const("alibi")[:, S - w:S], slope=2.0 ** -(h + 1),
                                  v=[v_tok[:, b, h * P:(h + 1) * P] for b in range(t + 1)], dv=P,
                                  out=y_a[:, t, h * P:(h + 1) * P]))
        attend("da", units, maps=2)

        def group_norm(tag, y, width, eps, gate):
            ng = NT * D // width
            squared, mean, rooted, scaled = (sem(tag + m) for m in ("_squared", "_mean", "_rooted", "_scaled"))
            flat = y.rearrange("p t (g w) -> p (t g) w", w=width)
            gated = gate.rearrange("p t (g w) -> p (t g) w", w=width) if gate is not None else None
            with nc.Block() as block:
                @block.scalar
                def _(act):
                    for g in range(ng):
                        act.activation(scr[:, g * width:(g + 1) * width], flat[:, g, :], ACT.Square, accum_out=ss[:, g:g + 1])\
                           .then_inc(squared, 1)

                @block.gpsimd
                def _(pool):
                    pool.wait_ge(mean, 1)
                    pool.tensor_tensor(rs[:, 0:ng], ms[:, 0:ng], neg_half[:, 0:ng], ALU.pow).then_inc(rooted, 1)

                @block.vector
                def _(dve):
                    dve.wait_ge(squared, ng)
                    dve.tensor_scalar(ms[:, 0:ng], ss[:, 0:ng], 1.0 / width, eps, ALU.mult, ALU.add).then_inc(mean, 1)
                    dve.wait_ge(rooted, 1)
                    for g in range(ng):
                        if gated is None:
                            dve.tensor_scalar(flat[:, g, :], flat[:, g, :], rs[:, g:g + 1], None, ALU.mult)\
                               .then_inc(scaled, 1)
                        else:
                            dve.scalar_tensor_tensor(flat[:, g, :], flat[:, g, :], rs[:, g:g + 1], gated[:, g, :],
                                                     ALU.mult, ALU.mult).then_inc(scaled, 1)

        group_norm("subln", y_a, P, EPS_A, g_tok)
        yT_a = part(0, [16, S])
        turn("ya", lambda t, k: y_a[:, t, k * P:(k + 1) * P], lambda k: yT_a[:, k, :], 8, lambda k: subln8)

        xs_tok, xdt = part(4096, [NT, D]), part(8192, [NT, D])
        XDD, DSTR, EXPS, CONV = 12288, 12800, 13824, 14848
        xdd, dstr, exps = arena[:, XDD:XDD + 512], part(DSTR, [8, P]), part(EXPS, [8, P])
        b_tok = scr[:, 0:1024].rearrange("p (c n) -> p c n", c=NT)
        cbm = scr[:, 1024:2048].rearrange("p (i l) -> p i l", i=8)
        state = scr[:, 2048:3072].rearrange("p (g d) -> p g d", g=2)
        dta = small[:, 400:464]
        dtv = small[:, 464:528]
        decays = small[:, 528:720]
        y_b = hT[:, :].rearrange("p (t d) -> p t d", t=NT)
        tap_done, conv_done, silu_done = sem("tap_done"), sem("conv_done"), sem("silu_done")
        dt_chain, dt_biased, dt_exp, dt_ln, dta_ready = (
            sem("dt_chain"), sem("dt_biased"), sem("dt_exp"), sem("dt_ln"), sem("dta_ready"))
        dt_all = dt.rearrange("p t h -> p (t h)")
        with nc.Block() as block:
            @block.vector
            def _(dve):
                taps = 0
                for j in range(12):
                    acc = arena[:, CONV + (j % 2) * 512:CONV + (j % 2) * 512 + 512]
                    if j >= 2:
                        dve.wait_ge(silu_done, j - 1)
                    dve.tensor_scalar(acc, xbc[:, j, :], col("conv_w", 4 * j + 3), col("conv_b", j), ALU.mult, ALU.add)\
                       .then_inc(tap_done, 1)
                    taps += 1
                    for s in (1, 2, 3):
                        dve.wait_ge(tap_done, taps)
                        last = dve.scalar_tensor_tensor(acc[:, s:S], xbc[:, j, 0:S - s], col("conv_w", 4 * j + 3 - s),
                                                        acc[:, s:S], ALU.mult, ALU.add)
                        if s < 3:
                            last.then_inc(tap_done, 1)
                            taps += 1
                    last.then_inc(conv_done, 1)
                v, nabs, relu = small[:, 720:784], small[:, 784:848], small[:, 848:912]
                dve.tensor_tensor(v.rearrange("p (t h) -> p t h", t=NT), dt,
                                  row("dt_bias").unsqueeze(1).broadcast_to([P, NT, 16]), ALU.add).then_inc(dt_chain, 1)
                dve.wait_ge(dt_chain, 1)
                dve.scalar_tensor_tensor(nabs, v, -1.0, v, ALU.mult, ALU.min).then_inc(dt_biased, 1)
                dve.tensor_scalar(relu, v, 0.0, None, ALU.max).then_inc(dt_chain, 1)
                dve.wait_ge(dt_ln, 1)
                dve.wait_ge(dt_chain, 2)
                dve.tensor_tensor(dtv, relu, nabs, ALU.add).then_inc(dt_chain, 1)
                dve.wait_ge(dt_chain, 3)
                dve.tensor_tensor(dta.rearrange("p (t h) -> p t h", t=NT), dtv.rearrange("p (t h) -> p t h", t=NT),
                                  neg_a.unsqueeze(1).broadcast_to([P, NT, 16]), ALU.mult).then_inc(dta_ready, 1)

            @block.scalar
            def _(act):
                for j in range(12):
                    acc = arena[:, CONV + (j % 2) * 512:CONV + (j % 2) * 512 + 512]
                    act.wait_ge(conv_done, j + 1)
                    act.activation(xbc[:, j, :], acc, ACT.Silu).then_inc(silu_done, 1)
                nabs = small[:, 784:848]
                act.wait_ge(dt_biased, 1)
                act.activation(nabs, nabs, ACT.Exp).then_inc(dt_exp, 1)
                act.wait_ge(dt_exp, 1)
                act.activation(nabs, nabs, ACT.Ln, bias=1.0).then_inc(dt_ln, 1)

        turned_x, xs_out_act, xs_out_dve, decay_sums, decays_ready, cb_done, cb_masked, xdt_ready = (
            sem(m) for m in ("turned_x", "xs_out_act", "xs_out_dve", "decay_sums", "decays_ready", "cb_done",
                             "cb_masked", "xdt_ready"))
        with nc.Block() as block:
            @block.tensor
            def _(pe):
                for i in range(10):
                    t, half = (i // 2, i % 2) if i < 8 else (2 * (i - 8), 2)
                    b = i % 5
                    if i >= 5:
                        pe.wait_ge(xs_out_act if (i - 5) % 2 == 0 else xs_out_dve, (i - 5) // 2 + 1)
                    for j in range(4):
                        if half < 2:
                            src = xbc[:, half * 4 + j, t * P:(t + 1) * P]
                        else:
                            src = xbc[:, 8 + j % 2, (t + j // 2) * P:(t + j // 2 + 1) * P]
                        last = pe.transpose(ps[:, b, j * P:(j + 1) * P], src, ident)
                    last.then_inc(turned_x, 1)
                for j, name in enumerate(("tri_le", "tri_gt", "ones")):
                    last = pe.matmul(ps[:, 5, j * 64:(j + 1) * 64], const(name), dta, start=True, stop=True)
                last.then_inc(decay_sums, 1)
                for i in range(8):
                    c, g = i // 2, i % 2
                    last = pe.matmul(ps[:, 6 + i // 4, (i % 4) * P:(i % 4 + 1) * P], xbc[:, 8 + g, c * P:(c + 1) * P],
                                     xbc[:, 10 + g, c * P:(c + 1) * P], start=True, stop=True)
                last.then_inc(cb_done, 1)

            def xs_dst(i):
                if i < 8:
                    return xs_tok[:, i // 2, (i % 2) * 512:(i % 2 + 1) * 512]
                return scr[:, (i - 8) * 512:(i - 7) * 512]

            @block.scalar
            def _(act):
                for i in range(0, 10, 2):
                    act.wait_ge(turned_x, i + 1)
                    act.activation(xs_dst(i), ps[:, i % 5, :], ACT.Copy).then_inc(xs_out_act, 1)
                act.wait_ge(decay_sums, 1)
                act.activation(decays, ps[:, 5, 0:192], ACT.Exp).then_inc(decays_ready, 1)

            @block.vector
            def _(dve):
                for i in range(1, 10, 2):
                    dve.wait_ge(turned_x, i + 1)
                    dve.tensor_copy(xs_dst(i), ps[:, i % 5, :]).then_inc(xs_out_dve, 1)
                dve.wait_ge(cb_done, 1)
                for i in range(2):
                    dve.tensor_tensor(cbm[:, 4 * i:4 * i + 4, :],
                                      ps[:, 6 + i, :].rearrange("p (i l) -> p i l", i=4),
                                      const("tri_le").unsqueeze(1).broadcast_to([P, 4, P]), ALU.mult)\
                       .then_inc(cb_masked, 1)
                dve.wait_ge(xs_out_act, 4)
                dve.wait_ge(xs_out_dve, 4)
                for t in range(NT):
                    dve.tensor_tensor(xdt[:, t, :].rearrange("p (h d) -> p h d", h=SSD_H),
                                      xs_tok[:, t, :].rearrange("p (h d) -> p h d", h=SSD_H),
                                      dtv[:, t * 16:(t + 1) * 16].unsqueeze(2).broadcast_to([P, SSD_H, SSD_P]),
                                      ALU.mult).then_inc(xdt_ready, 1)

        dstr_ready, xdd_ready, segs_done, segs_exp, mixed_s, y_done, st_done, st_out, y_out, ssd_chain = (
            sem(m) for m in ("dstr_ready", "xdd_ready", "segs_done", "segs_exp", "mixed_s", "y_done", "st_done",
                             "st_out", "y_out", "ssd_chain"))
        with nc.Block() as block:
            @block.tensor
            def _(pe):
                for i in range(8):
                    c, g = i // 2, i % 2
                    pe.wait_ge(dstr_ready, i + 1)
                    if i:
                        pe.wait_ge(segs_exp, 2 * i)
                    for j in range(8):
                        last = pe.matmul(ps[:, j // 4, (j % 4) * P:(j % 4 + 1) * P], dstr[:, j, :], const("tri_le"),
                                         start=True, stop=True)
                        if j % 4 == 3:
                            last.then_inc(segs_done, 1)
                    if i:
                        pe.wait_ge(y_out, i)
                    if c > 0:
                        pe.wait_ge(st_out, i - 1)
                        last = pe.matmul(ps[:, 3, :], xbc[:, 10 + g, c * P:(c + 1) * P], state[:, g, :],
                                         start=True, stop=True)
                    pe.wait_ge(mixed_s, i + 1)
                    for j in range(8):
                        h = g * 8 + j
                        last = pe.matmul(ps[:, 2, j * 64:(j + 1) * 64], exps[:, j, :],
                                         xdt[:, c, h * 64:(h + 1) * 64], start=True, stop=True)
                    last.then_inc(y_done, 1)
                    pe.wait_ge(xdd_ready, i + 1)
                    if i:
                        pe.wait_ge(st_out, i)
                    pe.matmul(ps[:, 4, :], b_tok[:, c, g * P:(g + 1) * P], xdd, start=True, stop=True)\
                      .then_inc(st_done, 1)

            @block.scalar
            def _(act):
                for i in range(8):
                    for half in range(2):
                        act.wait_ge(segs_done, 2 * i + half + 1)
                        if i and half == 0:
                            act.wait_ge(y_done, i)
                        act.activation(exps[:, 4 * half:4 * half + 4, :],
                                       ps[:, half, :].rearrange("p (i l) -> p i l", i=4), ACT.Exp)\
                           .then_inc(segs_exp, 1)

            @block.vector
            def _(dve):
                links = [0]

                def link(ins):
                    links[0] += 1
                    ins.then_inc(ssd_chain, 1)
                    dve.wait_ge(ssd_chain, links[0])

                def per_head(a):
                    return a.unsqueeze(2).broadcast_to([P, 8, SSD_P])

                def heads(a):
                    return a.rearrange("p (h d) -> p h d", h=8)

                for i in range(8):
                    c, g = i // 2, i % 2
                    hs = slice(c * 16 + g * 8, c * 16 + g * 8 + 8)
                    if i:
                        dve.wait_ge(segs_done, 2 * i)
                    dve.tensor_tensor(dstr, const("tri_gt").unsqueeze(1).broadcast_to([P, 8, P]),
                                      dta[:, hs].unsqueeze(2).broadcast_to([P, 8, P]), ALU.mult)\
                       .then_inc(dstr_ready, 1)
                    if i:
                        dve.wait_ge(st_done, i)
                    dve.tensor_tensor(heads(xdd), heads(xdt[:, c, g * 512:(g + 1) * 512]),
                                      per_head(decays[:, 64 + hs.start:64 + hs.stop]), ALU.mult)\
                       .then_inc(xdd_ready, 1)
                    dve.wait_ge(segs_exp, 2 * i + 2)
                    dve.tensor_tensor(exps, exps, cbm[:, i:i + 1, :].broadcast_to([P, 8, P]), ALU.mult)\
                       .then_inc(mixed_s, 1)
                    y = y_b[:, c, g * 512:(g + 1) * 512]
                    dsk = row("d_skip")[:, g * 8:(g + 1) * 8]
                    link(dve.tensor_tensor(heads(y), heads(xs_tok[:, c, g * 512:(g + 1) * 512]), per_head(dsk),
                                           ALU.mult))
                    dve.wait_ge(y_done, i + 1)
                    if c > 0:
                        tmp = arena[:, CONV:CONV + 512]
                        link(dve.tensor_tensor(heads(tmp), heads(ps[:, 3, :]), per_head(decays[:, hs]), ALU.mult))
                        link(dve.tensor_tensor(y, y, tmp, ALU.add))
                    dve.tensor_tensor(y, ps[:, 2, :], y, ALU.add).then_inc(y_out, 1)
                    dve.wait_ge(y_out, i + 1)
                    link(dve.tensor_tensor(y, y, z_tok[:, c, g * 512:(g + 1) * 512], ALU.mult))
                    if c > 0:
                        link(dve.tensor_tensor(heads(state[:, g, :]), heads(state[:, g, :]),
                                               per_head(decays[:, 128 + hs.start:128 + hs.stop]), ALU.mult))
                        dve.wait_ge(st_done, i + 1)
                        dve.tensor_tensor(state[:, g, :], ps[:, 4, :], state[:, g, :], ALU.add).then_inc(st_out, 1)
                    else:
                        dve.wait_ge(st_done, i + 1)
                        dve.tensor_copy(state[:, g, :], ps[:, 4, :]).then_inc(st_out, 1)

        group_norm("ssdn", y_b, 512, EPS_A, None)
        turn("yb", lambda t, k: y_b[:, t, k * P:(k + 1) * P], lambda k: yT_a[:, 8 + k, :], 8,
             lambda k: col("ssd_norm", k))
        combine("out_a", "out_a", lambda k: yT_a[:, k, :], 16)

        recycle()
        norm("norm_c", x, NT, EPS_A, "norm_c", part(0, [NT, D]))
        qT, kT, v_tok = part(0, [8, S]), part(4096, [2, S]), part(5120, [NT, P])
        g_tok, o_tok, oT = part(5632, [NT, D]), part(9728, [NT, D]), part(13824, [8, S])
        jobs = [("F",)] * 10 + [("T", 128, 8)] + [("T", 512, 2)] * 2
        outs = [("dve", "bias", qT[:, j, :], (col("bq", j), 0.125)) for j in range(8)]
        outs += [("dve", "bias", kT[:, j, :], (col("bk", j), 1.0)) for j in range(2)]
        outs += [("dve", "add_row", v_tok[:, t, :], row("bv")) for t in range(NT)]
        for c in range(2):
            outs += [("dve", "add_row", g_tok[:, t, c * 512:(c + 1) * 512], big_row[:, c * 512:(c + 1) * 512])
                     for t in range(NT)]
        project("in_c", "in_c", jobs, outs)
        gate_silu = sem("gate_silu")
        with nc.Block() as block:
            @block.scalar
            def _(act):
                for t in range(NT):
                    act.activation(g_tok[:, t, :], g_tok[:, t, :], ACT.Silu).then_inc(gate_silu, 1)

            @block.sync
            def _(sp):
                sp.dma_start(big_row[:, :], big_dram[1, :].partition_broadcast(P)).then_inc(big_loaded, 16)
        units = []
        for h in range(SW_H):
            kv, hp = h // 8, (h % 2) * 64
            for t in range(NT):
                lo = max(t - 1, 0) * P
                w = (t + 1) * P - lo
                units.append(dict(q=[token(qT[hp:hp + 64, h // 2, :], t)], k=[kT[hp:hp + 64, kv, lo:lo + w]], w=w,
                                  mask=const("sw")[:, 2 * P - w:], slope=2.0 ** (-8.0 * (h + 1) / SW_H),
                                  v=[v_tok[:, lo // P + b, kv * 64:kv * 64 + 64] for b in range(w // P)], dv=64,
                                  out=o_tok[:, t, h * 64:(h + 1) * 64], sink=row("sinks")[:, h:h + 1],
                                  neg_sink=neg_sink[:, h:h + 1]))
        attend("sw", units)
        gated = sem("gated")
        with nc.Block() as block:
            @block.vector
            def _(dve):
                for t in range(NT):
                    dve.tensor_tensor(o_tok[:, t, :], o_tok[:, t, :], g_tok[:, t, :], ALU.mult).then_inc(gated, 1)
        turn("oc", lambda t, k: o_tok[:, t, k * P:(k + 1) * P], lambda k: oT[:, k, :], 8)
        combine("out_c", "out_c", lambda k: oT[:, k, :], 8)

        def row_norm(tag, eps, store):
            squared, mean, rooted, scaled = (sem(tag + m) for m in ("_squared", "_mean", "_rooted", "_scaled"))
            with nc.Block() as block:
                @block.scalar
                def _(act):
                    for t in range(NT):
                        act.activation(scr[:, t * D:(t + 1) * D], x[:, t, :], ACT.Square, accum_out=ss[:, t:t + 1])\
                           .then_inc(squared, 1)

                @block.gpsimd
                def _(pool):
                    for t in range(NT):
                        pool.wait_ge(mean, t + 1)
                        pool.tensor_tensor(rs[:, t:t + 1], ms[:, t:t + 1], neg_half[:, 0:1], ALU.pow)\
                            .then_inc(rooted, 1)

                @block.vector
                def _(dve):
                    for t in range(NT):
                        dve.wait_ge(squared, t + 1)
                        dve.tensor_scalar(ms[:, t:t + 1], ss[:, t:t + 1], 1.0 / D, eps, ALU.mult, ALU.add)\
                           .then_inc(mean, 1)
                    dve.wait_ge(big_loaded, 48 if store else 32)
                    for t in range(NT):
                        dve.wait_ge(rooted, t + 1)
                        dve.scalar_tensor_tensor(x[:, t, :], x[:, t, :], rs[:, t:t + 1], big_row[:, :],
                                                 ALU.mult, ALU.mult).then_inc(scaled, 1)

                @block.sync
                def _(sp):
                    if store:
                        for t in range(NT):
                            sp.wait_ge(scaled, t + 1)
                            sp.dma_start(out_dram[t * P:(t + 1) * P, :], x[:, t, :]).then_inc(stored, 16)
                        sp.wait_ge(stored, 16 * NT)

        row_norm("final_a", EPS_A, False)

        recycle()
        norm("norm_m", x, NT, EPS_B, "norm_mix", part(0, [NT, D]))
        ft = part(0, [15, S])
        tv = part(7680, [NT, 512])
        gm = part(9728, [NT, 3 * D])
        o_abc = part(22016, [NT, 768])
        jobs = [("F",)] * 15 + [("T", 512, 2)] * 7
        outs = []
        for j in range(15):
            scale = 0.125 if j in (0, 1, 4, 5, 11, 12) else 1.0
            outs.append(("act" if j % 2 == 0 else "dve", "copy", ft[:, j, :], scale))
        outs += [("dve", "copy", tv[:, t, :], 1.0) for t in range(NT)]
        for c in range(6):
            outs += [("act", "sigmoid", gm[:, t, c * 512:(c + 1) * 512], None) for t in range(NT)]
        project("in_m", "in_m", jobs, outs)

        swapped, sin_done, cos_done, rope_done, gates_done, widx_done = (
            sem(m) for m in ("swapped", "sin_done", "cos_done", "rope_done", "gates_done", "widx_done"))
        with nc.Block() as block:
            @block.tensor
            def _(pe):
                for j in range(11):
                    if j >= 8:
                        pe.wait_ge(sin_done, j - 7)
                    pe.matmul(ps[:, j % 8, :], const("perm"), ft[:, j, :], start=True, stop=True).then_inc(swapped, 1)

            @block.vector
            def _(dve):
                for j in range(11):
                    hp = P if j < 10 else 64
                    tmp = scr[0:hp, (j % 4) * 512:(j % 4 + 1) * 512]
                    dve.wait_ge(swapped, j + 1)
                    dve.tensor_tensor(tmp, ps[0:hp, j % 8, :], const("sin")[0:hp, :], ALU.mult).then_inc(sin_done, 1)
                    dve.tensor_tensor(ft[0:hp, j, :], ft[0:hp, j, :], const("cos")[0:hp, :], ALU.mult)\
                       .then_inc(cos_done, 1)
                    dve.wait_ge(sin_done, j + 1)
                    dve.wait_ge(cos_done, j + 1)
                    dve.tensor_tensor(ft[0:hp, j, :], ft[0:hp, j, :], tmp, ALU.add).then_inc(rope_done, 1)
                for t in range(NT):
                    dve.tensor_scalar(tv[:, t, 448:452], tv[:, t, 448:452], 1.0 / 16, None, ALU.mult)\
                       .then_inc(widx_done, 1)

            @block.scalar
            def _(act):
                for t in range(NT):
                    act.activation(tv[:, t, 452:464], tv[:, t, 452:464], ACT.Sigmoid).then_inc(gates_done, 1)

        sa_names = ["sb_z", "sb_nabs", "sb_exp", "sb_ln", "sb_sp", "sb_mask", "sb_sum", "sb_w", "sb_o", "sb_out"]
        sb_z, sb_nabs, sb_exp, sb_ln, sb_sp, sb_mask, sb_sum, sb_w, sb_o, sb_out = (sem(m) for m in sa_names)
        nab = scr[:, 0:2048].rearrange("p (b q) -> p b q", b=NT)
        spl = scr[:, 2048:4096].rearrange("p (b q) -> p b q", b=NT)
        with nc.Block() as block:
            @block.tensor
            def _(pe):
                for h in range(4):
                    hp = (h % 2) * 64
                    qh, kh = ft[hp:hp + 64, 11 + h // 2, :], ft[hp:hp + 64, 13 + h // 2, :]
                    if h:
                        pe.wait_ge(sb_sp, 4 * h)
                    for b in range(NT):
                        pe.matmul(ps[:, b, b * P:S], kh[:, b * P:(b + 1) * P], qh[:, b * P:S], start=True, stop=True)\
                          .then_inc(sb_z, 1)
                    pe.wait_ge(sb_mask, 4 * (h + 1))
                    if h:
                        pe.wait_ge(sb_out, 4 * h)
                    for b in range(NT):
                        bank = ps[:, 4 + b, b * P:S]
                        pe.matmul(bank, kh[:, b * P:(b + 1) * P], qh[:, b * P:S], start=True, stop=False)
                        pe.matmul(bank, const("neg_ge"), spl[:, b, b * P:S], start=False, stop=False)
                        for later in range(b + 1, NT):
                            pe.matmul(ps[:, 4 + b, later * P:S], const("neg_ones"), spl[:, later, later * P:S],
                                      start=False, stop=False)
                        pe.matmul(ps[:, 4 + b, b * P:(b + 1) * P], ident, const("strict_neg"), start=False, stop=True)\
                          .then_inc(sb_sum, 1)
                    pe.wait_ge(sb_w, 4 * (h + 1))
                    for t in range(NT):
                        for b in range(t + 1):
                            last = pe.matmul(ps[:, 4 + t, 0:64], nab[:, b, t * P:(t + 1) * P],
                                             tv[:, b, h * 64:(h + 1) * 64], start=b == 0, stop=b == t)
                        last.then_inc(sb_o, 1)

            @block.scalar
            def _(act):
                for h in range(4):
                    for b in range(NT):
                        act.wait_ge(sb_z, 4 * h + b + 1)
                        if h and b == 0:
                            act.wait_ge(sb_o, 4 * h)
                        act.activation(nab[:, b, b * P:S], ps[:, b, b * P:S], ACT.Abs).then_inc(sb_nabs, 1)
                    for b in range(NT):
                        act.wait_ge(sb_nabs, 4 * h + b + 1)
                        act.activation(nab[:, b, b * P:S], nab[:, b, b * P:S], ACT.Exp, scale=-1.0).then_inc(sb_exp, 1)
                    for b in range(NT):
                        act.wait_ge(sb_exp, 4 * h + b + 1)
                        act.activation(nab[:, b, b * P:S], nab[:, b, b * P:S], ACT.Ln, bias=1.0).then_inc(sb_ln, 1)
                    for b in range(NT):
                        act.wait_ge(sb_sum, 4 * h + b + 1)
                        act.activation(nab[:, b, b * P:S], ps[:, 4 + b, b * P:S], ACT.Exp).then_inc(sb_w, 1)

            @block.vector
            def _(dve):
                for h in range(4):
                    for b in range(NT):
                        dve.wait_ge(sb_ln, 4 * h + b + 1)
                        if h and b == 0:
                            dve.wait_ge(sb_sum, 4 * h)
                        dve.scalar_tensor_tensor(spl[:, b, b * P:S], ps[:, b, b * P:S], 0.0, nab[:, b, b * P:S],
                                                 ALU.max, ALU.add).then_inc(sb_sp, 1)
                        dve.wait_ge(sb_sp, 4 * h + b + 1)
                        dve.tensor_tensor(spl[:, b, b * P:(b + 1) * P], spl[:, b, b * P:(b + 1) * P],
                                          const("strict01"), ALU.mult).then_inc(sb_mask, 1)
                    for t in range(NT):
                        dve.wait_ge(sb_o, 4 * h + t + 1)
                        dve.tensor_copy(o_abc[:, t, h * 64:(h + 1) * 64], ps[:, 4 + t, 0:64]).then_inc(sb_out, 1)

        sel = hT[:, 0:2048].rearrange("p (t s) -> p t s", t=NT)
        relu_h = hT[:, 2048:4096].rearrange("p (h s) -> p h s", h=4)
        ix_scored, ix_relu, ix_sum, ix_top, ix_sel = (
            sem(m) for m in ("ix_scored", "ix_relu", "ix_sum", "ix_top", "ix_sel"))
        with nc.Block() as block:
            @block.tensor
            def _(pe):
                for t in range(1, NT):
                    w = (t + 1) * P
                    for h in range(4):
                        i = 4 * (t - 1) + h
                        hp = (h % 2) * 64
                        if i >= 8:
                            pe.wait_ge(ix_relu, i - 7)
                        pe.matmul(ps[:, i % 8, 0:w], ft[hp:hp + 64, 2 + h // 2, t * P:(t + 1) * P],
                                  ft[hp:hp + 64, 7, 0:w], start=True, stop=True).then_inc(ix_scored, 1)

            @block.scalar
            def _(act):
                for i in range(12):
                    t, h = 1 + i // 4, i % 4
                    w = (t + 1) * P
                    act.wait_ge(ix_scored, i + 1)
                    if t >= 2:
                        act.wait_ge(ix_sum, 4 * (t - 2) + h + 1)
                    act.activation(relu_h[:, h, 0:w], ps[:, i % 8, 0:w], ACT.Relu).then_inc(ix_relu, 1)

            @block.vector
            def _(dve):
                sums = tops = 0
                for t in range(1, NT):
                    w = (t + 1) * P
                    score = sel[:, t, 0:w]
                    acc = const("causal")[:, S - w:S]
                    for h in range(4):
                        dve.wait_ge(ix_relu, 4 * (t - 1) + h + 1)
                        if sums % 4:
                            dve.wait_ge(ix_sum, sums)
                        dve.scalar_tensor_tensor(score, relu_h[:, h, 0:w], tv[:, t, 448 + h:449 + h], acc,
                                                 ALU.mult, ALU.add).then_inc(ix_sum, 1)
                        sums += 1
                        acc = score
                    dve.wait_ge(ix_sum, sums)
                    for r in range(P // 8):
                        top = small[:, 912 + 8 * (r % 2):920 + 8 * (r % 2)]
                        dve.max(top, score).then_inc(ix_top, 1)
                        dve.wait_ge(ix_top, tops + 1)
                        dve.match_replace(score, top, score, -3.0e38).then_inc(ix_top, 1)
                        dve.wait_ge(ix_top, tops + 2)
                        tops += 2
                    dve.tensor_scalar(score, score, -2.0e38, NEG, ALU.is_gt, ALU.mult).then_inc(ix_sel, 1)

        units = []
        for t in range(NT):
            w = (t + 1) * P
            for h in range(4):
                hp = (h % 2) * 64
                units.append(dict(q=[ft[hp:hp + 64, h // 2, t * P:(t + 1) * P]], k=[ft[hp:hp + 64, 6, 0:w]], w=w,
                                  mask=sel[:, t, 0:w] if t else const("causal")[:, S - w:S], slope=1.0,
                                  v=[tv[:, b, 256:320] for b in range(t + 1)], dv=64,
                                  out=o_abc[:, t, 256 + h * 64:256 + (h + 1) * 64]))
        attend("dsa", units)

        blocks = part(25088, [32, 32])
        hid = scr[:, 0:64]
        kc_T = scr[:, 64:96]
        vc = scr[0:32, 96:160]
        cm_blocks, cm_hid, cm_gelu, cm_two, cm_out, cm_zero = (
            sem(m) for m in ("cm_blocks", "cm_hid", "cm_gelu", "cm_two", "cm_out", "cm_zero"))
        with nc.Block() as block:
            @block.sync
            def _(sp):
                stream(sp, "cmp")

            @block.vector
            def _(dve):
                dve.memset(hid, 0.0).then_inc(cm_zero, 1)
                src = ft[:, 10, :].rearrange("p (n j) -> p j n", j=16)
                for half in range(2):
                    dve.tensor_tensor(blocks[:, half * 16:half * 16 + 16, 0:N_CMP], src[:, :, half:half + N_CMP],
                                      col("pos", half * 16, 16).unsqueeze(2).broadcast_to([P, 16, N_CMP]),
                                      ALU.add).then_inc(cm_blocks, 1)
                dve.wait_ge(cm_two, 1)
                dve.tensor_copy(kc_T, ps[:, 2, 0:32]).then_inc(cm_out, 1)
                dve.tensor_copy(vc, ps[0:32, 3, 0:64]).then_inc(cm_out, 1)

            @block.scalar
            def _(act):
                act.wait_ge(cm_zero, 1)
                act.wait_ge(cm_hid, 1)
                for j in range(2):
                    act.activation(hid[:, j * 32:j * 32 + N_CMP], ps[:, j, 0:N_CMP], ACT.Gelu_apprx_tanh)\
                       .then_inc(cm_gelu, 1)

            @block.tensor
            def _(pe):
                pe.wait_ge(cm_blocks, 2)
                u = START["cmp"]
                for q in range(4):
                    w = unit(pe, u + q)
                    for l in range(8):
                        for j in range(2):
                            mm = pe.matmul(ps[:, j, 0:N_CMP], w[j * 64:j * 64 + 64, l * P:(l + 1) * P],
                                           blocks[j * 64:j * 64 + 64, q * 8 + l, 0:N_CMP],
                                           start=q + l == 0, stop=q * 8 + l == 31)
                            if l + j == 0:
                                mm.then_inc(weights_used, 1)
                mm.then_inc(cm_hid, 1)
                w = unit(pe, u + 4)
                pe.wait_ge(cm_gelu, 2)
                pe.matmul(ps[:, 2, 0:32], w[:, 0:P], hid[:, 0:32], start=True, stop=True).then_inc(weights_used, 1)
                pe.matmul(ps[0:32, 3, 0:64], hid[:, 32:64], w[:, P:P + 64], start=True, stop=True).then_inc(cm_two, 1)

        cmp_store = hT[:, 2048:2208]
        moved = sem("moved")
        with nc.Block() as block:
            @block.vector
            def _(dve):
                dve.tensor_copy(cmp_store[:, 0:32], kc_T).then_inc(moved, 1)
                dve.tensor_copy(cmp_store[0:32, 32:96], vc).then_inc(moved, 1)
        units = []
        for t in range(NT):
            for h in range(4):
                hp = (h % 2) * 64
                units.append(dict(q=[ft[hp:hp + 64, 4 + h // 2, t * P:(t + 1) * P]], k=[cmp_store[hp:hp + 64, 0:32]],
                                  w=32, mask=const("cmp_neg")[:, t * 32:(t + 1) * 32], slope=1.0,
                                  keep01=const("cmp01")[:, t * 32:(t + 1) * 32], v=[cmp_store[0:32, 32:96]], dv=64,
                                  out=o_abc[:, t, 512 + h * 64:512 + (h + 1) * 64],
                                  gate=tv[:, t, 452 + 3 * h:453 + 3 * h]))
        attend("cmpa", units, keep=True)
        units = []
        for j, (kt, vo) in enumerate(((8, 320), (9, 384))):
            for t in range(NT):
                w = (t + 1) * P
                for h in range(4):
                    hp = (h % 2) * 64
                    units.append(dict(q=[ft[hp:hp + 64, 4 + h // 2, t * P:(t + 1) * P]], k=[ft[hp:hp + 64, kt, 0:w]],
                                      w=w, mask=const("causal")[:, S - w:S], slope=1.0,
                                      v=[tv[:, b, vo:vo + 64] for b in range(t + 1)], dv=64,
                                      out=o_abc[:, t, 512 + h * 64:512 + (h + 1) * 64],
                                      gate=tv[:, t, 453 + j + 3 * h:454 + j + 3 * h], add=True))
        attend("swa", units)

        oT = part(0, [6, S])
        turn("om", lambda t, k: o_abc[:, t, k * P:(k + 1) * P], lambda k: oT[:, k, :], 6)
        merged = part(3072, [NT, D])
        up_done, up_gated, up_added = sem("up_done"), sem("up_gated"), sem("up_added")
        with nc.Block() as block:
            @block.sync
            def _(sp):
                stream(sp, "up")

            @block.tensor
            def _(pe):
                for br in range(3):
                    for k in range(2):
                        w = unit(pe, START["up"] + 2 * br + k)
                        for b in range(8):
                            if br and k == 0:
                                pe.wait_ge(up_gated, 8 * (br - 1) + b + 1)
                            mm = pe.matmul(ps[:, b, :], oT[:, 2 * br + k, (b // 2) * P:(b // 2 + 1) * P],
                                           w[:, (b % 2) * 512:(b % 2 + 1) * 512], start=k == 0, stop=k == 1)
                            if b == 0:
                                mm.then_inc(weights_used, 1)
                            elif k == 1:
                                mm.then_inc(up_done, 1)

            @block.vector
            def _(dve):
                for br in range(3):
                    for b in range(8):
                        t, cs = b // 2, slice((b % 2) * 512, (b % 2 + 1) * 512)
                        gate = gm[:, t, br * D + cs.start:br * D + cs.stop]
                        dve.wait_ge(up_done, 7 * br + max(b, 1))
                        dst = merged[:, t, cs] if br == 0 else scr[:, (b % 4) * 512:(b % 4 + 1) * 512]
                        dve.tensor_tensor(dst, ps[:, b, :], gate, ALU.mult).then_inc(up_gated, 1)
                        if br:
                            dve.wait_ge(up_gated, 8 * br + b + 1)
                            dve.tensor_tensor(merged[:, t, cs], merged[:, t, cs], dst, ALU.add).then_inc(up_added, 1)
        mT = part(9728, [8, S])
        turn("mt", lambda t, k: merged[:, t, k * P:(k + 1) * P], lambda k: mT[:, k, :], 8)
        combine("out_m", "out_m", lambda k: mT[:, k, :], 8)

        recycle()
        mem_loaded = sem("mem_loaded")
        mem_x, mem_kT, mem_v = part(8192, [2, D]), part(10240, [2, 256]), part(10752, [2, 256])
        mem_q, o_mem, omT = part(11264, [2, S]), part(12288, [NT, 256]), part(13312, [2, S])
        with nc.Block() as block:
            @block.sync
            def _(sp):
                sp.dma_start(mem_x, mem_dram.rearrange("(t p) d -> p t d", p=P)).then_inc(mem_loaded, 16)
                sp.dma_start(big_row[:, :], big_dram[2, :].partition_broadcast(P)).then_inc(big_loaded, 16)
                sp.wait_ge(mem_loaded, 16)
        norm("norm_kv", mem_x, 2, EPS_B, "norm_mem_kv", part(0, [NT, D]))
        project("mem_kv", "mem_kv", [("F",)] * 2 + [("T", 256, 4)],
                [("act", "copy", mem_kT[:, 0, :], 1.0), ("dve", "copy", mem_kT[:, 1, :], 1.0),
                 ("act", "copy", mem_v[:, 0, :], 1.0), ("dve", "copy", mem_v[:, 1, :], 1.0)], nt=2)
        norm("norm_q", x, NT, EPS_B, "norm_mem_q", part(0, [NT, D]))
        project("mem_q", "mem_q", [("F",)] * 2,
                [("act", "copy", mem_q[:, 0, :], 0.125), ("dve", "copy", mem_q[:, 1, :], 0.125)])
        units = []
        for h in range(4):
            hp = (h % 2) * 64
            for t in range(NT):
                units.append(dict(q=[mem_q[hp:hp + 64, h // 2, t * P:(t + 1) * P]], k=[mem_kT[hp:hp + 64, h // 2, :]],
                                  w=256, mask=None, slope=1.0, v=[mem_v[:, b, h * 64:(h + 1) * 64] for b in range(2)],
                                  dv=64, out=o_mem[:, t, h * 64:(h + 1) * 64]))
        attend("mem", units)
        turn("omem", lambda t, k: o_mem[:, t, k * P:(k + 1) * P], lambda k: omT[:, k, :], 2)
        combine("mem_out", "mem_out", lambda k: omT[:, k, :], 2)

        norm("norm_f", x, NT, EPS_B, "norm_ffn", part(0, [NT, D]))
        ff = part(0, [NFF, S])
        outs = []
        for j in range(NFF):
            outs += [("act", "silu", ff[:, j, :], None), ("dve", "times", ff[:, j, :], j + 1)]
        project("ffn_in", "ffn_in", [("F",)] * (2 * NFF), outs)
        combine("ffn_out", "ffn_out", lambda k: ff[:, k, :], NFF)
        row_norm("final_b", EPS_B, True)


def tables():
    c = np.zeros((P, N_CONST), np.float32)
    i, j = np.arange(P)[:, None], np.arange(P)[None, :]

    def put(name, value):
        a, w = CONSTS[name]
        c[:, a:a + w] = value

    put("ident", i == j)
    put("tri_le", i <= j)
    put("tri_gt", i > j)
    put("neg_ge", -1.0 * (i >= j))
    put("neg_ones", -1.0)
    put("ones", 1.0)
    put("strict_neg", np.where(i < j, 0.0, NEG))
    put("strict01", i < j)
    u = np.arange(S)[None, :] - (S - P)
    put("alibi", np.where(u <= i, u - i, NEG))
    put("causal", np.where(u <= i, 0.0, NEG))
    d = i + P - np.arange(2 * P)[None, :]
    put("sw", np.where((d >= 0) & (d < P), -d, NEG))
    inv = np.float32(10000.0) ** (-np.arange(0, 64, 2, dtype=np.float32) / np.float32(64))
    ang = np.arange(S, dtype=np.float32)[None, :] * inv.astype(np.float32)[:, None]
    put("cos", np.tile(np.cos(ang), (4, 1)))
    put("sin", np.concatenate([-np.sin(ang), np.sin(ang)] * 2, 0))
    put("perm", (i // 32 ^ 1) * 32 + i % 32 == j)
    n = np.arange(32)[None, :]
    for t in range(NT):
        ok = (n < N_CMP) & (n * 16 + 31 <= t * P + i)
        a = CONSTS["cmp_neg"][0] + t * 32
        c[:, a:a + 32] = np.where(ok, 0.0, NEG)
        a = CONSTS["cmp01"][0] + t * 32
        c[:, a:a + 32] = ok
    return c


def kernel(**inputs):
    import concourse.bacc as bacc
    from concourse.bass_utils import run_bass_kernel_spmd

    a = {k: np.asarray(v, np.float32) for k, v in inputs.items()}

    stream = []

    def feature(w):
        for j in range(w.shape[1] // P):
            stream.append(w[:, j * P:(j + 1) * P].reshape(KD, P, P).transpose(1, 0, 2).reshape(P, UNIT))

    def chunk(w, n, bk):
        for j in range(w.shape[1] // n):
            for b in range(KD // bk):
                v = w[b * bk * P:(b + 1) * bk * P, j * n:(j + 1) * n].reshape(bk, P, n).transpose(1, 0, 2)
                stream.append(padded(v.reshape(P, bk * n)))

    def rows_of(w):
        for k in range(w.shape[0] // P):
            stream.append(w[k * P:(k + 1) * P, :])

    def padded(v):
        return v if v.shape[1] == UNIT else np.concatenate([v, np.zeros((P, UNIT - v.shape[1]), np.float32)], 1)

    w = a["w_in_a"][0]
    feature(w[:, 0:2048])
    feature(w[:, 5120:6656])
    chunk(w[:, 2048:5120], 512, 2)
    chunk(w[:, 6656:6672], 16, 8)
    rows_of(a["w_out_a"][0])
    w = a["w_in_c"][0]
    feature(w[:, 0:1024])
    feature(np.concatenate([w[:, 1024:1088]] * 2 + [w[:, 1088:1152]] * 2, 1))
    chunk(w[:, 1152:1280], 128, 8)
    chunk(w[:, 1280:2304], 512, 2)
    rows_of(a["w_out_c"][0])
    w = a["w_in_2"][0]
    names = ["q_a", 256, "k_a", 256, "v_a", 256, "q_b", 256, "k_b", 64, "v_b", 64, "q_idx", 256, "k_idx", 64,
             "w_idx", 4, "q_c", 256, "k_cmp", 64, "v_cmp", 64, "k_sel", 64, "v_sel", 64, "k_win", 64, "v_win", 64,
             "g_c", 12, "g_merge", 3072]
    p, at = {}, 0
    for name, n in zip(names[::2], names[1::2]):
        p[name] = w[:, at:at + n]
        at += n
    feature(np.concatenate([p["q_b"], p["q_idx"], p["q_c"]] + [p[n] for n in ("k_b", "k_idx", "k_sel", "k_win")
                                                              for _ in range(2)]
                           + [p["k_cmp"], p["v_cmp"], p["q_a"], p["k_a"]], 1))
    chunk(np.concatenate([p["v_a"], p["v_b"], p["v_sel"], p["v_win"], p["w_idx"], p["g_c"],
                          np.zeros((D, 48), np.float32)], 1), 512, 2)
    chunk(p["g_merge"], 512, 2)
    w1 = [a[n][0].reshape(4, 8, 64, P).transpose(0, 2, 1, 3).reshape(4, 64, UNIT) for n in ("cmp_w1_k_2", "cmp_w1_v_2")]
    for q in range(4):
        stream.append(np.concatenate([w1[0][q], w1[1][q]], 0))
    stream.append(padded(np.concatenate([a["cmp_w2_k_2"][0]] * 2 + [a["cmp_w2_v_2"][0]], 1)))
    for br in range(3):
        rows_of(a["w_up_2"][0, br])
    rows_of(a["w_out_2"][0])
    kv = a["w_mem_kv_2"][0]
    feature(kv[:, 0:256])
    chunk(kv[:, 256:512], 256, 4)
    feature(a["w_mem_q_2"][0])
    rows_of(a["w_mem_o_2"][0])
    w = a["w_ffn_in_2"][0]
    for j in range(NFF):
        feature(w[:, j * P:(j + 1) * P])
        feature(w[:, FF + j * P:FF + (j + 1) * P])
    rows_of(a["w_ffn_out_2"][0])
    assert len(stream) == N_UNITS
    weights = np.ascontiguousarray(np.stack(stream))

    def tiles(v):
        return v.reshape(-1, P).T

    pos = np.concatenate([a["cmp_pos_k_2"][0].T, a["cmp_pos_v_2"][0].T], 0)
    conv_w = a["conv_w_a"][0].reshape(4, 12, P).transpose(2, 1, 0).reshape(P, 48)
    bc = a["b_in_c"][0]
    cols = np.ascontiguousarray(np.concatenate(
        [tiles(a["norm_a"][0]), tiles(a["norm_c"][0]), tiles(a["norm_mix_2"][0]), tiles(a["norm_mem_q_2"][0]),
         tiles(a["norm_mem_kv_2"][0]), tiles(a["norm_ffn_2"][0]), tiles(a["ssd_norm_a"][0]), tiles(a["subln_a"][0]),
         conv_w, tiles(a["conv_b_a"][0]), tiles(bc[0:1024]),
         tiles(np.concatenate([bc[1024:1088]] * 2 + [bc[1088:1152]] * 2)), pos], 1))
    rows = np.ascontiguousarray(np.concatenate(
        [a["dt_bias_a"][0], a["a_log_a"][0], a["d_skip_a"][0], a["sinks_c"][0], a["lambda_q1_a"][0],
         a["lambda_k1_a"][0], a["lambda_q2_a"][0], a["lambda_k2_a"][0], bc[1152:1280]]))
    big = np.ascontiguousarray(np.stack([bc[1280:2304], a["final_norm"], a["norm_final_2"]]))

    nc = bacc.Bacc("TRN2", target_bir_lowering=False, num_devices=1,
                   dynamic_dma_scratch_size=1024)
    arrays = {"weights": weights, "x_in": np.ascontiguousarray(a["x"][0]),
              "mem_in": np.ascontiguousarray(a["mem_2"][0]), "tables": tables(), "cols_in": cols, "rows_in": rows,
              "big_in": big}
    args = [nc.dram_tensor(n, v.shape, F32, kind="ExternalInput").ap() for n, v in arrays.items()]
    out = nc.dram_tensor("out", (S, D), F32, kind="ExternalOutput").ap()
    build(nc, *args, out)
    got = run_bass_kernel_spmd(nc, [arrays], core_ids=[0])
    return got.results[0]["out"].reshape(1, S, D)
```

```python
import math
from contextlib import ExitStack

import concourse.bass as bass
import numpy as np
from concourse import mybir

F32 = mybir.dt.float32
F32R = mybir.dt.float32r
ALU = mybir.AluOpType
ACT = mybir.ActivationFunctionType
AXX = mybir.AxisListType.X

P = 128
D = 1024
S = 512
NT = S // P
KD = D // P
UNIT = 1024
NEG = -1.0e30
DA_H = 8
SSD_H = 16
SSD_P = 64
SW_H = 16
FF = 2816
NFF = FF // P
N_CMP = 31
EPS_A = 1e-5
EPS_B = 1e-6
LAMBDA_INIT = 0.8 - 0.6 * math.exp(-0.3 * 0)
RAW = 3
CUT = 2

CONSTS = {}
_at = 0
for _n, _w in [("ident", P), ("tri_le", P), ("tri_gt", P), ("neg_ge", P), ("neg_ones", P), ("strict_neg", P),
               ("strict01", P), ("ones", P), ("alibi", S), ("sw", 2 * P), ("causal", S), ("cos", S), ("sin", S),
               ("perm", P), ("cmp_neg", NT * 32), ("cmp01", NT * 32)]:
    CONSTS[_n] = (_at, _w)
    _at += _w
N_CONST = _at

COLS = {}
_at = 0
for _n, _w in [("norm_a", 8), ("norm_c", 8), ("norm_mix", 8), ("norm_mem_q", 8), ("norm_mem_kv", 8),
               ("norm_ffn", 8), ("ssd_norm", 8), ("subln", 1), ("conv_w", 48), ("conv_b", 12), ("bq", 8), ("bk", 2),
               ("pos", 32), ("bg", 8), ("w2", 192)]:
    COLS[_n] = (_at, _w)
    _at += _w
N_COLS = _at

ROWS = {}
_at = 0
for _n, _w in [("dt_bias", 16), ("a_log", 16), ("d_skip", 16), ("sinks", 16), ("lq1", 64), ("lk1", 64),
               ("lq2", 64), ("lk2", 64), ("bv", 128)]:
    ROWS[_n] = (_at, _w)
    _at += _w
N_ROWS = _at

STAGES = [("in_a", 33), ("in_a2", 20), ("out_a", 16), ("in_c", 11), ("in_c2", 8), ("out_c", 8), ("in_m", 19),
          ("in_m2", 10), ("in_m3", 14), ("cmp", 4), ("up", 6),
          ("out_m", 8), ("mem_kv", 4), ("mem_q", 2), ("mem_out", 2), ("ffn_in", 2 * NFF), ("ffn_out", NFF)]
START = {}
_at = 0
for _n, _c in STAGES:
    START[_n] = _at
    _at += _c
N_UNITS = _at


def build(nc, w_dram, x_dram, mem_dram, const_dram, cols_dram, rows_dram, big_dram, out_dram):
    ctx = ExitStack()
    with ctx:
        room = (nc.sbuf_bytes_remaining - 64) // 4
        fence = ctx.enter_context(nc.sbuf_tensor("fence", [P, room], F32))
        base = nc.sbuf_base - 4 * room
        top = [0]

        def at(name, shape, dtype, place):
            return nc.alloc_sbuf_tensor_at(name, shape, dtype, offset=base + 4 * place)

        def take(floats):
            place = top[0]
            top[0] += (floats + 7) // 8 * 8
            assert top[0] <= room, (top[0], room)
            return place

        def sb(name, shape):
            return at(name, shape, F32, take(math.prod(shape[1:])))

        raw = sb("raw", [P, RAW, UNIT])
        cut_hi = at("cut_hi", [P, CUT, UNIT], F32R, take(CUT * UNIT))
        cut_lo = at("cut_lo", [P, CUT, UNIT], F32R, take(CUT * UNIT))
        x = sb("x", [P, NT, D])
        H_PLACE, HL_PLACE = take(KD * S), take(KD * S)
        h_hi = at("h_hi", [P, KD, S], F32R, H_PLACE)
        h_lo = at("h_lo", [P, KD, S], F32R, HL_PLACE)
        consts = sb("consts", [P, N_CONST])
        cols = sb("cols", [P, N_COLS])
        rows = sb("rows", [P, N_ROWS])
        big_row = sb("big_row", [P, D])
        scr = sb("scr", [P, 4096])
        small = sb("small", [P, 936])
        ARENA = take(26784)
        arena = at("arena", [P, 26784], F32, ARENA)
        ps = ctx.enter_context(nc.psum_tensor("ps", [P, 8, 512], F32))

        def halves(name, place_hi, place_lo, n):
            return (at(name + "_hi", [P, n, S], F32R, place_hi), at(name + "_lo", [P, n, S], F32R, place_lo))

        stage_sems = []

        def sem(name):
            stage_sems.append(nc.alloc_semaphore(name))
            return stage_sems[-1]

        def lasting_sem(name):
            return ctx.enter_context(nc.semaphore(name))

        def recycle():
            with nc.Block() as block:
                @block.sync
                def _(sp):
                    for s in stage_sems:
                        sp.sem_clear(s)
            for s in stage_sems:
                nc.release_semaphore(s)
            stage_sems.clear()

        def const(name):
            a, w = CONSTS[name]
            return consts[:, a:a + w]

        def col(name, i=0, n=1):
            a = COLS[name][0] + i
            return cols[:, a:a + n]

        def row(name):
            a, w = ROWS[name]
            return rows[:, a:a + w]

        def part(a, shape):
            n = 1
            for d in shape:
                n *= d
            v = arena[:, a:a + n]
            if len(shape) == 2:
                return v.rearrange("p (a b) -> p a b", a=shape[0])
            return v

        ident = const("ident")
        ss = small[:, 0:64]
        ms = small[:, 64:128]
        rs = small[:, 128:192]
        neg_half = small[:, 192:256]
        subln8 = small[:, 257:258]
        neg_lam = small[:, 290:291]
        neg_a = small[:, 258:274]
        neg_sink = small[:, 274:290]
        neg_max = small[:, 300:308]
        den = small[:, 308:316]
        rden = small[:, 316:324]
        esink = small[:, 324:332]

        raw_loaded = [lasting_sem(f"raw_loaded{i}") for i in range(RAW)]
        hi_ready, lo_ready = lasting_sem("hi_ready"), lasting_sem("lo_ready")
        weights_used = lasting_sem("weights_used")
        stored = lasting_sem("stored")
        issued = [0]
        cut_before = [0]

        def stream(sp, n_cut):
            end = min(cut_before[0] + n_cut + RAW, N_UNITS)
            for u in range(issued[0], end):
                if u >= RAW:
                    sp.wait_ge(lo_ready, u - RAW + 1)
                sp.dma_start(raw[:, u % RAW, :], w_dram[u]).then_inc(raw_loaded[u % RAW], 16)
            issued[0] = max(issued[0], end)

        def cut_high(act, u, first):
            act.wait_ge(raw_loaded[u % RAW], 16 * (u // RAW + 1))
            if u - CUT >= first:
                act.wait_ge(weights_used, u - CUT + 1)
            act.activation(cut_hi[:, u % CUT, :], raw[:, u % RAW, :], ACT.Copy).then_inc(hi_ready, 1)

        def cut_low(eng, u):
            eng.wait_ge(hi_ready, u + 1)
            eng.tensor_tensor(cut_lo[:, u % CUT, :], raw[:, u % RAW, :], cut_hi[:, u % CUT, :].bitcast(F32),
                              ALU.subtract).then_inc(lo_ready, 1)

        def unit(pe, u):
            pe.wait_ge(lo_ready, u + 1)
            return cut_hi[:, u % CUT, :], cut_lo[:, u % CUT, :]


        def product(pe, out, left, right, start, stop):
            a = pe.matmul(out, left[0], right[0], start=start, stop=False)
            pe.matmul(out, left[0], right[1], start=False, stop=False)
            return a, pe.matmul(out, left[1], right[0], start=False, stop=stop)

        const_loaded, x_loaded, small_loaded, big_loaded = (
            sem("const_loaded"), lasting_sem("x_loaded"), sem("small_loaded"), lasting_sem("big_loaded"))
        setup_chain, lam_dots, lam_exps, sub_ready = sem("setup_chain"), sem("lam_dots"), sem("lam_exps"), sem("sub_ready")
        with nc.Block() as block:
            @block.sync
            def _(sp):
                sp.dma_start(x[:, :, :], x_dram.rearrange("(t p) d -> p t d", p=P)).then_inc(x_loaded, 16)
                stream(sp, 0)

            @block.scalar
            def _(act):
                act.dma_start(consts[:, :], const_dram).then_inc(const_loaded, 16)
                act.dma_start(cols[:, :], cols_dram).then_inc(small_loaded, 16)
                act.dma_start(rows[:, :], rows_dram.partition_broadcast(P)).then_inc(small_loaded, 16)
                act.wait_ge(lam_dots, 2)
                act.activation(small[:, 334:336], small[:, 332:334], ACT.Exp).then_inc(lam_exps, 1)
                act.activation(small[:, 336:352], row("a_log"), ACT.Exp).then_inc(lam_exps, 1)

            @block.vector
            def _(dve):
                dve.memset(neg_half, -0.5).then_inc(setup_chain, 1)
                dve.wait_ge(small_loaded, 32)
                dve.tensor_tensor(scr[:, 0:64], row("lq1"), row("lk1"), ALU.mult).then_inc(setup_chain, 1)
                dve.tensor_tensor(scr[:, 64:128], row("lq2"), row("lk2"), ALU.mult).then_inc(setup_chain, 1)
                dve.wait_ge(setup_chain, 3)
                dve.tensor_reduce(small[:, 332:333], scr[:, 0:64], AXX, ALU.add).then_inc(lam_dots, 1)
                dve.tensor_reduce(small[:, 333:334], scr[:, 64:128], AXX, ALU.add).then_inc(lam_dots, 1)
                dve.tensor_scalar(subln8, col("subln"), 1.0 - LAMBDA_INIT, None, ALU.mult).then_inc(sub_ready, 1)
                dve.tensor_scalar(neg_sink, row("sinks"), -1.0, None, ALU.mult).then_inc(sub_ready, 1)
                dve.wait_ge(lam_exps, 2)
                dve.tensor_scalar(neg_a, small[:, 336:352], -1.0, None, ALU.mult).then_inc(sub_ready, 1)
                dve.tensor_tensor(small[:, 352:353], small[:, 334:335], small[:, 335:336], ALU.subtract)\
                   .then_inc(setup_chain, 1)
                dve.wait_ge(setup_chain, 4)
                dve.tensor_scalar(neg_lam, small[:, 352:353], LAMBDA_INIT, -1.0, ALU.add, ALU.mult)\
                   .then_inc(sub_ready, 1)
                dve.wait_ge(const_loaded, 16)
                dve.wait_ge(x_loaded, 16)

        def norm(tag, src, nt, eps, gain, xs, ahead=None):
            squared, mean, rooted, scaled, turned, out_hi, out_lo = (
                sem(tag + n) for n in ("_squared", "_mean", "_rooted", "_scaled", "_turned", "_out_hi", "_out_lo"))
            n_tok = nt * P
            with nc.Block() as block:
                @block.sync
                def _(sp):
                    stream(sp, 1 if ahead else 0)

                @block.scalar
                def _(act):
                    for t in range(nt):
                        act.activation(xs[:, t, :], src[:, t, :], ACT.Square, accum_out=ss[:, t:t + 1])\
                           .then_inc(squared, 1)
                    if ahead:
                        cut_high(act, START[ahead], START[ahead])
                    for k in range(KD):
                        act.wait_ge(turned, k + 1)
                        act.activation(h_hi[:, k, 0:n_tok], ps[:, k, 0:n_tok], ACT.Copy, scale=col(gain, k))\
                           .then_inc(out_hi, 1)

                @block.vector
                def _(dve):
                    for t in range(nt):
                        dve.wait_ge(squared, t + 1)
                        dve.tensor_scalar(ms[:, t:t + 1], ss[:, t:t + 1], 1.0 / D, eps, ALU.mult, ALU.add)\
                           .then_inc(mean, 1)
                    for t in range(nt):
                        dve.wait_ge(rooted, t + 1)
                        dve.tensor_scalar(xs[:, t, :], src[:, t, :], rs[:, t:t + 1], None, ALU.mult)\
                           .then_inc(scaled, 1)
                    for k in range(KD):
                        dve.wait_ge(out_hi, k + 1)
                        dve.scalar_tensor_tensor(h_lo[:, k, 0:n_tok], ps[:, k, 0:n_tok], col(gain, k),
                                                 h_hi[:, k, 0:n_tok].bitcast(F32), ALU.mult, ALU.subtract)\
                           .then_inc(out_lo, 1)

                @block.gpsimd
                def _(pool):
                    for t in range(nt):
                        pool.wait_ge(mean, t + 1)
                        pool.tensor_tensor(rs[:, t:t + 1], ms[:, t:t + 1], neg_half[:, 0:1], ALU.pow)\
                            .then_inc(rooted, 1)
                    if ahead:
                        cut_low(pool, START[ahead])

                @block.tensor
                def _(pe):
                    for t in range(nt):
                        pe.wait_ge(scaled, t + 1)
                        for k in range(KD):
                            last = pe.transpose(ps[:, k, t * P:(t + 1) * P], xs[:, t, k * P:(k + 1) * P], ident)
                            if t == nt - 1:
                                last.then_inc(turned, 1)
            if ahead:
                cut_before[0] = START[ahead] + 1

        class Projection:

            def __init__(self, tag, stage, jobs, outs, nt=NT, banks=(0, 1, 2, 3, 4, 5, 6, 7)):
                self.done, self.out_act, self.out_dve = sem(tag + "_done"), sem(tag + "_out_act"), sem(tag + "_out_dve")
                self.u0, self.jobs, self.outs, self.nt, self.banks = START[stage], jobs, outs, nt, banks
                self.n = dict(STAGES)[stage]
                self.widths, self.last_unit = [], []
                u = 0
                for job in jobs:
                    u += 1 if job[0] == "F" else KD // job[2]
                    for _ in range(1 if job[0] == "F" else nt):
                        self.widths.append(nt * P if job[0] == "F" else job[1])
                        self.last_unit.append(u - 1)
                assert u == self.n and len(self.widths) == len(outs), (tag, u, self.n)

            def bank(self, i, n):
                return ps[:, self.banks[i % len(self.banks)], 0:n]

            def emptied(self, pe, i):
                j = i - len(self.banks)
                if j >= 0:
                    who = self.outs[j][0]
                    n = sum(o[0] == who for o in self.outs[:j + 1])
                    pe.wait_ge(self.out_act if who == "act" else self.out_dve, n)

            def pe(self, pe):
                u, i, n_tok = self.u0, 0, self.nt * P
                for job in self.jobs:
                    if job[0] == "F":
                        self.emptied(pe, i)
                        w = unit(pe, u)
                        for k in range(KD):
                            a, z = product(pe, self.bank(i, n_tok), [v[:, k * P:(k + 1) * P] for v in w],
                                           (h_hi[:, k, 0:n_tok], h_lo[:, k, 0:n_tok]), k == 0, k == KD - 1)
                            if k == 0 and u:
                                a.then_inc(weights_used, 1)
                        z.then_inc(self.done, 1)
                        u += 1
                        i += 1
                        yield
                        continue
                    n, bk = job[1:]
                    for t in range(self.nt):
                        self.emptied(pe, i + t)
                    for k in range(KD):
                        if k % bk == 0:
                            w = unit(pe, u)
                        for t in range(self.nt):
                            a, z = product(pe, self.bank(i + t, n),
                                           (h_hi[:, k, t * P:(t + 1) * P], h_lo[:, k, t * P:(t + 1) * P]),
                                           [v[:, (k % bk) * n:(k % bk + 1) * n] for v in w], k == 0, k == KD - 1)
                            if k % bk == 0 and t == 0 and u:
                                a.then_inc(weights_used, 1)
                            if k == KD - 1:
                                z.then_inc(self.done, 1)
                        if k % bk == bk - 1:
                            u += 1
                            yield
                    i += self.nt

            def act(self, act):
                for f in range(self.n + 1):
                    if f < self.n:
                        cut_high(act, self.u0 + f + 1, self.u0)
                    for i, (who, what, dst, arg) in enumerate(self.outs):
                        if who != "act" or self.last_unit[i] != f - 1:
                            continue
                        act.wait_ge(self.done, i + 1)
                        bank = self.bank(i, self.widths[i])
                        if what == "copy":
                            act.activation(dst, bank, ACT.Copy, scale=arg).then_inc(self.out_act, 1)
                        elif what == "silu":
                            act.activation(dst, bank, ACT.Silu).then_inc(self.out_act, 1)
                    yield

            def dve(self, dve, low=True):
                for f in range(self.n + 1):
                    if low and f < self.n:
                        cut_low(dve, self.u0 + f + 1)
                    for i, (who, what, dst, arg) in enumerate(self.outs):
                        if who != "dve" or self.last_unit[i] != f - 1:
                            continue
                        dve.wait_ge(self.done, i + 1)
                        bank = self.bank(i, self.widths[i])
                        if what == "copy":
                            dve.tensor_scalar(dst, bank, arg, None, ALU.mult).then_inc(self.out_dve, 1)
                        elif what == "bias":
                            dve.tensor_scalar(dst, bank, arg[0], arg[1], ALU.add, ALU.mult)\
                               .then_inc(self.out_dve, 1)
                        elif what == "conv":
                            w_col, b_col, chain = arg
                            last = dve.tensor_scalar(dst, bank, col("conv_w", w_col + 3), col("conv_b", b_col),
                                                     ALU.mult, ALU.add)
                            for tap in (1, 2, 3):
                                last.then_inc(chain, 1)
                                dve.wait_ge(chain, 3 * b_col + tap)
                                last = dve.scalar_tensor_tensor(dst[:, tap:S], bank[:, 0:S - tap],
                                                                col("conv_w", w_col + 3 - tap), dst[:, tap:S],
                                                                ALU.mult, ALU.add)
                            last.then_inc(self.out_dve, 1)
                        elif what == "add_row":
                            dve.tensor_tensor(dst, bank, arg, ALU.add).then_inc(self.out_dve, 1)
                    yield

            def pool(self, pool):
                for f in range(1, self.n + 1):
                    cut_low(pool, self.u0 + f)

        def project(*args, **more):
            work = Projection(*args, **more)
            with nc.Block() as block:
                @block.sync
                def _(sp):
                    stream(sp, work.n)

                @block.tensor
                def _(pe):
                    for _ in work.pe(pe):
                        pass

                @block.scalar
                def _(act):
                    for _ in work.act(act):
                        pass

                @block.vector
                def _(dve):
                    for _ in work.dve(dve):
                        pass
            cut_before[0] = work.u0 + work.n + 1

        def combine(tag, stage, y, nk):
            done, out_dve = sem(tag + "_done"), sem(tag + "_out_dve")
            u0 = START[stage]
            with nc.Block() as block:
                @block.sync
                def _(sp):
                    stream(sp, nk)

                @block.scalar
                def _(act):
                    for k in range(1, nk + 1):
                        if u0 + k < N_UNITS:
                            cut_high(act, u0 + k, u0)

                @block.tensor
                def _(pe):
                    for k in range(nk):
                        w = unit(pe, u0 + k)
                        for b in range(8):
                            t, half = b // 2, b % 2
                            a, z = product(pe, ps[:, b, :], [v[:, t * P:(t + 1) * P] for v in y(k)],
                                           [v[:, half * 512:(half + 1) * 512] for v in w], k == 0, k == nk - 1)
                            if b == 0:
                                a.then_inc(weights_used, 1)
                            if k == nk - 1:
                                z.then_inc(done, 1)

                @block.vector
                def _(dve):
                    for k in range(1, nk + 1):
                        if u0 + k < N_UNITS:
                            cut_low(dve, u0 + k)
                    for b in range(8):
                        t, half = b // 2, b % 2
                        xv = x[:, t, half * 512:(half + 1) * 512]
                        dve.wait_ge(done, b + 1)
                        dve.tensor_tensor(xv, ps[:, b, :], xv, ALU.add).then_inc(out_dve, 1)
            cut_before[0] = u0 + nk + 1

        def turn(tag, src, dst, nk, gain=None, gate=None):
            turned, silued, gated, out_hi, out_lo = (
                sem(tag + n) for n in ("_turned", "_silued", "_gated", "_out_hi", "_out_lo"))
            with nc.Block() as block:
                @block.tensor
                def _(pe):
                    for k in range(nk):
                        for t in range(NT):
                            last = pe.transpose(ps[:, k, t * P:(t + 1) * P], src(t, k), ident)
                        last.then_inc(turned, 1)

                @block.scalar
                def _(act):
                    if gate:
                        for k in range(nk):
                            act.activation(gate(k), gate(k), ACT.Silu).then_inc(silued, 1)
                    for k in range(nk):
                        if gate:
                            act.wait_ge(gated, k + 1)
                            act.activation(dst(k)[0], scr[:, k * S:(k + 1) * S], ACT.Copy).then_inc(out_hi, 1)
                        else:
                            act.wait_ge(turned, k + 1)
                            act.activation(dst(k)[0], ps[:, k, :], ACT.Copy, scale=gain(k) if gain else 1.0)\
                               .then_inc(out_hi, 1)

                def low(dve, k):
                    dve.wait_ge(out_hi, k + 1)
                    high = dst(k)[0].bitcast(F32)
                    if gate:
                        dve.tensor_tensor(dst(k)[1], scr[:, k * S:(k + 1) * S], high, ALU.subtract)\
                           .then_inc(out_lo, 1)
                    else:
                        dve.scalar_tensor_tensor(dst(k)[1], ps[:, k, :], gain(k) if gain else 1.0, high,
                                                 ALU.mult, ALU.subtract).then_inc(out_lo, 1)

                @block.vector
                def _(dve):
                    for k in range(nk):
                        dve.wait_ge(turned, k + 1)
                        if gate:
                            dve.wait_ge(silued, k + 1)
                            dve.scalar_tensor_tensor(scr[:, k * S:(k + 1) * S], ps[:, k, :], gain(k) if gain else 1.0,
                                                     gate(k), ALU.mult, ALU.mult).then_inc(gated, 1)
                            if k:
                                low(dve, k - 1)
                        else:
                            low(dve, k)
                    if gate:
                        low(dve, nk - 1)

        def attend(tag, units, maps=1, fill=None):
            n = len(units)
            t_bank, nb_t, o_bank, nb_o = (2, 2, 4, 2) if maps == 1 else (4, 1, 5, 1)
            NS = 2
            NP = 4
            fills = fill.n if fill else 0

            def turns(step):
                return (step + 1) * fills // n - step * fills // n if step < n else 0

            def out_bank(i):
                return ps[:, o_bank + i % nb_o, 0:units[i]["dv"]]

            def turn_bank(i):
                return t_bank + i % nb_t

            names = ["scored", "lifted", "maxed", "expd", "mixed", "turned", "pT_out", "valued", "out", "chain", "esink"]
            scored, lifted, maxed, expd, mixed, turned, pT_out, valued, out_done, dve_chain, esunk = (
                sem(tag + "_" + m) for m in names)

            def score(i, m):
                return ps[:, (i % NS) * maps + m, 0:units[i]["w"]]

            def prob(i, m):
                a = ((i % NP) * maps + m) * 512
                return scr[:, a:a + units[i]["w"]]

            def pT(i):
                a = (i % 2) * 512
                return big_row[:, a:a + 512] if maps == 2 else scr[:, 2048 + a:2560 + a]

            def stat(first, i, m=None):
                a = first + 2 * (i % 4)
                return small[:, a:a + maps] if m is None else small[:, a + m:a + m + 1]

            NMAX, DEN, RDEN, ESINK, RATIO = 300, 308, 316, 324, 354

            with nc.Block() as block:
                @block.sync
                def _(sp):
                    stream(sp, fills)

                @block.gpsimd
                def _(pool):
                    if fill:
                        fill.pool(pool)

                @block.tensor
                def _(pe):
                    filler = fill.pe(pe) if fill else None
                    for step in range(n + 3):
                        if step < n:
                            i, u = step, units[step]
                            if i >= NS:
                                pe.wait_ge(lifted, i - NS + 1)
                            for m in range(maps):
                                last = pe.matmul(score(i, m), u["q"][m], u["k"][m], start=True, stop=True)
                            last.then_inc(scored, 1)
                        for _ in range(turns(step)):
                            next(filler)
                        if 2 <= step < n + 2:
                            i, u = step - 2, units[step - 2]
                            pe.wait_ge(mixed if maps == 2 else expd, i + 1)
                            if i >= nb_t:
                                pe.wait_ge(pT_out, i - nb_t + 1)
                            for b in range(len(u["v"])):
                                last = pe.transpose(ps[:, turn_bank(i), b * P:(b + 1) * P],
                                                    prob(i, 0)[:, b * P:(b + 1) * P], ident)
                            last.then_inc(turned, 1)
                        if step >= 3:
                            i, u = step - 3, units[step - 3]
                            nb = len(u["v"])
                            pe.wait_ge(pT_out, i + 1)
                            if i >= nb_o:
                                pe.wait_ge(out_done, i - nb_o + 1)
                            for b in range(nb):
                                last = pe.matmul(out_bank(i), pT(i)[:, b * P:(b + 1) * P],
                                                 u["v"][b], start=b == 0, stop=b == nb - 1)
                            last.then_inc(valued, 1)
                    for _ in filler or ():
                        pass

                @block.scalar
                def _(act):
                    filler = fill.act(act) if fill else None
                    for step in range(n + 2):
                        for _ in range(turns(step)):
                            next(filler)
                        if step < n:
                            i, u = step, units[step]
                            act.wait_ge(maxed, i + 1)
                            if "sink" in u:
                                act.activation(stat(ESINK, i), u["sink"], ACT.Exp, bias=stat(NMAX, i))\
                                   .then_inc(esunk, 1)
                            for m in range(maps):
                                last = act.activation(prob(i, m), prob(i, m), ACT.Exp, bias=stat(NMAX, i, m),
                                                      accum_out=stat(DEN, i, m))
                            last.then_inc(expd, 1)
                        if step >= 2:
                            i, u = step - 2, units[step - 2]
                            nb = len(u["v"])
                            act.wait_ge(turned, i + 1)
                            if i >= 2:
                                act.wait_ge(valued, i - 1)
                            act.activation(pT(i)[:, 0:nb * P], ps[:, turn_bank(i), 0:nb * P], ACT.Copy)\
                               .then_inc(pT_out, 1)
                    for _ in filler or ():
                        pass

                @block.vector
                def _(dve):
                    links = [0]
                    filler = fill.dve(dve, low=False) if fill else None

                    def link(ins):
                        links[0] += 1
                        ins.then_inc(dve_chain, 1)
                        dve.wait_ge(dve_chain, links[0])

                    for step in range(n + 4):
                        if step >= 4:
                            i, u = step - 4, units[step - 4]
                            if maps == 1:
                                dve.wait_ge(expd, i + 1)
                                if "sink" in u:
                                    dve.wait_ge(esunk, i + 1)
                                    link(dve.tensor_tensor(stat(DEN, i), stat(DEN, i), stat(ESINK, i), ALU.add))
                                link(dve.reciprocal(stat(RDEN, i), stat(DEN, i)))
                                if "gate" in u:
                                    link(dve.tensor_tensor(stat(RDEN, i), stat(RDEN, i), u["gate"], ALU.mult))
                            dve.wait_ge(valued, i + 1)
                            if u.get("add"):
                                last = dve.scalar_tensor_tensor(u["out"], out_bank(i), stat(RDEN, i), u["out"],
                                                                ALU.mult, ALU.add)
                            else:
                                last = dve.tensor_scalar(u["out"], out_bank(i), stat(RDEN, i, 0), None, ALU.mult)
                            last.then_inc(out_done, 1)
                        if step < n:
                            i, u = step, units[step]
                            dve.wait_ge(scored, i + 1)
                            if i >= NP:
                                dve.wait_ge(turned, i - NP + 1)
                            for m in range(maps):
                                if u["mask"] is None:
                                    last = dve.tensor_copy(prob(i, m), score(i, m))
                                else:
                                    last = dve.scalar_tensor_tensor(prob(i, m), u["mask"], u["slope"], score(i, m),
                                                                    ALU.mult, ALU.add)
                            last.then_inc(lifted, 1)
                            dve.wait_ge(lifted, i + 1)
                            for m in range(maps):
                                last = dve.tensor_reduce(stat(NMAX, i, m), prob(i, m), AXX, ALU.max, negate=True)
                            if "sink" in u:
                                link(last)
                                last = dve.tensor_tensor(stat(NMAX, i), stat(NMAX, i), u["neg_sink"], ALU.min)
                            last.then_inc(maxed, 1)
                        for _ in range(turns(step)):
                            next(filler)
                        if maps == 2 and 1 <= step <= n:
                            i, u = step - 1, units[step - 1]
                            dve.wait_ge(expd, i + 1)
                            link(dve.reciprocal(stat(RDEN, i), stat(DEN, i)))
                            link(dve.scalar_tensor_tensor(stat(RATIO, i, 0), stat(DEN, i, 0), neg_lam,
                                                          stat(RDEN, i, 1), ALU.mult, ALU.mult))
                            dve.scalar_tensor_tensor(prob(i, 0), prob(i, 1), stat(RATIO, i, 0), prob(i, 0),
                                                     ALU.mult, ALU.add).then_inc(mixed, 1)
                    for _ in filler or ():
                        pass
            if fill:
                cut_before[0] = fill.u0 + fills + 1

        def token(ap, t):
            return ap[:, t * P:(t + 1) * P]

        Q, K, V, G, Z, XBC, DT = 0, 4096, 8192, 12288, 16384, 20480, 26624
        norm("norm_a", x, NT, EPS_A, "norm_a", part(0, [NT, D]), "in_a")
        qT, kT, gT = part(Q, [8, S]), part(K, [8, S]), part(G, [8, S])
        v_tok, z_tok = part(V, [NT, D]), part(Z, [NT, D])
        xbc = part(XBC, [12, S])
        dt = part(DT, [NT, 16])
        jobs = [("F",)] * 16 + [("T", 512, 2)] * 4 + [("T", 16, 8)]
        outs = [("act" if j % 2 == 0 else "dve", "copy", qT[:, j, :], 0.125) for j in range(8)]
        outs += [("act" if j % 2 == 0 else "dve", "copy", kT[:, j, :], 1.0) for j in range(8)]
        for tok, what in ((v_tok, "copy"), (z_tok, "silu")):
            for c in range(2):
                for t in range(NT):
                    who = "act" if what == "silu" or t % 2 == 0 else "dve"
                    outs.append((who, what, tok[:, t, c * 512:(c + 1) * 512], 1.0))
        outs += [("dve", "copy", dt[:, t, :], 1.0) for t in range(NT)]
        project("in_a", "in_a", jobs, outs)

        y_a = x
        conv_chain = sem("conv_chain")
        outs = [("dve", "conv", xbc[:, j, :], (4 * j, j, conv_chain)) for j in range(12)]
        outs += [("act", "copy", gT[:, j, :], 1.0) for j in range(8)]
        fill_a = Projection("in_a2", "in_a2", [("F",)] * 20, outs, banks=(6, 7))
        units = []
        for h in range(DA_H):
            for t in range(NT):
                w = (t + 1) * P
                units.append(dict(q=[token(qT[m * 64:m * 64 + 64, h, :], t) for m in range(2)],
                                  k=[kT[m * 64:m * 64 + 64, h, 0:w] for m in range(2)], w=w,
                                  mask=const("alibi")[:, S - w:S], slope=2.0 ** -(h + 1),
                                  v=[v_tok[:, b, h * P:(h + 1) * P] for b in range(t + 1)], dv=P,
                                  out=y_a[:, t, h * P:(h + 1) * P]))
        attend("da", units, maps=2, fill=fill_a)

        def group_norm(tag, y, width, eps):
            ng = NT * D // width
            squared, mean, rooted, scaled = (sem(tag + m) for m in ("_squared", "_mean", "_rooted", "_scaled"))
            flat = y[:, :, :].rearrange("p t (g w) -> p (t g) w", w=width)
            with nc.Block() as block:
                @block.scalar
                def _(act):
                    for g in range(ng):
                        act.activation(scr[:, g * width:(g + 1) * width], flat[:, g, :], ACT.Square, accum_out=ss[:, g:g + 1])\
                           .then_inc(squared, 1)

                @block.gpsimd
                def _(pool):
                    pool.wait_ge(mean, 1)
                    pool.tensor_tensor(rs[:, 0:ng], ms[:, 0:ng], neg_half[:, 0:ng], ALU.pow).then_inc(rooted, 1)

                @block.vector
                def _(dve):
                    dve.wait_ge(squared, ng)
                    dve.tensor_scalar(ms[:, 0:ng], ss[:, 0:ng], 1.0 / width, eps, ALU.mult, ALU.add).then_inc(mean, 1)
                    dve.wait_ge(rooted, 1)
                    for g in range(ng):
                        dve.tensor_scalar(flat[:, g, :], flat[:, g, :], rs[:, g:g + 1], None, ALU.mult)\
                           .then_inc(scaled, 1)

        dta = small[:, 400:464]
        dtv = small[:, 464:528]
        decays = small[:, 528:720]
        dt_all = dt.rearrange("p t h -> p (t h)")
        sl_squared, sl_mean, sl_rooted, sl_scaled, silu_done = (
            sem(m) for m in ("sl_squared", "sl_mean", "sl_rooted", "sl_scaled", "silu_done"))
        dt_chain, dt_biased, dt_exp, dt_ln, dta_ready = (
            sem(m) for m in ("dt_chain", "dt_biased", "dt_exp", "dt_ln", "dta_ready"))
        heads_a = y_a[:, :, :].rearrange("p t (g w) -> p (t g) w", w=P)
        with nc.Block() as block:
            @block.scalar
            def _(act):
                nabs = small[:, 784:848]
                act.wait_ge(dt_biased, 1)
                act.activation(nabs, nabs, ACT.Exp).then_inc(dt_exp, 1)
                act.wait_ge(dt_exp, 1)
                act.activation(nabs, nabs, ACT.Ln, bias=1.0).then_inc(dt_ln, 1)
                for j in range(12):
                    act.activation(xbc[:, j, :], xbc[:, j, :], ACT.Silu).then_inc(silu_done, 1)

            @block.gpsimd
            def _(pool):
                for t in range(NT):
                    pool.wait_ge(sl_mean, t + 1)
                    pool.tensor_tensor(rs[:, t * 8:t * 8 + 8], ms[:, t * 8:t * 8 + 8], neg_half[:, 0:8], ALU.pow)\
                        .then_inc(sl_rooted, 1)

            @block.vector
            def _(dve):
                v, nabs, relu = small[:, 720:784], small[:, 784:848], small[:, 848:912]
                dve.tensor_tensor(v.rearrange("p (t h) -> p t h", t=NT), dt,
                                  row("dt_bias").unsqueeze(1).broadcast_to([P, NT, 16]), ALU.add).then_inc(dt_chain, 1)
                dve.wait_ge(dt_chain, 1)
                dve.scalar_tensor_tensor(nabs, v, -1.0, v, ALU.mult, ALU.min).then_inc(dt_biased, 1)
                dve.tensor_scalar(relu, v, 0.0, None, ALU.max).then_inc(dt_chain, 1)
                for t in range(NT):
                    dve.tensor_tensor(scr[:, t * D:(t + 1) * D], y_a[:, t, :], y_a[:, t, :], ALU.mult)\
                       .then_inc(sl_squared, 1)
                for t in range(NT):
                    dve.wait_ge(sl_squared, NT + t)
                    dve.tensor_reduce(ss[:, t * 8:t * 8 + 8],
                                      scr[:, t * D:(t + 1) * D].rearrange("p (g w) -> p g w", w=P), AXX, ALU.add)\
                       .then_inc(sl_squared, 1)
                    dve.wait_ge(sl_squared, NT + t + 1)
                    dve.tensor_scalar(ms[:, t * 8:t * 8 + 8], ss[:, t * 8:t * 8 + 8], 1.0 / P, EPS_A,
                                      ALU.mult, ALU.add).then_inc(sl_mean, 1)
                dve.wait_ge(dt_ln, 1)
                dve.wait_ge(dt_chain, 2)
                dve.tensor_tensor(dtv, relu, nabs, ALU.add).then_inc(dt_chain, 1)
                dve.wait_ge(dt_chain, 3)
                dve.tensor_tensor(dta.rearrange("p (t h) -> p t h", t=NT), dtv.rearrange("p (t h) -> p t h", t=NT),
                                  neg_a.unsqueeze(1).broadcast_to([P, NT, 16]), ALU.mult).then_inc(dta_ready, 1)
                for t in range(NT):
                    dve.wait_ge(sl_rooted, t + 1)
                    ya_t = heads_a[:, t * 8:t * 8 + 8, :]
                    dve.tensor_tensor(ya_t, ya_t, rs[:, t * 8:t * 8 + 8].unsqueeze(2).broadcast_to([P, 8, P]),
                                      ALU.mult).then_inc(sl_scaled, 1)

        turn("ya", lambda t, k: y_a[:, t, k * P:(k + 1) * P], lambda k: (h_hi[:, k, :], h_lo[:, k, :]), 8,
             lambda k: subln8, lambda k: gT[:, k, :])

        xs_tok, xdt = part(0, [NT, D]), part(4096, [NT, D])
        TMP = 8192
        x_place = x[:, :, :].rearrange("p t d -> p (t d)")

        def two(v, n):
            return [v[:, 0:n], v[:, n:2 * n]]

        xdd = two(arena[:, 8704:9728], 512)
        dstr = [v.rearrange("p (h l) -> p h l", h=8) for v in two(x_place[:, 0:2048], 1024)]
        exps = [v.rearrange("p (h l) -> p h l", h=8) for v in two(x_place[:, 2048:4096], 1024)]
        b_tok = scr[:, 0:1024].rearrange("p (c n) -> p c n", c=NT)
        cbm = scr[:, 1024:2048].rearrange("p (i l) -> p i l", i=8)
        state = scr[:, 2048:3072].rearrange("p (g d) -> p g d", g=2)
        y_b = part(G, [NT, D])
        turned_x, xs_out_act, xs_out_dve, decay_sums, decays_ready, cb_done, cb_masked, xdt_ready = (
            sem(m) for m in ("turned_x", "xs_out_act", "xs_out_dve", "decay_sums", "decays_ready", "cb_done",
                             "cb_masked", "xdt_ready"))
        with nc.Block() as block:
            @block.tensor
            def _(pe):
                for i in range(10):
                    t, half = (i // 2, i % 2) if i < 8 else (2 * (i - 8), 2)
                    b = i % 5
                    if i >= 5:
                        pe.wait_ge(xs_out_act if (i - 5) % 2 == 0 else xs_out_dve, (i - 5) // 2 + 1)
                    for j in range(4):
                        if half < 2:
                            src = xbc[:, half * 4 + j, t * P:(t + 1) * P]
                        else:
                            src = xbc[:, 8 + j % 2, (t + j // 2) * P:(t + j // 2 + 1) * P]
                        last = pe.transpose(ps[:, b, j * P:(j + 1) * P], src, ident)
                    last.then_inc(turned_x, 1)
                for j, name in enumerate(("tri_le", "tri_gt", "ones")):
                    last = pe.matmul(ps[:, 5, j * 64:(j + 1) * 64], const(name), dta, start=True, stop=True)
                last.then_inc(decay_sums, 1)
                for i in range(8):
                    c, g = i // 2, i % 2
                    last = pe.matmul(ps[:, 6 + i // 4, (i % 4) * P:(i % 4 + 1) * P], xbc[:, 8 + g, c * P:(c + 1) * P],
                                     xbc[:, 10 + g, c * P:(c + 1) * P], start=True, stop=True)
                last.then_inc(cb_done, 1)

            def xs_dst(i):
                if i < 8:
                    return xs_tok[:, i // 2, (i % 2) * 512:(i % 2 + 1) * 512]
                return scr[:, (i - 8) * 512:(i - 7) * 512]

            @block.scalar
            def _(act):
                for i in range(0, 10, 2):
                    act.wait_ge(turned_x, i + 1)
                    act.activation(xs_dst(i), ps[:, i % 5, :], ACT.Copy).then_inc(xs_out_act, 1)
                act.wait_ge(decay_sums, 1)
                act.activation(decays, ps[:, 5, 0:192], ACT.Exp).then_inc(decays_ready, 1)

            @block.vector
            def _(dve):
                for i in range(1, 10, 2):
                    dve.wait_ge(turned_x, i + 1)
                    dve.tensor_copy(xs_dst(i), ps[:, i % 5, :]).then_inc(xs_out_dve, 1)
                dve.wait_ge(cb_done, 1)
                for i in range(2):
                    dve.tensor_tensor(cbm[:, 4 * i:4 * i + 4, :],
                                      ps[:, 6 + i, :].rearrange("p (i l) -> p i l", i=4),
                                      const("tri_le").unsqueeze(1).broadcast_to([P, 4, P]), ALU.mult)\
                       .then_inc(cb_masked, 1)
                dve.wait_ge(xs_out_act, 4)
                dve.wait_ge(xs_out_dve, 4)
                for t in range(NT):
                    dve.tensor_tensor(xdt[:, t, :].rearrange("p (h d) -> p h d", h=SSD_H),
                                      xs_tok[:, t, :].rearrange("p (h d) -> p h d", h=SSD_H),
                                      dtv[:, t * 16:(t + 1) * 16].unsqueeze(2).broadcast_to([P, SSD_H, SSD_P]),
                                      ALU.mult).then_inc(xdt_ready, 1)

        dstr_ready, xdd_ready, skip_ready, segs_done, segs_exp, mixed_s, y_done, st_done, st_out, y_out, ssd_chain = (
            sem(m) for m in ("dstr_ready", "xdd_ready", "skip_ready", "segs_done", "segs_exp", "mixed_s", "y_done",
                             "st_done", "st_out", "y_out", "ssd_chain"))

        def per_head(a):
            return a.unsqueeze(2).broadcast_to([P, 8, SSD_P])

        def heads(a):
            return a.rearrange("p (h d) -> p h d", h=8)

        with nc.Block() as block:
            @block.tensor
            def _(pe):
                def segs(i):
                    pe.wait_ge(dstr_ready, i + 1)
                    if i >= 2:
                        pe.wait_ge(segs_exp, 2 * i - 2)
                    for j in range(8):
                        last = pe.matmul(ps[:, 2 * (i % 2) + j // 4, (j % 4) * P:(j % 4 + 1) * P],
                                         dstr[i % 2][:, j, :], const("tri_le"), start=True, stop=True)
                        if j % 4 == 3:
                            last.then_inc(segs_done, 1)

                segs(0)
                for i in range(8):
                    c, g = i // 2, i % 2
                    if i < 7:
                        segs(i + 1)
                    if i:
                        pe.wait_ge(y_out, i)
                    if c > 0:
                        pe.wait_ge(st_out, i - 1)
                        pe.matmul(ps[:, 5, :], xbc[:, 10 + g, c * P:(c + 1) * P], state[:, g, :],
                                  start=True, stop=True)
                    pe.wait_ge(mixed_s, i + 1)
                    for j in range(8):
                        h = g * 8 + j
                        last = pe.matmul(ps[:, 4, j * 64:(j + 1) * 64], exps[i % 2][:, j, :],
                                         xdt[:, c, h * 64:(h + 1) * 64], start=True, stop=True)
                    last.then_inc(y_done, 1)
                    pe.wait_ge(xdd_ready, i + 1)
                    if i:
                        pe.wait_ge(st_out, i)
                    pe.matmul(ps[:, 6, :], b_tok[:, c, g * P:(g + 1) * P], xdd[i % 2], start=True, stop=True)\
                      .then_inc(st_done, 1)

            @block.scalar
            def _(act):
                for i in range(8):
                    for half in range(2):
                        act.wait_ge(segs_done, 2 * i + half + 1)
                        if i >= 2 and half == 0:
                            act.wait_ge(y_done, i - 1)
                        act.activation(exps[i % 2][:, 4 * half:4 * half + 4, :],
                                       ps[:, 2 * (i % 2) + half, :].rearrange("p (i l) -> p i l", i=4), ACT.Exp)\
                           .then_inc(segs_exp, 1)

            @block.gpsimd
            def _(pool):
                for i in range(8):
                    c, g = i // 2, i % 2
                    hs = slice(c * 16 + g * 8, c * 16 + g * 8 + 8)
                    if i >= 2:
                        pool.wait_ge(segs_done, 2 * i - 2)
                    pool.tensor_tensor(dstr[i % 2], const("tri_gt").unsqueeze(1).broadcast_to([P, 8, P]),
                                       dta[:, hs].unsqueeze(2).broadcast_to([P, 8, P]), ALU.mult)\
                        .then_inc(dstr_ready, 1)
                    if i >= 2:
                        pool.wait_ge(st_done, i - 1)
                    pool.tensor_tensor(heads(xdd[i % 2]), heads(xdt[:, c, g * 512:(g + 1) * 512]),
                                       per_head(decays[:, 64 + hs.start:64 + hs.stop]), ALU.mult)\
                        .then_inc(xdd_ready, 1)
                    pool.tensor_tensor(heads(y_b[:, c, g * 512:(g + 1) * 512]),
                                       heads(xs_tok[:, c, g * 512:(g + 1) * 512]),
                                       per_head(row("d_skip")[:, g * 8:(g + 1) * 8]), ALU.mult)\
                        .then_inc(skip_ready, 1)

            @block.vector
            def _(dve):
                links = [0]

                def link(ins):
                    links[0] += 1
                    ins.then_inc(ssd_chain, 1)
                    dve.wait_ge(ssd_chain, links[0])

                def mix(i):
                    dve.wait_ge(segs_exp, 2 * i + 2)
                    dve.tensor_tensor(exps[i % 2], exps[i % 2], cbm[:, i:i + 1, :].broadcast_to([P, 8, P]), ALU.mult)\
                       .then_inc(mixed_s, 1)

                mix(0)
                for i in range(8):
                    c, g = i // 2, i % 2
                    hs = slice(c * 16 + g * 8, c * 16 + g * 8 + 8)
                    if i < 7:
                        mix(i + 1)
                    y = y_b[:, c, g * 512:(g + 1) * 512]
                    tmp = arena[:, TMP:TMP + 512]
                    if c > 0:
                        dve.wait_ge(y_done, i + 1)
                        link(dve.tensor_tensor(heads(tmp), heads(ps[:, 5, :]), per_head(decays[:, hs]), ALU.mult))
                        dve.wait_ge(skip_ready, i + 1)
                        link(dve.tensor_tensor(y, y, tmp, ALU.add))
                    dve.wait_ge(skip_ready, i + 1)
                    dve.wait_ge(y_done, i + 1)
                    dve.tensor_tensor(y, ps[:, 4, :], y, ALU.add).then_inc(y_out, 1)
                    if c > 0:
                        link(dve.tensor_tensor(heads(state[:, g, :]), heads(state[:, g, :]),
                                               per_head(decays[:, 128 + hs.start:128 + hs.stop]), ALU.mult))
                        dve.wait_ge(st_done, i + 1)
                        dve.tensor_tensor(state[:, g, :], ps[:, 6, :], state[:, g, :], ALU.add).then_inc(st_out, 1)
                    else:
                        dve.wait_ge(st_done, i + 1)
                        dve.tensor_copy(state[:, g, :], ps[:, 6, :]).then_inc(st_out, 1)
                    dve.wait_ge(y_out, i + 1)
                    link(dve.tensor_tensor(y, y, z_tok[:, c, g * 512:(g + 1) * 512], ALU.mult))

        group_norm("ssdn", y_b, 512, EPS_A)
        yb = halves("yb", ARENA, ARENA + 4096, 8)
        with nc.Block() as block:
            @block.sync
            def _(sp):
                sp.dma_start(x[:, :, :], x_dram.rearrange("(t p) d -> p t d", p=P)).then_inc(x_loaded, 16)
                sp.dma_start(big_row[:, :], big_dram[0, :].partition_broadcast(P)).then_inc(big_loaded, 16)
        turn("yb", lambda t, k: y_b[:, t, k * P:(k + 1) * P], lambda k: (yb[0][:, k, :], yb[1][:, k, :]), 8,
             lambda k: col("ssd_norm", k))
        with nc.Block() as block:
            @block.vector
            def _(dve):
                dve.wait_ge(x_loaded, 32)
        combine("out_a", "out_a", lambda k: (h_hi[:, k, :], h_lo[:, k, :]) if k < 8
                else (yb[0][:, k - 8, :], yb[1][:, k - 8, :]), 16)

        recycle()
        norm("norm_c", x, NT, EPS_A, "norm_c", part(0, [NT, D]))
        qT, kT, v_tok = part(0, [8, S]), part(4096, [2, S]), part(5120, [NT, P])
        gT, o_tok = part(5632, [8, S]), part(9728, [NT, D])
        jobs = [("F",)] * 10 + [("T", 128, 8)]
        outs = [("dve", "bias", qT[:, j, :], (col("bq", j), 0.125)) for j in range(8)]
        outs += [("dve", "bias", kT[:, j, :], (col("bk", j), 1.0)) for j in range(2)]
        outs += [("dve", "add_row", v_tok[:, t, :], row("bv")) for t in range(NT)]
        project("in_c", "in_c", jobs, outs)
        fill_c = Projection("in_c2", "in_c2", [("F",)] * 8,
                            [("dve", "bias", gT[:, j, :], (col("bg", j), 1.0)) for j in range(8)], banks=(6, 7))
        units = []
        for h in range(SW_H):
            kv, hp = h // 8, (h % 2) * 64
            for t in range(NT):
                lo = max(t - 1, 0) * P
                w = (t + 1) * P - lo
                units.append(dict(q=[token(qT[hp:hp + 64, h // 2, :], t)], k=[kT[hp:hp + 64, kv, lo:lo + w]], w=w,
                                  mask=const("sw")[:, 2 * P - w:], slope=2.0 ** (-8.0 * (h + 1) / SW_H),
                                  v=[v_tok[:, lo // P + b, kv * 64:kv * 64 + 64] for b in range(w // P)], dv=64,
                                  out=o_tok[:, t, h * 64:(h + 1) * 64], sink=row("sinks")[:, h:h + 1],
                                  neg_sink=neg_sink[:, h:h + 1]))
        attend("sw", units, fill=fill_c)
        turn("oc", lambda t, k: o_tok[:, t, k * P:(k + 1) * P], lambda k: (h_hi[:, k, :], h_lo[:, k, :]), 8,
             gate=lambda k: gT[:, k, :])
        combine("out_c", "out_c", lambda k: (h_hi[:, k, :], h_lo[:, k, :]), 8)

        def row_norm(tag, eps, store):
            squared, mean, rooted, scaled = (sem(tag + m) for m in ("_squared", "_mean", "_rooted", "_scaled"))
            with nc.Block() as block:
                @block.scalar
                def _(act):
                    for t in range(NT):
                        act.activation(scr[:, t * D:(t + 1) * D], x[:, t, :], ACT.Square, accum_out=ss[:, t:t + 1])\
                           .then_inc(squared, 1)

                @block.gpsimd
                def _(pool):
                    for t in range(NT):
                        pool.wait_ge(mean, t + 1)
                        pool.tensor_tensor(rs[:, t:t + 1], ms[:, t:t + 1], neg_half[:, 0:1], ALU.pow)\
                            .then_inc(rooted, 1)

                @block.vector
                def _(dve):
                    for t in range(NT):
                        dve.wait_ge(squared, t + 1)
                        dve.tensor_scalar(ms[:, t:t + 1], ss[:, t:t + 1], 1.0 / D, eps, ALU.mult, ALU.add)\
                           .then_inc(mean, 1)
                    dve.wait_ge(big_loaded, 32 if store else 16)
                    for t in range(NT):
                        dve.wait_ge(rooted, t + 1)
                        dve.scalar_tensor_tensor(x[:, t, :], x[:, t, :], rs[:, t:t + 1], big_row[:, :],
                                                 ALU.mult, ALU.mult).then_inc(scaled, 1)

                @block.sync
                def _(sp):
                    if store:
                        for t in range(NT):
                            sp.wait_ge(scaled, t + 1)
                            sp.dma_start(out_dram[t * P:(t + 1) * P, :], x[:, t, :]).then_inc(stored, 16)
                        sp.wait_ge(stored, 16 * NT)

        row_norm("final_a", EPS_A, False)

        recycle()
        norm("norm_m", x, NT, EPS_B, "norm_mix", part(0, [NT, D]))
        ft = part(0, [15, S])
        tv = part(7680, [NT, 512])
        gm = part(9728, [24, S])
        o_abc = part(22016, [NT, 768])
        jobs = [("F",)] * 15 + [("T", 512, 2)]
        outs = []
        for j in range(15):
            scale = 0.125 if j in (0, 1, 4, 5, 11, 12) else 1.0
            outs.append(("act" if j % 2 == 0 else "dve", "copy", ft[:, j, :], scale))
        outs += [("dve", "copy", tv[:, t, :], 1.0) for t in range(NT)]
        project("in_m", "in_m", jobs, outs)

        swapped, sin_done, cos_done, rope_done, gates_done, widx_done = (
            sem(m) for m in ("swapped", "sin_done", "cos_done", "rope_done", "gates_done", "widx_done"))
        with nc.Block() as block:
            @block.tensor
            def _(pe):
                for j in range(11):
                    if j >= 8:
                        pe.wait_ge(sin_done, j - 7)
                    pe.matmul(ps[:, j % 8, :], const("perm"), ft[:, j, :], start=True, stop=True).then_inc(swapped, 1)

            @block.vector
            def _(dve):
                for j in range(11):
                    hp = P if j < 10 else 64
                    tmp = scr[0:hp, (j % 4) * 512:(j % 4 + 1) * 512]
                    dve.wait_ge(swapped, j + 1)
                    dve.tensor_tensor(tmp, ps[0:hp, j % 8, :], const("sin")[0:hp, :], ALU.mult).then_inc(sin_done, 1)
                    dve.tensor_tensor(ft[0:hp, j, :], ft[0:hp, j, :], const("cos")[0:hp, :], ALU.mult)\
                       .then_inc(cos_done, 1)
                    dve.wait_ge(sin_done, j + 1)
                    dve.wait_ge(cos_done, j + 1)
                    dve.tensor_tensor(ft[0:hp, j, :], ft[0:hp, j, :], tmp, ALU.add).then_inc(rope_done, 1)
                for t in range(NT):
                    dve.tensor_scalar(tv[:, t, 448:452], tv[:, t, 448:452], 1.0 / 16, None, ALU.mult)\
                       .then_inc(widx_done, 1)

            @block.scalar
            def _(act):
                for t in range(NT):
                    act.activation(tv[:, t, 452:464], tv[:, t, 452:464], ACT.Sigmoid).then_inc(gates_done, 1)

        sa_names = ["sb_z", "sb_nabs", "sb_exp", "sb_ln", "sb_sp", "sb_mask", "sb_sum", "sb_w", "sb_o", "sb_out"]
        sb_z, sb_nabs, sb_exp, sb_ln, sb_sp, sb_mask, sb_sum, sb_w, sb_o, sb_out = (sem(m) for m in sa_names)
        def z_bank(first, b):
            if b == 3:
                return ps[:, first + 1, 384:512]
            return ps[:, first + b, 0:S - b * P]

        def sb_out_bank(t):
            return ps[:, 5, 256 + t * 64:256 + (t + 1) * 64]

        fill_m2 = Projection("in_m2", "in_m2", [("F",)] * 10,
                             [("dve", "copy", gm[:, j, :], 1.0) for j in range(10)], banks=(6, 7))
        nab = scr[:, 0:2048].rearrange("p (b q) -> p b q", b=NT)
        spl = scr[:, 2048:4096].rearrange("p (b q) -> p b q", b=NT)
        with nc.Block() as block:
            @block.sync
            def _(sp):
                stream(sp, fill_m2.n)

            @block.gpsimd
            def _(pool):
                fill_m2.pool(pool)

            @block.tensor
            def _(pe):
                filler = fill_m2.pe(pe)
                for h in range(4):
                    hp = (h % 2) * 64
                    qh, kh = ft[hp:hp + 64, 11 + h // 2, :], ft[hp:hp + 64, 13 + h // 2, :]
                    if h:
                        pe.wait_ge(sb_sp, 4 * h)
                    for b in range(NT):
                        pe.matmul(z_bank(0, b), kh[:, b * P:(b + 1) * P], qh[:, b * P:S], start=True, stop=True)\
                          .then_inc(sb_z, 1)
                    next(filler)
                    pe.wait_ge(sb_mask, 4 * (h + 1))
                    if h:
                        pe.wait_ge(sb_out, 4 * h)
                    for b in range(NT):
                        bank = z_bank(3, b)
                        pe.matmul(bank, kh[:, b * P:(b + 1) * P], qh[:, b * P:S], start=True, stop=False)
                        pe.matmul(bank, const("neg_ge"), spl[:, b, b * P:S], start=False, stop=False)
                        for later in range(b + 1, NT):
                            pe.matmul(bank[:, (later - b) * P:], const("neg_ones"), spl[:, later, later * P:S],
                                      start=False, stop=False)
                        pe.matmul(bank[:, 0:P], ident, const("strict_neg"), start=False, stop=True)\
                          .then_inc(sb_sum, 1)
                    next(filler)
                    pe.wait_ge(sb_w, 4 * (h + 1))
                    for t in range(NT):
                        for b in range(t + 1):
                            last = pe.matmul(sb_out_bank(t), nab[:, b, t * P:(t + 1) * P],
                                             tv[:, b, h * 64:(h + 1) * 64], start=b == 0, stop=b == t)
                        last.then_inc(sb_o, 1)
                    if h < 2:
                        next(filler)

            @block.scalar
            def _(act):
                filler = fill_m2.act(act)
                for h in range(4):
                    for b in range(NT):
                        act.wait_ge(sb_z, 4 * h + 4)
                        if h and b == 0:
                            act.wait_ge(sb_o, 4 * h)
                        act.activation(nab[:, b, b * P:S], z_bank(0, b), ACT.Abs).then_inc(sb_nabs, 1)
                    for b in range(NT):
                        act.wait_ge(sb_nabs, 4 * h + b + 1)
                        act.activation(nab[:, b, b * P:S], nab[:, b, b * P:S], ACT.Exp, scale=-1.0).then_inc(sb_exp, 1)
                    for b in range(NT):
                        act.wait_ge(sb_exp, 4 * h + b + 1)
                        act.activation(nab[:, b, b * P:S], nab[:, b, b * P:S], ACT.Ln, bias=1.0).then_inc(sb_ln, 1)
                    next(filler)
                    for b in range(NT):
                        act.wait_ge(sb_sum, 4 * h + 4)
                        act.activation(nab[:, b, b * P:S], z_bank(3, b), ACT.Exp).then_inc(sb_w, 1)
                    for _ in range(2 if h < 2 else 1):
                        next(filler)
                next(filler)

            @block.vector
            def _(dve):
                filler = fill_m2.dve(dve, low=False)
                for h in range(4):
                    for b in range(NT):
                        dve.wait_ge(sb_ln, 4 * h + b + 1)
                        if h and b == 0:
                            dve.wait_ge(sb_sum, 4 * h)
                        dve.scalar_tensor_tensor(spl[:, b, b * P:S], z_bank(0, b), 0.0, nab[:, b, b * P:S],
                                                 ALU.max, ALU.add).then_inc(sb_sp, 1)
                        dve.wait_ge(sb_sp, 4 * h + b + 1)
                        dve.tensor_tensor(spl[:, b, b * P:(b + 1) * P], spl[:, b, b * P:(b + 1) * P],
                                          const("strict01"), ALU.mult).then_inc(sb_mask, 1)
                    next(filler)
                    next(filler)
                    for t in range(NT):
                        dve.wait_ge(sb_o, 4 * h + 4)
                        dve.tensor_copy(o_abc[:, t, h * 64:(h + 1) * 64], sb_out_bank(t)).then_inc(sb_out, 1)
                    if h < 2:
                        next(filler)
                next(filler)
        cut_before[0] = fill_m2.u0 + fill_m2.n + 1

        sel = arena[:, 25088:26624]
        sel_at = (None, 0, 256, 640)
        relu_at = ((), (0, 256, 512, 768), (1024, 1408, 1792, 2176), (2560, 3072, 3584, 0))
        ix_scored, ix_relu, ix_sum, ix_top, ix_sel, gate_m2 = (
            sem(m) for m in ("ix_scored", "ix_relu", "ix_sum", "ix_top", "ix_sel", "gate_m2"))
        fill_m3 = Projection("in_m3", "in_m3", [("F",)] * 14,
                             [("act", "copy", gm[:, 10 + j, :], 1.0) for j in range(14)], banks=(6, 7))

        def selected(t):
            return sel[:, sel_at[t]:sel_at[t] + (t + 1) * P]

        def relu_of(t, h):
            return scr[:, relu_at[t][h]:relu_at[t][h] + (t + 1) * P]

        with nc.Block() as block:
            @block.sync
            def _(sp):
                stream(sp, fill_m3.n)

            @block.gpsimd
            def _(pool):
                fill_m3.pool(pool)

            @block.tensor
            def _(pe):
                for t in range(1, NT):
                    w = (t + 1) * P
                    for h in range(4):
                        i = 4 * (t - 1) + h
                        hp = (h % 2) * 64
                        if i >= 6:
                            pe.wait_ge(ix_relu, i - 5)
                        pe.matmul(ps[:, i % 6, 0:w], ft[hp:hp + 64, 2 + h // 2, t * P:(t + 1) * P],
                                  ft[hp:hp + 64, 7, 0:w], start=True, stop=True).then_inc(ix_scored, 1)
                for _ in fill_m3.pe(pe):
                    pass

            @block.scalar
            def _(act):
                for i in range(12):
                    t, h = 1 + i // 4, i % 4
                    act.wait_ge(ix_scored, i + 1)
                    if i == 11:
                        act.wait_ge(ix_sum, 4)
                    act.activation(relu_of(t, h), ps[:, i % 6, 0:(t + 1) * P], ACT.Relu).then_inc(ix_relu, 1)
                for j in range(10):
                    act.activation(gm[:, j, :], gm[:, j, :], ACT.Sigmoid).then_inc(gate_m2, 1)
                for _ in fill_m3.act(act):
                    pass

            @block.vector
            def _(dve):
                sums = tops = 0
                for t in range(1, NT):
                    w = (t + 1) * P
                    score = selected(t)
                    acc = const("causal")[:, S - w:S]
                    for h in range(4):
                        dve.wait_ge(ix_relu, 4 * (t - 1) + h + 1)
                        if sums % 4:
                            dve.wait_ge(ix_sum, sums)
                        dve.scalar_tensor_tensor(score, relu_of(t, h), tv[:, t, 448 + h:449 + h], acc,
                                                 ALU.mult, ALU.add).then_inc(ix_sum, 1)
                        sums += 1
                        acc = score
                    dve.wait_ge(ix_sum, sums)
                    for r in range(P // 8):
                        top = small[:, 912 + 8 * (r % 2):920 + 8 * (r % 2)]
                        dve.max(top, score).then_inc(ix_top, 1)
                        dve.wait_ge(ix_top, tops + 1)
                        dve.match_replace(score, top, score, -3.0e38).then_inc(ix_top, 1)
                        dve.wait_ge(ix_top, tops + 2)
                        tops += 2
                    dve.tensor_scalar(score, score, -2.0e38, NEG, ALU.is_gt, ALU.mult).then_inc(ix_sel, 1)

        cut_before[0] = fill_m3.u0 + fill_m3.n + 1

        blocks = at("blocks", [P, 32, 32], F32, H_PLACE + 1024)[:, :, :]
        block_hi = at("block_hi", [P, 32, 32], F32R, H_PLACE)
        block_lo = at("block_lo", [P, 32, 32], F32R, HL_PLACE)
        hid_k = small[:, 0:32]
        hid_v4 = small[:, 400:528]
        kc_T = small[:, 528:560]
        vc_diag = small[:, 560:816]
        cm_zero, cm_blocks, cm_hi, cm_lo, cm_hid, cm_gelu, cm_two, cm_out, gate_m3 = (
            sem(m) for m in ("cm_zero", "cm_blocks", "cm_hi", "cm_lo", "cm_hid", "cm_gelu", "cm_two", "cm_out",
                             "gate_m3"))

        class Compression:
            n = 4
            u0 = START["cmp"]

            def pe(self, pe):
                pe.wait_ge(cm_lo, 1)
                for q in range(4):
                    w = unit(pe, self.u0 + q)
                    for l in range(8):
                        for j in range(2):
                            rows_j = slice(j * 64, j * 64 + 64)
                            a, z = product(pe, ps[:, 6 + j, 0:32], [v[rows_j, l * P:(l + 1) * P] for v in w],
                                           (block_hi[rows_j, q * 8 + l, :], block_lo[rows_j, q * 8 + l, :]),
                                           q + l == 0, q * 8 + l == 31)
                            if l + j == 0:
                                a.then_inc(weights_used, 1)
                    if q == 3:
                        z.then_inc(cm_hid, 1)
                    yield
                pe.wait_ge(cm_gelu, 2)
                pe.matmul(ps[:, 6, 0:32], col("w2", 0, P), hid_k, start=True, stop=True)
                pe.matmul(ps[:, 7, 0:64], hid_v4, col("w2", P, 64), start=True, stop=True).then_inc(cm_two, 1)

            def act(self, act):
                act.wait_ge(cm_blocks, 2)
                act.activation(block_hi[:, :, :], blocks, ACT.Copy).then_inc(cm_hi, 1)
                for q in range(1, 5):
                    cut_high(act, self.u0 + q, self.u0)
                    for j in range(3 * q - 3, 3 * q):
                        act.activation(gm[:, 10 + j, :], gm[:, 10 + j, :], ACT.Sigmoid).then_inc(gate_m3, 1)
                    yield
                act.wait_ge(cm_zero, 4)
                act.wait_ge(cm_hid, 1)
                act.activation(hid_k[:, 0:N_CMP], ps[:, 6, 0:N_CMP], ACT.Gelu_apprx_tanh).then_inc(cm_gelu, 1)
                act.activation(hid_v4.rearrange("p (h n) -> p h n", h=4)[:, :, 0:N_CMP],
                               ps[:, 7, 0:N_CMP].unsqueeze(1).broadcast_to([P, 4, N_CMP]), ACT.Gelu_apprx_tanh)\
                   .then_inc(cm_gelu, 1)
                for j in (12, 13):
                    act.activation(gm[:, 10 + j, :], gm[:, 10 + j, :], ACT.Sigmoid).then_inc(gate_m3, 1)

            def dve(self, dve, low):
                for place in (hid_k, hid_v4, vc_diag, blocks):
                    dve.memset(place, 0.0).then_inc(cm_zero, 1)
                dve.wait_ge(cm_zero, 4)
                src = ft[:, 10, :].rearrange("p (n j) -> p j n", j=16)
                for half in range(2):
                    dve.tensor_tensor(blocks[:, half * 16:half * 16 + 16, 0:N_CMP], src[:, :, half:half + N_CMP],
                                      col("pos", half * 16, 16).unsqueeze(2).broadcast_to([P, 16, N_CMP]),
                                      ALU.add).then_inc(cm_blocks, 1)
                dve.wait_ge(cm_hi, 1)
                dve.tensor_tensor(block_lo[:, :, :], blocks, block_hi[:, :, :].bitcast(F32), ALU.subtract)\
                   .then_inc(cm_lo, 1)
                for _ in range(4):
                    yield
                dve.wait_ge(cm_two, 1)
                dve.tensor_copy(kc_T, ps[:, 6, 0:32]).then_inc(cm_out, 1)
                for h in range(4):
                    rows_h = slice(32 * h, 32 * h + 32)
                    dve.tensor_copy(vc_diag[rows_h, h * 64:(h + 1) * 64], ps[rows_h, 7, 0:64]).then_inc(cm_out, 1)

            def pool(self, pool):
                for q in range(1, 5):
                    cut_low(pool, self.u0 + q)

        units = []
        for t in range(NT):
            w = (t + 1) * P
            for h in range(4):
                hp = (h % 2) * 64
                units.append(dict(q=[ft[hp:hp + 64, h // 2, t * P:(t + 1) * P]], k=[ft[hp:hp + 64, 6, 0:w]], w=w,
                                  mask=selected(t) if t else const("causal")[:, S - w:S], slope=1.0,
                                  v=[tv[:, b, 256:320] for b in range(t + 1)], dv=64,
                                  out=o_abc[:, t, 256 + h * 64:256 + (h + 1) * 64]))
        attend("dsa", units, fill=Compression())

        cs_names = ["cs_scored", "cs_chain", "cs_shifted", "cs_exp", "cs_prob", "cs_turned", "cs_pT", "cs_valued",
                    "cs_out"]
        cs_scored, cs_chain, cs_shifted, cs_exp, cs_prob, cs_turned, cs_pT, cs_valued, cs_out = (
            sem(m) for m in cs_names)
        cs_flat, cs_turned_p = scr[:, 0:512], scr[:, 512:1024]
        cs_p = cs_flat.rearrange("p (i n) -> p i n", n=32)
        cs_p4 = cs_flat.rearrange("p (t h n) -> p t h n", t=NT, h=4)
        cs_max, cs_den = small[:, 64:80], small[:, 80:96]

        def per_row(a):
            return a.unsqueeze(2).broadcast_to([P, 16, 32])

        def per_tile(name):
            return const(name).rearrange("p (t n) -> p t n", t=NT).unsqueeze(2).broadcast_to([P, NT, 4, 32])

        with nc.Block() as block:
            @block.tensor
            def _(pe):
                for i in range(16):
                    t, h = i // 4, i % 4
                    hp = (h % 2) * 64
                    at_s = (2 * t + h // 2) * 32
                    last = pe.matmul(ps[:, h % 2, at_s:at_s + 32], ft[hp:hp + 64, 4 + h // 2, t * P:(t + 1) * P],
                                     kc_T[hp:hp + 64, :], start=True, stop=True)
                last.then_inc(cs_scored, 1)
                pe.wait_ge(cs_prob, 1)
                for t in range(NT):
                    last = pe.transpose(ps[:, 4, t * P:(t + 1) * P], cs_flat[:, t * P:(t + 1) * P], ident)
                last.then_inc(cs_turned, 1)
                pe.wait_ge(cs_pT, 1)
                for t in range(NT):
                    last = pe.matmul(ps[:, 2 + t // 2, t % 2 * 256:(t % 2 + 1) * 256],
                                     cs_turned_p[:, t * P:(t + 1) * P], vc_diag, start=True, stop=True)
                    if t % 2:
                        last.then_inc(cs_valued, 1)

            @block.scalar
            def _(act):
                act.wait_ge(cs_shifted, 1)
                act.activation(cs_flat, cs_flat, ACT.Exp).then_inc(cs_exp, 1)
                act.wait_ge(cs_turned, 1)
                act.activation(cs_turned_p, ps[:, 4, :], ACT.Copy).then_inc(cs_pT, 1)

            @block.vector
            def _(dve):
                links = [0]

                def link(ins):
                    links[0] += 1
                    ins.then_inc(cs_chain, 1)
                    dve.wait_ge(cs_chain, links[0])

                dve.wait_ge(cs_scored, 1)
                for odd in range(2):
                    link(dve.tensor_tensor(cs_p4[:, :, odd::2, :],
                                           ps[:, odd, 0:256].rearrange("p (t h n) -> p t h n", t=NT, h=2),
                                           per_tile("cmp_neg")[:, :, 0:2, :], ALU.add))
                link(dve.tensor_reduce(cs_max, cs_p, AXX, ALU.max))
                dve.tensor_tensor(cs_p, cs_p, per_row(cs_max), ALU.subtract).then_inc(cs_shifted, 1)
                dve.wait_ge(cs_exp, 1)
                link(dve.tensor_tensor(cs_p4, cs_p4, per_tile("cmp01"), ALU.mult))
                link(dve.tensor_reduce(cs_den, cs_p, AXX, ALU.add))
                link(dve.tensor_scalar(cs_den, cs_den, 1e-30, None, ALU.max))
                link(dve.reciprocal(cs_den, cs_den))
                gate = tv[:, :, 452:464].rearrange("p t (h g) -> p t h g", g=3)[:, :, :, 0]
                den4 = cs_den.rearrange("p (t h) -> p t h", t=NT)
                link(dve.tensor_tensor(den4, den4, gate, ALU.mult))
                dve.tensor_tensor(cs_p, cs_p, per_row(cs_den), ALU.mult).then_inc(cs_prob, 1)
                for i in range(2):
                    dve.wait_ge(cs_valued, i + 1)
                    dve.tensor_copy(o_abc[:, 2 * i:2 * i + 2, 512:768],
                                    ps[:, 2 + i, :].rearrange("p (t d) -> p t d", t=2)).then_inc(cs_out, 1)

        units = []
        for j, (kt, vo) in enumerate(((8, 320), (9, 384))):
            for t in range(NT):
                w = (t + 1) * P
                for h in range(4):
                    hp = (h % 2) * 64
                    units.append(dict(q=[ft[hp:hp + 64, 4 + h // 2, t * P:(t + 1) * P]], k=[ft[hp:hp + 64, kt, 0:w]],
                                      w=w, mask=const("causal")[:, S - w:S], slope=1.0,
                                      v=[tv[:, b, vo:vo + 64] for b in range(t + 1)], dv=64,
                                      out=o_abc[:, t, 512 + h * 64:512 + (h + 1) * 64],
                                      gate=tv[:, t, 453 + j + 3 * h:454 + j + 3 * h], add=True))
        attend("swa", units)

        o_parts = halves("o_abc", ARENA, ARENA + 3072, 6)
        turn("om", lambda t, k: o_abc[:, t, k * P:(k + 1) * P], lambda k: (o_parts[0][:, k, :], o_parts[1][:, k, :]),
             6)
        up_done, up_gated, up_added, merged_hi, merged_lo = (
            sem(m) for m in ("up_done", "up_gated", "up_added", "merged_hi", "merged_lo"))
        m_sum = scr[:, 0:4096].rearrange("p (j s) -> p j s", j=8)
        m_new = part(6144, [4, S])
        u0 = START["up"]
        with nc.Block() as block:
            @block.sync
            def _(sp):
                stream(sp, 6)

            @block.tensor
            def _(pe):
                for i in range(24):
                    half, br, j = i // 12, i // 4 % 3, i % 4
                    if j == 0:
                        w = unit(pe, u0 + i // 4)
                    if i >= 8:
                        pe.wait_ge(up_gated, i - 7)
                    for k in range(2):
                        at_w = (2 * j + k) * P
                        a, z = product(pe, ps[:, i % 8, :], [v[:, at_w:at_w + P] for v in w],
                                       [v[:, 2 * br + k, :] for v in o_parts], k == 0, k == 1)
                        if j + k == 0:
                            a.then_inc(weights_used, 1)
                    z.then_inc(up_done, 1)

            @block.scalar
            def _(act):
                for f in range(1, 6):
                    cut_high(act, u0 + f, u0)
                    if f == 4:
                        for j in range(4):
                            act.wait_ge(up_added, 5 + j)
                            act.activation(h_hi[:, j, :], m_sum[:, j, :], ACT.Copy).then_inc(merged_hi, 1)
                cut_high(act, u0 + 6, u0)
                for j in range(4, 8):
                    act.wait_ge(up_added, 9 + j)
                    act.activation(h_hi[:, j, :], m_sum[:, j, :], ACT.Copy).then_inc(merged_hi, 1)

            @block.vector
            def _(dve):
                for i in range(24):
                    half, br, j = i // 12, i // 4 % 3, i % 4
                    tile = 4 * half + j
                    if j == 0 and i < 20:
                        cut_low(dve, u0 + i // 4 + 1)
                    dve.wait_ge(up_done, i + 1)
                    if i >= 8 and br:
                        dve.wait_ge(up_added, 8 * half + 4 * br - 8 + j + 1 if br == 2 else 8 * half - 4 + j + 1)
                    dve.tensor_tensor(m_new[:, j, :] if br else m_sum[:, tile, :], ps[:, i % 8, :],
                                      gm[:, 8 * br + tile, :], ALU.mult).then_inc(up_gated, 1)
                cut_low(dve, u0 + 6)
                for j in range(8):
                    dve.wait_ge(merged_hi, j + 1)
                    dve.tensor_tensor(h_lo[:, j, :], m_sum[:, j, :], h_hi[:, j, :].bitcast(F32), ALU.subtract)\
                       .then_inc(merged_lo, 1)

            @block.gpsimd
            def _(pool):
                added = 0
                for i in range(24):
                    half, br, j = i // 12, i // 4 % 3, i % 4
                    if br == 0:
                        continue
                    tile = 4 * half + j
                    pool.wait_ge(up_gated, i + 1)
                    if br == 2:
                        pool.wait_ge(up_added, added - 3)
                    pool.tensor_tensor(m_sum[:, tile, :], m_sum[:, tile, :], m_new[:, j, :], ALU.add)\
                        .then_inc(up_added, 1)
                    added += 1
        cut_before[0] = u0 + 7
        combine("out_m", "out_m", lambda k: (h_hi[:, k, :], h_lo[:, k, :]), 8)

        recycle()
        mem_loaded = sem("mem_loaded")
        mem_x, mem_kT, mem_v = part(8192, [2, D]), part(10240, [2, 256]), part(10752, [2, 256])
        mem_q, o_mem = part(11264, [2, S]), part(12288, [NT, 256])
        om_parts = halves("o_mem", ARENA + 13312, ARENA + 14336, 2)
        with nc.Block() as block:
            @block.sync
            def _(sp):
                sp.dma_start(mem_x, mem_dram.rearrange("(t p) d -> p t d", p=P)).then_inc(mem_loaded, 16)
                sp.dma_start(big_row[:, :], big_dram[1, :].partition_broadcast(P)).then_inc(big_loaded, 16)
                sp.wait_ge(mem_loaded, 16)
        norm("norm_kv", mem_x, 2, EPS_B, "norm_mem_kv", part(0, [NT, D]))
        project("mem_kv", "mem_kv", [("F",)] * 2 + [("T", 256, 4)],
                [("act", "copy", mem_kT[:, 0, :], 1.0), ("dve", "copy", mem_kT[:, 1, :], 1.0),
                 ("act", "copy", mem_v[:, 0, :], 1.0), ("dve", "copy", mem_v[:, 1, :], 1.0)], nt=2)
        norm("norm_q", x, NT, EPS_B, "norm_mem_q", part(0, [NT, D]))
        project("mem_q", "mem_q", [("F",)] * 2,
                [("act", "copy", mem_q[:, 0, :], 0.125), ("dve", "copy", mem_q[:, 1, :], 0.125)])
        units = []
        for h in range(4):
            hp = (h % 2) * 64
            for t in range(NT):
                units.append(dict(q=[mem_q[hp:hp + 64, h // 2, t * P:(t + 1) * P]], k=[mem_kT[hp:hp + 64, h // 2, :]],
                                  w=256, mask=None, slope=1.0, v=[mem_v[:, b, h * 64:(h + 1) * 64] for b in range(2)],
                                  dv=64, out=o_mem[:, t, h * 64:(h + 1) * 64]))
        attend("mem", units)
        turn("omem", lambda t, k: o_mem[:, t, k * P:(k + 1) * P], lambda k: (om_parts[0][:, k, :], om_parts[1][:, k, :]), 2)
        combine("mem_out", "mem_out", lambda k: (om_parts[0][:, k, :], om_parts[1][:, k, :]), 2)

        norm("norm_f", x, NT, EPS_B, "norm_ffn", part(0, [NT, D]))
        ff = halves("ff", ARENA, ARENA + NFF * S, NFF)
        ff_done, ff_silu, ff_prod, ff_hi, ff_lo = (
            sem(m) for m in ("ff_done", "ff_silu", "ff_prod", "ff_hi", "ff_lo"))
        silu_of = scr[:, 0:1536].rearrange("p (i s) -> p i s", i=3)
        prod_of = scr[:, 1536:3072].rearrange("p (i s) -> p i s", i=3)
        u0 = START["ffn_in"]
        with nc.Block() as block:
            @block.sync
            def _(sp):
                stream(sp, 2 * NFF)

            @block.tensor
            def _(pe):
                for i in range(2 * NFF):
                    if i >= 8:
                        pe.wait_ge(ff_silu if i % 2 == 0 else ff_prod, (i - 8) // 2 + 1)
                    w = unit(pe, u0 + i)
                    for k in range(KD):
                        a, z = product(pe, ps[:, i % 8, :], [v[:, k * P:(k + 1) * P] for v in w],
                                       (h_hi[:, k, :], h_lo[:, k, :]), k == 0, k == KD - 1)
                        if k == 0:
                            a.then_inc(weights_used, 1)
                    z.then_inc(ff_done, 1)

            @block.scalar
            def _(act):
                for j in range(NFF + 1):
                    if j < NFF:
                        cut_high(act, u0 + 2 * j + 1, u0)
                        act.wait_ge(ff_done, 2 * j + 1)
                        if j >= 3:
                            act.wait_ge(ff_prod, j - 2)
                        act.activation(silu_of[:, j % 3, :], ps[:, 2 * j % 8, :], ACT.Silu).then_inc(ff_silu, 1)
                        cut_high(act, u0 + 2 * j + 2, u0)
                    if j:
                        act.wait_ge(ff_prod, j)
                        act.activation(ff[0][:, j - 1, :], prod_of[:, (j - 1) % 3, :], ACT.Copy).then_inc(ff_hi, 1)

            @block.vector
            def _(dve):
                for j in range(NFF + 1):
                    if j < NFF:
                        cut_low(dve, u0 + 2 * j + 1)
                        cut_low(dve, u0 + 2 * j + 2)
                        dve.wait_ge(ff_done, 2 * j + 2)
                        dve.wait_ge(ff_silu, j + 1)
                        if j >= 3:
                            dve.wait_ge(ff_lo, j - 2)
                        dve.tensor_tensor(prod_of[:, j % 3, :], ps[:, (2 * j + 1) % 8, :], silu_of[:, j % 3, :],
                                          ALU.mult).then_inc(ff_prod, 1)
                    if j:
                        dve.wait_ge(ff_hi, j)
                        dve.tensor_tensor(ff[1][:, j - 1, :], prod_of[:, (j - 1) % 3, :],
                                          ff[0][:, j - 1, :].bitcast(F32), ALU.subtract).then_inc(ff_lo, 1)
        cut_before[0] = u0 + 2 * NFF + 1
        combine("ffn_out", "ffn_out", lambda k: (ff[0][:, k, :], ff[1][:, k, :]), NFF)
        row_norm("final_b", EPS_B, True)


def tables():
    c = np.zeros((P, N_CONST), np.float32)
    i, j = np.arange(P)[:, None], np.arange(P)[None, :]

    def put(name, value):
        a, w = CONSTS[name]
        c[:, a:a + w] = value

    put("ident", i == j)
    put("tri_le", i <= j)
    put("tri_gt", i > j)
    put("neg_ge", -1.0 * (i >= j))
    put("neg_ones", -1.0)
    put("ones", 1.0)
    put("strict_neg", np.where(i < j, 0.0, NEG))
    put("strict01", i < j)
    u = np.arange(S)[None, :] - (S - P)
    put("alibi", np.where(u <= i, u - i, NEG))
    put("causal", np.where(u <= i, 0.0, NEG))
    d = i + P - np.arange(2 * P)[None, :]
    put("sw", np.where((d >= 0) & (d < P), -d, NEG))
    inv = np.float32(10000.0) ** (-np.arange(0, 64, 2, dtype=np.float32) / np.float32(64))
    ang = np.arange(S, dtype=np.float32)[None, :] * inv.astype(np.float32)[:, None]
    put("cos", np.tile(np.cos(ang), (4, 1)))
    put("sin", np.concatenate([-np.sin(ang), np.sin(ang)] * 2, 0))
    put("perm", (i // 32 ^ 1) * 32 + i % 32 == j)
    n = np.arange(32)[None, :]
    for t in range(NT):
        ok = (n < N_CMP) & (n * 16 + 31 <= t * P + i)
        a = CONSTS["cmp_neg"][0] + t * 32
        c[:, a:a + 32] = np.where(ok, 0.0, NEG)
        a = CONSTS["cmp01"][0] + t * 32
        c[:, a:a + 32] = ok
    return c


def kernel(**inputs):
    import concourse.bacc as bacc
    from concourse.bass_utils import run_bass_kernel_spmd

    a = {k: np.asarray(v, np.float32) for k, v in inputs.items()}

    stream = []

    def feature(w):
        for j in range(w.shape[1] // P):
            stream.append(w[:, j * P:(j + 1) * P].reshape(KD, P, P).transpose(1, 0, 2).reshape(P, UNIT))

    def chunk(w, n, bk):
        for j in range(w.shape[1] // n):
            for b in range(KD // bk):
                v = w[b * bk * P:(b + 1) * bk * P, j * n:(j + 1) * n].reshape(bk, P, n).transpose(1, 0, 2)
                stream.append(padded(v.reshape(P, bk * n)))

    def rows_of(w):
        for k in range(w.shape[0] // P):
            stream.append(w[k * P:(k + 1) * P, :])

    def padded(v):
        return v if v.shape[1] == UNIT else np.concatenate([v, np.zeros((P, UNIT - v.shape[1]), np.float32)], 1)

    w = a["w_in_a"][0]
    feature(w[:, 0:2048])
    chunk(w[:, 2048:3072], 512, 2)
    chunk(w[:, 4096:5120], 512, 2)
    chunk(w[:, 6656:6672], 16, 8)
    feature(w[:, 5120:6656])
    feature(w[:, 3072:4096])
    rows_of(a["w_out_a"][0])
    w = a["w_in_c"][0]
    feature(w[:, 0:1024])
    feature(np.concatenate([w[:, 1024:1088]] * 2 + [w[:, 1088:1152]] * 2, 1))
    chunk(w[:, 1152:1280], 128, 8)
    feature(w[:, 1280:2304])
    rows_of(a["w_out_c"][0])
    w = a["w_in_2"][0]
    names = ["q_a", 256, "k_a", 256, "v_a", 256, "q_b", 256, "k_b", 64, "v_b", 64, "q_idx", 256, "k_idx", 64,
             "w_idx", 4, "q_c", 256, "k_cmp", 64, "v_cmp", 64, "k_sel", 64, "v_sel", 64, "k_win", 64, "v_win", 64,
             "g_c", 12, "g_merge", 3072]
    p, at = {}, 0
    for name, n in zip(names[::2], names[1::2]):
        p[name] = w[:, at:at + n]
        at += n
    feature(np.concatenate([p["q_b"], p["q_idx"], p["q_c"]] + [p[n] for n in ("k_b", "k_idx", "k_sel", "k_win")
                                                              for _ in range(2)]
                           + [p["k_cmp"], p["v_cmp"], p["q_a"], p["k_a"]], 1))
    chunk(np.concatenate([p["v_a"], p["v_b"], p["v_sel"], p["v_win"], p["w_idx"], p["g_c"],
                          np.zeros((D, 48), np.float32)], 1), 512, 2)
    feature(p["g_merge"])
    w1 = [a[n][0].reshape(4, 8, 64, P).transpose(0, 2, 1, 3).reshape(4, 64, UNIT) for n in ("cmp_w1_k_2", "cmp_w1_v_2")]
    for q in range(4):
        stream.append(np.concatenate([w1[0][q], w1[1][q]], 0))
    for half in range(2):
        for br in range(3):
            v = a["w_up_2"][0, br][:, half * 512:(half + 1) * 512].reshape(2, P, 4, P)
            stream.append(v.transpose(1, 2, 0, 3).reshape(P, UNIT))
    rows_of(a["w_out_2"][0])
    kv = a["w_mem_kv_2"][0]
    feature(kv[:, 0:256])
    chunk(kv[:, 256:512], 256, 4)
    feature(a["w_mem_q_2"][0])
    rows_of(a["w_mem_o_2"][0])
    w = a["w_ffn_in_2"][0]
    for j in range(NFF):
        feature(w[:, j * P:(j + 1) * P])
        feature(w[:, FF + j * P:FF + (j + 1) * P])
    rows_of(a["w_ffn_out_2"][0])
    assert len(stream) == N_UNITS
    weights = np.ascontiguousarray(np.stack(stream))

    def tiles(v):
        return v.reshape(-1, P).T

    pos = np.concatenate([a["cmp_pos_k_2"][0].T, a["cmp_pos_v_2"][0].T], 0)
    conv_w = a["conv_w_a"][0].reshape(4, 12, P).transpose(2, 1, 0).reshape(P, 48)
    bc = a["b_in_c"][0]
    cols = np.ascontiguousarray(np.concatenate(
        [tiles(a["norm_a"][0]), tiles(a["norm_c"][0]), tiles(a["norm_mix_2"][0]), tiles(a["norm_mem_q_2"][0]),
         tiles(a["norm_mem_kv_2"][0]), tiles(a["norm_ffn_2"][0]), tiles(a["ssd_norm_a"][0]), tiles(a["subln_a"][0]),
         conv_w, tiles(a["conv_b_a"][0]), tiles(bc[0:1024]),
         tiles(np.concatenate([bc[1024:1088]] * 2 + [bc[1088:1152]] * 2)), pos,
         tiles(bc[1280:2304]), a["cmp_w2_k_2"][0], a["cmp_w2_k_2"][0], a["cmp_w2_v_2"][0]], 1))
    rows = np.ascontiguousarray(np.concatenate(
        [a["dt_bias_a"][0], a["a_log_a"][0], a["d_skip_a"][0], a["sinks_c"][0], a["lambda_q1_a"][0],
         a["lambda_k1_a"][0], a["lambda_q2_a"][0], a["lambda_k2_a"][0], bc[1152:1280]]))
    big = np.ascontiguousarray(np.stack([a["final_norm"], a["norm_final_2"]]))

    nc = bacc.Bacc("TRN2", target_bir_lowering=False, num_devices=1,
                   dynamic_dma_scratch_size=1024)
    arrays = {"weights": weights, "x_in": np.ascontiguousarray(a["x"][0]),
              "mem_in": np.ascontiguousarray(a["mem_2"][0]), "tables": tables(), "cols_in": cols, "rows_in": rows,
              "big_in": big}
    args = [nc.dram_tensor(n, v.shape, F32, kind="ExternalInput").ap() for n, v in arrays.items()]
    out = nc.dram_tensor("out", (S, D), F32, kind="ExternalOutput").ap()
    build(nc, *args, out)
    got = run_bass_kernel_spmd(nc, [arrays], core_ids=[0])
    return got.results[0]["out"].reshape(1, S, D)
```

```python
import math
from contextlib import ExitStack

import concourse.bass as bass
import numpy as np
from concourse import mybir

F32 = mybir.dt.float32
F32R = mybir.dt.float32r
ALU = mybir.AluOpType
ACT = mybir.ActivationFunctionType
AXX = mybir.AxisListType.X

P = 128
D = 1024
S = 512
NT = S // P
KD = D // P
UNIT = 1024
NEG = -1.0e30
DA_H = 8
SSD_H = 16
SSD_P = 64
SW_H = 16
FF = 2816
NFF = FF // P
N_CMP = 31
EPS_A = 1e-5
EPS_B = 1e-6
LAMBDA_INIT = 0.8 - 0.6 * math.exp(-0.3 * 0)
RAW = 3
CUT = 2

CONSTS = {}
_at = 0
for _n, _w in [("ident", P), ("tri_le", P), ("tri_gt", P), ("neg_ge", P), ("neg_ones", P), ("strict_neg", P),
               ("strict01", P), ("ones", P), ("alibi", S), ("sw", 2 * P), ("causal", S), ("cos", S), ("sin", S),
               ("perm", P), ("cmp_neg", NT * 32), ("cmp01", NT * 32)]:
    CONSTS[_n] = (_at, _w)
    _at += _w
N_CONST = _at

COLS = {}
_at = 0
for _n, _w in [("norm_a", 8), ("norm_c", 8), ("norm_mix", 8), ("norm_mem_q", 8), ("norm_mem_kv", 8),
               ("norm_ffn", 8), ("ssd_norm", 8), ("subln", 1), ("conv_w", 48), ("conv_b", 12), ("bq", 8), ("bk", 2),
               ("pos", 32), ("bg", 8), ("w2", 192)]:
    COLS[_n] = (_at, _w)
    _at += _w
N_COLS = _at

ROWS = {}
_at = 0
for _n, _w in [("dt_bias", 16), ("a_log", 16), ("d_skip", 16), ("sinks", 16), ("lq1", 64), ("lk1", 64),
               ("lq2", 64), ("lk2", 64), ("bv", 128)]:
    ROWS[_n] = (_at, _w)
    _at += _w
N_ROWS = _at

STAGES = [("in_a", 33), ("in_a2", 20), ("out_a", 16), ("in_c", 11), ("in_c2", 8), ("out_c", 8), ("in_m", 19),
          ("in_m2", 10), ("in_m3", 14), ("cmp", 4), ("mem_kv", 4), ("up", 6),
          ("out_m", 8), ("mem_q", 2), ("mem_out", 2), ("ffn_in", 2 * NFF), ("ffn_out", NFF)]
START = {}
_at = 0
for _n, _c in STAGES:
    START[_n] = _at
    _at += _c
N_UNITS = _at


def build(nc, w_dram, x_dram, mem_dram, const_dram, cols_dram, rows_dram, big_dram, out_dram):
    ctx = ExitStack()
    with ctx:
        room = (nc.sbuf_bytes_remaining - 64) // 4
        fence = ctx.enter_context(nc.sbuf_tensor("fence", [P, room], F32))
        base = nc.sbuf_base - 4 * room
        top = [0]

        def at(name, shape, dtype, place):
            return nc.alloc_sbuf_tensor_at(name, shape, dtype, offset=base + 4 * place)

        def take(floats):
            place = top[0]
            top[0] += (floats + 7) // 8 * 8
            assert top[0] <= room, (top[0], room)
            return place

        def sb(name, shape):
            return at(name, shape, F32, take(math.prod(shape[1:])))

        raw = sb("raw", [P, RAW, UNIT])
        cut_hi = at("cut_hi", [P, CUT, UNIT], F32R, take(CUT * UNIT))
        cut_lo = at("cut_lo", [P, CUT, UNIT], F32R, take(CUT * UNIT))
        x = sb("x", [P, NT, D])
        H_PLACE, HL_PLACE = take(KD * S), take(KD * S)
        h_hi = at("h_hi", [P, KD, S], F32R, H_PLACE)
        h_lo = at("h_lo", [P, KD, S], F32R, HL_PLACE)
        consts = sb("consts", [P, N_CONST])
        cols = sb("cols", [P, N_COLS])
        rows = sb("rows", [P, N_ROWS])
        big_row = sb("big_row", [P, D])
        scr = sb("scr", [P, 4096])
        small = sb("small", [P, 936])
        junk = sb("junk", [P, P])
        ARENA = take(26784)
        arena = at("arena", [P, 26784], F32, ARENA)
        ps = ctx.enter_context(nc.psum_tensor("ps", [P, 8, 512], F32))

        def halves(name, place_hi, place_lo, n):
            return (at(name + "_hi", [P, n, S], F32R, place_hi), at(name + "_lo", [P, n, S], F32R, place_lo))

        stage_sems, old_sems = [], []

        def sem(name):
            stage_sems.append(nc.alloc_semaphore(name))
            return stage_sems[-1]

        def lasting_sem(name):
            return ctx.enter_context(nc.semaphore(name))

        def recycle():
            old_sems.extend(stage_sems)
            stage_sems.clear()

        def const(name):
            a, w = CONSTS[name]
            return consts[:, a:a + w]

        def col(name, i=0, n=1):
            a = COLS[name][0] + i
            return cols[:, a:a + n]

        def row(name):
            a, w = ROWS[name]
            return rows[:, a:a + w]

        def part(a, shape):
            n = 1
            for d in shape:
                n *= d
            v = arena[:, a:a + n]
            if len(shape) == 2:
                return v.rearrange("p (a b) -> p a b", a=shape[0])
            return v

        ident = const("ident")
        ss = small[:, 0:64]
        ms = small[:, 64:128]
        rs = small[:, 128:192]
        neg_half = small[:, 192:256]
        subln8 = small[:, 257:258]
        neg_lam = small[:, 290:291]
        neg_a = small[:, 258:274]
        neg_sink = small[:, 274:290]

        raw_loaded = [lasting_sem(f"raw_loaded{i}") for i in range(RAW)]
        hi_ready, lo_ready = lasting_sem("hi_ready"), lasting_sem("lo_ready")
        weights_used = lasting_sem("weights_used")
        stored = lasting_sem("stored")
        issued = [0]
        cut_before = [0]

        def stream(sp, n_cut):
            end = min(cut_before[0] + n_cut + RAW, N_UNITS)
            for u in range(issued[0], end):
                if u >= RAW:
                    sp.wait_ge(lo_ready, u - RAW + 1)
                sp.dma_start(raw[:, u % RAW, :], w_dram[u]).then_inc(raw_loaded[u % RAW], 16)
            issued[0] = max(issued[0], end)

        first_unit = [0]

        def cut_high(act, u):
            act.wait_ge(raw_loaded[u % RAW], 16 * (u // RAW + 1))
            if u - CUT >= first_unit[0]:
                act.wait_ge(weights_used, u - CUT + 1)
            act.activation(cut_hi[:, u % CUT, :], raw[:, u % RAW, :], ACT.Copy).then_inc(hi_ready, 1)

        def cut_low(eng, u):
            eng.wait_ge(hi_ready, u + 1)
            eng.tensor_tensor(cut_lo[:, u % CUT, :], raw[:, u % RAW, :], cut_hi[:, u % CUT, :].bitcast(F32),
                              ALU.subtract).then_inc(lo_ready, 1)

        def unit(pe, u):
            pe.wait_ge(lo_ready, u + 1)
            return cut_hi[:, u % CUT, :], cut_lo[:, u % CUT, :]


        def product(pe, out, left, right, start, stop):
            a = pe.matmul(out, left[0], right[0], start=start, stop=False)
            pe.matmul(out, left[0], right[1], start=False, stop=False)
            return a, pe.matmul(out, left[1], right[0], start=False, stop=stop)

        def run(*parts):
            n_cut = sum(p.cuts for p in parts)

            with nc.Block() as block:
                @block.sync
                def _(sp):
                    for s in old_sems:
                        sp.sem_clear(s)
                    for p in parts:
                        p.sync(sp)
                    stream(sp, n_cut)
                    for p in parts:
                        p.store(sp)

                @block.tensor
                def _(pe):
                    for p in parts:
                        for _ in p.pe(pe) or ():
                            pass

                @block.scalar
                def _(act):
                    for p in parts:
                        for _ in p.act(act) or ():
                            pass

                @block.vector
                def _(dve):
                    for p in parts:
                        for _ in p.dve(dve) or ():
                            pass

                @block.gpsimd
                def _(pool):
                    for p in parts:
                        p.pool(pool)
            end_stage(n_cut)

        def end_stage(n_cut):
            cut_before[0] += n_cut
            first_unit[0] = cut_before[0] - 1
            for s in old_sems:
                nc.release_semaphore(s)
            old_sems.clear()

        class Part:
            cuts = 0

            def sync(self, sp):
                pass

            def store(self, sp):
                pass

            def pe(self, pe):
                pass

            def act(self, act):
                pass

            def dve(self, dve):
                pass

            def pool(self, pool):
                pass

            def prepare(self, dve):
                pass

        const_loaded, x_loaded, small_loaded, big_loaded = (
            sem("const_loaded"), lasting_sem("x_loaded"), sem("small_loaded"), lasting_sem("big_loaded"))
        tables_loaded = sem("tables_loaded")
        x_tile = [sem(f"x_tile{t}") for t in range(NT)]
        setup_chain, lam_dots, lam_exps, sub_ready = (
            sem(m) for m in ("setup_chain", "lam_dots", "lam_exps", "sub_ready"))

        class Setup(Part):

            def sync(self, sp):
                for t in range(NT):
                    sp.dma_start(x[:, t, :], x_dram[t * P:(t + 1) * P, :]).then_inc(x_tile[t], 16)

            def act(self, act):
                act.dma_start(consts[:, 0:P], const_dram[:, 0:P]).then_inc(const_loaded, 16)
                act.dma_start(cols[:, :], cols_dram).then_inc(small_loaded, 16)
                act.dma_start(rows[:, :], rows_dram.partition_broadcast(P)).then_inc(small_loaded, 16)

            def pe(self, pe):
                pe.wait_ge(const_loaded, 16)

            def dve(self, dve):
                dve.memset(neg_half, -0.5).then_inc(setup_chain, 1)

            def pool(self, pool):
                pool.wait_ge(setup_chain, 1)

        class Lambda(Part):

            def act(self, act):
                act.wait_ge(lam_dots, 2)
                act.activation(small[:, 334:336], small[:, 332:334], ACT.Exp).then_inc(lam_exps, 1)
                act.activation(small[:, 336:352], row("a_log"), ACT.Exp).then_inc(lam_exps, 1)
                act.wait_ge(tables_loaded, 16)

            def dve(self, dve):
                dve.wait_ge(small_loaded, 32)
                dve.tensor_tensor(scr[:, 0:64], row("lq1"), row("lk1"), ALU.mult).then_inc(setup_chain, 1)
                dve.tensor_tensor(scr[:, 64:128], row("lq2"), row("lk2"), ALU.mult).then_inc(setup_chain, 1)
                dve.wait_ge(setup_chain, 3)
                dve.tensor_reduce(small[:, 332:333], scr[:, 0:64], AXX, ALU.add).then_inc(lam_dots, 1)
                dve.tensor_reduce(small[:, 333:334], scr[:, 64:128], AXX, ALU.add).then_inc(lam_dots, 1)
                dve.tensor_scalar(subln8, col("subln"), 1.0 - LAMBDA_INIT, None, ALU.mult).then_inc(sub_ready, 1)
                dve.tensor_scalar(neg_sink, row("sinks"), -1.0, None, ALU.mult).then_inc(sub_ready, 1)
                dve.wait_ge(lam_exps, 2)
                dve.tensor_scalar(neg_a, small[:, 336:352], -1.0, None, ALU.mult).then_inc(sub_ready, 1)
                dve.tensor_tensor(small[:, 352:353], small[:, 334:335], small[:, 335:336], ALU.subtract)\
                   .then_inc(setup_chain, 1)
                dve.wait_ge(setup_chain, 4)
                dve.tensor_scalar(neg_lam, small[:, 352:353], LAMBDA_INIT, -1.0, ALU.add, ALU.mult)\
                   .then_inc(sub_ready, 1)

        class Norm(Part):

            def __init__(self, tag, src, nt, eps, gain, xs, ready=None, ahead=False):
                (self.squared, self.mean, self.rooted, self.scaled, self.turned, self.out_hi, self.out_lo) = (
                    sem(tag + n) for n in ("_squared", "_mean", "_rooted", "_scaled", "_turned", "_out_hi", "_out_lo"))
                self.src, self.nt, self.eps, self.gain, self.xs, self.ready, self.ahead = (
                    src, nt, eps, gain, xs, ready, ahead)
                self.n_tok = nt * P
                self.cuts = 1 if ahead else 0

            def act(self, act):
                for t in range(self.nt):
                    if self.ready:
                        act.wait_ge(*self.ready(t))
                    act.activation(self.xs[:, t, :], self.src[:, t, :], ACT.Square, accum_out=ss[:, t:t + 1])\
                       .then_inc(self.squared, 1)
                yield
                if self.ahead:
                    act.dma_start(consts[:, P:], const_dram[:, P:]).then_inc(tables_loaded, 16)
                    act.wait_ge(small_loaded, 32)
                    cut_high(act, 0)
                for k in range(KD):
                    act.wait_ge(self.turned, k + 1)
                    act.activation(h_hi[:, k, 0:self.n_tok], ps[:, k, 0:self.n_tok], ACT.Copy,
                                   scale=col(self.gain, k)).then_inc(self.out_hi, 1)

            def dve(self, dve):
                for t in range(self.nt + 1):
                    if t < self.nt:
                        dve.wait_ge(self.squared, t + 1)
                        dve.tensor_scalar(ms[:, t:t + 1], ss[:, t:t + 1], 1.0 / D, self.eps, ALU.mult, ALU.add)\
                           .then_inc(self.mean, 1)
                    if t:
                        dve.wait_ge(self.rooted, t)
                        dve.tensor_scalar(self.xs[:, t - 1, :], self.src[:, t - 1, :], rs[:, t - 1:t], None, ALU.mult)\
                           .then_inc(self.scaled, 1)
                yield
                if self.ahead:
                    cut_low(dve, 0)
                for k in range(KD):
                    dve.wait_ge(self.out_hi, k + 1)
                    dve.scalar_tensor_tensor(h_lo[:, k, 0:self.n_tok], ps[:, k, 0:self.n_tok], col(self.gain, k),
                                             h_hi[:, k, 0:self.n_tok].bitcast(F32), ALU.mult, ALU.subtract)\
                       .then_inc(self.out_lo, 1)

            def pool(self, pool):
                for t in range(self.nt):
                    pool.wait_ge(self.mean, t + 1)
                    pool.tensor_tensor(rs[:, t:t + 1], ms[:, t:t + 1], neg_half[:, 0:1], ALU.pow)\
                        .then_inc(self.rooted, 1)
            def pe(self, pe):
                for t in range(self.nt):
                    pe.wait_ge(self.scaled, t + 1)
                    for k in range(KD):
                        last = pe.transpose(ps[:, k, t * P:(t + 1) * P], self.xs[:, t, k * P:(k + 1) * P], ident)
                        if t == self.nt - 1:
                            last.then_inc(self.turned, 1)

        class Projection(Part):

            def __init__(self, tag, stage, jobs, outs, nt=NT, banks=(0, 1, 2, 3, 4, 5, 6, 7), norm=None, low="dve"):
                self.done, self.out_act, self.out_dve = sem(tag + "_done"), sem(tag + "_out_act"), sem(tag + "_out_dve")
                self.u0, self.jobs, self.outs, self.nt, self.banks = START[stage], jobs, outs, nt, banks
                self.n = self.cuts = dict(STAGES)[stage]
                self.pe_turns = KD * len(jobs)
                self.starts = []
                for j, job in enumerate(jobs):
                    bk = KD if job[0] == "F" else job[2]
                    self.starts += range(KD * j, KD * (j + 1), bk)
                self.norm, self.low = norm, low
                self.widths, self.last_unit = [], []
                u = 0
                for job in jobs:
                    u += 1 if job[0] == "F" else KD // job[2]
                    for _ in range(1 if job[0] == "F" else nt):
                        self.widths.append(nt * P if job[0] == "F" else job[1])
                        self.last_unit.append(u - 1)
                assert u == self.n and len(self.widths) == len(outs), (tag, u, self.n)

            def bank(self, i, n):
                return ps[:, self.banks[i % len(self.banks)], 0:n]

            def emptied(self, pe, i):
                j = i - len(self.banks)
                if j >= 0:
                    who = self.outs[j][0]
                    n = sum(o[0] == who for o in self.outs[:j + 1])
                    pe.wait_ge(self.out_act if who == "act" else self.out_dve, n)

            def pe(self, pe):
                u, i, n_tok = self.u0, 0, self.nt * P
                for job in self.jobs:
                    if job[0] == "F":
                        self.emptied(pe, i)
                        w = unit(pe, u)
                        for k in range(KD):
                            if self.norm and i == 0:
                                pe.wait_ge(self.norm.out_lo, k + 1)
                            a, z = product(pe, self.bank(i, n_tok), [v[:, k * P:(k + 1) * P] for v in w],
                                           (h_hi[:, k, 0:n_tok], h_lo[:, k, 0:n_tok]), k == 0, k == KD - 1)
                            if k == 0 and u:
                                a.then_inc(weights_used, 1)
                            if k < KD - 1:
                                yield
                        z.then_inc(self.done, 1)
                        u += 1
                        i += 1
                        yield
                        continue
                    n, bk = job[1:]
                    for t in range(self.nt):
                        self.emptied(pe, i + t)
                    for k in range(KD):
                        if k % bk == 0:
                            w = unit(pe, u)
                        for t in range(self.nt):
                            a, z = product(pe, self.bank(i + t, n),
                                           (h_hi[:, k, t * P:(t + 1) * P], h_lo[:, k, t * P:(t + 1) * P]),
                                           [v[:, (k % bk) * n:(k % bk + 1) * n] for v in w], k == 0, k == KD - 1)
                            if k % bk == 0 and t == 0 and u:
                                a.then_inc(weights_used, 1)
                            if k == KD - 1:
                                z.then_inc(self.done, 1)
                        if k % bk == bk - 1:
                            u += 1
                        yield
                    i += self.nt

            def act(self, act):
                for f in range(self.n + 1):
                    if f < self.n:
                        cut_high(act, self.u0 + f + 1)
                    for i, (who, what, dst, arg) in enumerate(self.outs):
                        if who != "act" or self.last_unit[i] != f - 1:
                            continue
                        act.wait_ge(self.done, i + 1)
                        bank = self.bank(i, self.widths[i])
                        if what == "copy":
                            act.activation(dst, bank, ACT.Copy, scale=arg).then_inc(self.out_act, 1)
                        elif what == "silu":
                            act.activation(dst, bank, ACT.Silu).then_inc(self.out_act, 1)
                        elif what == "sigmoid":
                            act.activation(dst, bank, ACT.Sigmoid).then_inc(self.out_act, 1)
                    yield

            def dve(self, dve):
                for f in range(self.n + 1):
                    if self.low == "dve" and f < self.n:
                        cut_low(dve, self.u0 + f + 1)
                    for i, (who, what, dst, arg) in enumerate(self.outs):
                        if who != "dve" or self.last_unit[i] != f - 1:
                            continue
                        dve.wait_ge(self.done, i + 1)
                        bank = self.bank(i, self.widths[i])
                        if what == "copy":
                            dve.tensor_scalar(dst, bank, arg, None, ALU.mult).then_inc(self.out_dve, 1)
                        elif what == "bias":
                            dve.tensor_scalar(dst, bank, arg[0], arg[1], ALU.add, ALU.mult)\
                               .then_inc(self.out_dve, 1)
                        elif what == "conv":
                            w_col, b_col, chain = arg
                            last = dve.tensor_scalar(dst, bank, col("conv_w", w_col + 3), col("conv_b", b_col),
                                                     ALU.mult, ALU.add)
                            for tap in (1, 2, 3):
                                last.then_inc(chain, 1)
                                dve.wait_ge(chain, 3 * b_col + tap)
                                last = dve.scalar_tensor_tensor(dst[:, tap:S], bank[:, 0:S - tap],
                                                                col("conv_w", w_col + 3 - tap), dst[:, tap:S],
                                                                ALU.mult, ALU.add)
                            last.then_inc(self.out_dve, 1)
                        elif what == "add_row":
                            dve.tensor_tensor(dst, bank, arg, ALU.add).then_inc(self.out_dve, 1)
                    yield

            def pool(self, pool):
                if self.low == "pool":
                    for f in range(1, self.n + 1):
                        cut_low(pool, self.u0 + f)

        class Combine(Part):

            def __init__(self, tag, stage, y, nk, x_back=0, before=None):
                self.done, self.out_dve = sem(tag + "_done"), sem(tag + "_out_dve")
                self.u0, self.y, self.nk, self.x_back, self.before = START[stage], y, nk, x_back, before
                self.cuts = nk if START[stage] + nk < N_UNITS else nk - 1

            def ready(self, t):
                return self.out_dve, 2 * t + 2

            def act(self, act):
                for k in range(1, self.cuts + 1):
                    cut_high(act, self.u0 + k)

            def pe(self, pe):
                for k in range(self.nk):
                    if k == 0 and self.before:
                        pe.wait_ge(*self.before.banks_read())
                    if self.before and k < self.before.nk:
                        pe.wait_ge(self.before.out_lo, k + 1)
                    w = unit(pe, self.u0 + k)
                    for b in range(8):
                        t, half = b // 2, b % 2
                        a, z = product(pe, ps[:, b, :], [v[:, t * P:(t + 1) * P] for v in self.y(k)],
                                       [v[:, half * 512:(half + 1) * 512] for v in w], k == 0, k == self.nk - 1)
                        if b == 0:
                            a.then_inc(weights_used, 1)
                        if k == self.nk - 1:
                            z.then_inc(self.done, 1)

            def dve(self, dve):
                for k in range(1, self.cuts + 1):
                    cut_low(dve, self.u0 + k)
                if self.x_back:
                    dve.wait_ge(x_loaded, self.x_back)
                for b in range(8):
                    t, half = b // 2, b % 2
                    xv = x[:, t, half * 512:(half + 1) * 512]
                    dve.wait_ge(self.done, b + 1)
                    dve.tensor_tensor(xv, ps[:, b, :], xv, ALU.add).then_inc(self.out_dve, 1)

        class Turn(Part):

            def __init__(self, tag, src, dst, nk, gain=None, gate=None):
                self.turned, self.silued, self.gated, self.out_hi, self.out_lo = (
                    sem(tag + n) for n in ("_turned", "_silued", "_gated", "_out_hi", "_out_lo"))
                self.src, self.dst, self.nk, self.gate, self.silus_issued = src, dst, nk, gate, False
                self.gain = gain or (lambda k: 1.0)

            def pe(self, pe):
                for k in range(self.nk):
                    for t in range(NT):
                        last = pe.transpose(ps[:, k, t * P:(t + 1) * P], self.src(t, k), ident)
                    last.then_inc(self.turned, 1)

            def silus(self, act):
                self.silus_issued = True
                for k in range(self.nk):
                    act.activation(self.gate(k), self.gate(k), ACT.Silu).then_inc(self.silued, 1)

            def act(self, act):
                if self.gate and not self.silus_issued:
                    self.silus(act)
                for k in range(self.nk):
                    if self.gate:
                        act.wait_ge(self.gated, k + 1)
                        act.activation(self.dst(k)[0], self.gate(k), ACT.Copy).then_inc(self.out_hi, 1)
                    else:
                        act.wait_ge(self.turned, k + 1)
                        act.activation(self.dst(k)[0], ps[:, k, :], ACT.Copy, scale=self.gain(k))\
                           .then_inc(self.out_hi, 1)

            def dve(self, dve):
                for k in range(self.nk):
                    if self.gate:
                        dve.wait_ge(self.turned, k + 1)
                        dve.wait_ge(self.silued, k + 1)
                        dve.scalar_tensor_tensor(self.gate(k), ps[:, k, :], self.gain(k), self.gate(k),
                                                 ALU.mult, ALU.mult).then_inc(self.gated, 1)
                    else:
                        dve.wait_ge(self.out_hi, k + 1)
                        dve.scalar_tensor_tensor(self.dst(k)[1], ps[:, k, :], self.gain(k),
                                                 self.dst(k)[0].bitcast(F32), ALU.mult, ALU.subtract)\
                           .then_inc(self.out_lo, 1)

            def pool(self, pool):
                for k in range(self.nk if self.gate else 0):
                    pool.wait_ge(self.out_hi, k + 1)
                    pool.tensor_tensor(self.dst(k)[1], self.gate(k), self.dst(k)[0].bitcast(F32),
                                       ALU.subtract).then_inc(self.out_lo, 1)

            def banks_read(self):
                return (self.gated, self.nk) if self.gate else (self.out_lo, self.nk)

        def attend(tag, units, maps=1, fill=None, squares=None):
            n = len(units)
            t_bank, nb_t, o_bank, nb_o = (2, 2, 4, 2) if maps == 1 else (4, 1, 5, 1)
            NS = 2
            NP = 4
            LAG = 3 if maps == 2 else 4
            NPT = LAG - 1
            fills = fill.n if fill else 0

            def first_turn(step):
                return min(step, n) * fill.pe_turns // n

            def turns(step):
                return sum(first_turn(step) <= f < first_turn(step + 1) for f in fill.starts) if fill else 0

            def pe_turns(step):
                return first_turn(step + 1) - first_turn(step) if fill else 0

            def out_bank(i):
                return ps[:, o_bank + i % nb_o, 0:units[i]["dv"]]

            def turn_bank(i):
                return t_bank + i % nb_t

            names = ["scored", "lifted", "maxed", "expd", "mixed", "turned", "pT_out", "valued", "out", "chain",
                     "esink", "squared"]
            scored, lifted, maxed, expd, mixed, turned, pT_out, valued, out_done, dve_chain, esunk, squared = (
                sem(tag + "_" + m) for m in names)

            def score(i, m):
                return ps[:, (i % NS) * maps + m, 0:units[i]["w"]]

            def prob(i, m):
                a = ((i % NP) * maps + m) * 512
                return scr[:, a:a + units[i]["w"]]

            def pT(i):
                a = (i % NPT) * 512
                return big_row[:, a:a + 512] if maps == 2 else scr[:, 2048 + a:2560 + a]

            def stat(first, i, m=None):
                a = first + (2 * (i % 4) if maps == 2 else i % 8)
                return small[:, a:a + maps] if m is None else small[:, a + m:a + m + 1]

            NMAX, DEN, RDEN, ESINK, RATIO = 300, 308, 316, 324, 354

            with nc.Block() as block:
                @block.sync
                def _(sp):
                    stream(sp, fills)

                @block.gpsimd
                def _(pool):
                    if fill:
                        fill.pool(pool)

                @block.tensor
                def _(pe):
                    filler = fill.pe(pe) if fill else None
                    for step in range(n + LAG):
                        if step < n:
                            i, u = step, units[step]
                            if i >= NS:
                                pe.wait_ge(lifted, i - NS + 1)
                            for m in range(maps):
                                last = pe.matmul(score(i, m), u["q"][m], u["k"][m], start=True, stop=True)
                            last.then_inc(scored, 1)
                        for _ in range(pe_turns(step)):
                            next(filler)
                        if 2 <= step < n + 2:
                            i, u = step - 2, units[step - 2]
                            pe.wait_ge(mixed if maps == 2 else expd, i + 1)
                            if i >= nb_t:
                                pe.wait_ge(pT_out, i - nb_t + 1)
                            for b in range(len(u["v"])):
                                last = pe.transpose(ps[:, turn_bank(i), b * P:(b + 1) * P],
                                                    prob(i, 0)[:, b * P:(b + 1) * P], ident)
                            last.then_inc(turned, 1)
                        if step >= LAG:
                            i, u = step - LAG, units[step - LAG]
                            nb = len(u["v"])
                            pe.wait_ge(pT_out, i + 1)
                            if i >= nb_o:
                                pe.wait_ge(out_done, i - nb_o + 1)
                            for b in range(nb):
                                last = pe.matmul(out_bank(i), pT(i)[:, b * P:(b + 1) * P],
                                                 u["v"][b], start=b == 0, stop=b == nb - 1)
                            last.then_inc(valued, 1)
                    for _ in filler or ():
                        pass

                @block.scalar
                def _(act):
                    filler = fill.act(act) if fill else None
                    for step in range(n + (LAG + 2 if squares else 2)):
                        for _ in range(turns(step)):
                            next(filler)
                        if step < n:
                            i, u = step, units[step]
                            act.wait_ge(maxed, i + 1)
                            if "sink" in u:
                                act.activation(stat(ESINK, i), u["sink"], ACT.Exp, bias=stat(NMAX, i))\
                                   .then_inc(esunk, 1)
                            for m in range(maps):
                                last = act.activation(prob(i, m), prob(i, m), ACT.Exp, bias=stat(NMAX, i, m),
                                                      accum_out=stat(DEN, i, m))
                            last.then_inc(expd, 1)
                        if 2 <= step < n + 2:
                            i, u = step - 2, units[step - 2]
                            nb = len(u["v"])
                            act.wait_ge(turned, i + 1)
                            if i >= NPT:
                                act.wait_ge(valued, i - NPT + 1)
                            act.activation(pT(i)[:, 0:nb * P], ps[:, turn_bank(i), 0:nb * P], ACT.Copy)\
                               .then_inc(pT_out, 1)
                        if squares and step >= LAG + 2:
                            i, u = step - LAG - 2, units[step - LAG - 2]
                            act.wait_ge(out_done, i + 1)
                            if i:
                                act.wait_ge(squared, i)
                            act.activation(junk[:, :], u["out"], ACT.Square, accum_out=squares(i))\
                               .then_inc(squared, 1)
                    for _ in filler or ():
                        pass

                @block.vector
                def _(dve):
                    links = [0]
                    filler = fill.dve(dve) if fill else None

                    def link(ins):
                        links[0] += 1
                        ins.then_inc(dve_chain, 1)
                        dve.wait_ge(dve_chain, links[0])

                    for step in range(n + LAG + 1):
                        if step > LAG:
                            i, u = step - LAG - 1, units[step - LAG - 1]
                            if maps == 1:
                                dve.wait_ge(expd, i + 1)
                                if "sink" in u:
                                    dve.wait_ge(esunk, i + 1)
                                    link(dve.tensor_tensor(stat(DEN, i), stat(DEN, i), stat(ESINK, i), ALU.add))
                                link(dve.reciprocal(stat(RDEN, i), stat(DEN, i)))
                                if "gate" in u:
                                    link(dve.tensor_tensor(stat(RDEN, i), stat(RDEN, i), u["gate"], ALU.mult))
                            dve.wait_ge(valued, i + 1)
                            if u.get("add"):
                                last = dve.scalar_tensor_tensor(u["out"], out_bank(i), stat(RDEN, i), u["out"],
                                                                ALU.mult, ALU.add)
                            else:
                                last = dve.tensor_scalar(u["out"], out_bank(i), stat(RDEN, i, 0), None, ALU.mult)
                            last.then_inc(out_done, 1)
                        if step < n:
                            i, u = step, units[step]
                            dve.wait_ge(scored, i + 1)
                            if i >= NP:
                                dve.wait_ge(turned, i - NP + 1)
                            for m in range(maps):
                                if u["mask"] is None:
                                    last = dve.tensor_copy(prob(i, m), score(i, m))
                                else:
                                    last = dve.scalar_tensor_tensor(prob(i, m), u["mask"], u["slope"], score(i, m),
                                                                    ALU.mult, ALU.add)
                            last.then_inc(lifted, 1)
                            dve.wait_ge(lifted, i + 1)
                            for m in range(maps):
                                last = dve.tensor_reduce(stat(NMAX, i, m), prob(i, m), AXX, ALU.max, negate=True)
                            if "sink" in u:
                                link(last)
                                last = dve.tensor_tensor(stat(NMAX, i), stat(NMAX, i), u["neg_sink"], ALU.min)
                            last.then_inc(maxed, 1)
                        if fill and step == 0:
                            fill.prepare(dve)
                        for _ in range(turns(step)):
                            next(filler)
                        if maps == 2 and 1 <= step <= n:
                            i, u = step - 1, units[step - 1]
                            dve.wait_ge(expd, i + 1)
                            link(dve.reciprocal(stat(RDEN, i), stat(DEN, i)))
                            link(dve.scalar_tensor_tensor(stat(RATIO, i, 0), stat(DEN, i, 0), neg_lam,
                                                          stat(RDEN, i, 1), ALU.mult, ALU.mult))
                            dve.scalar_tensor_tensor(prob(i, 0), prob(i, 1), stat(RATIO, i, 0), prob(i, 0),
                                                     ALU.mult, ALU.add).then_inc(mixed, 1)
                    for _ in filler or ():
                        pass
            end_stage(fills)

        def token(ap, t):
            return ap[:, t * P:(t + 1) * P]

        Q, K, V, G, Z, XBC = 0, 4096, 8192, 12288, 16384, 20480
        qT, kT, gT = part(Q, [8, S]), part(K, [8, S]), part(G, [8, S])
        v_tok, z_tok = part(V, [NT, D]), part(Z, [NT, D])
        xbc = part(XBC, [12, S])
        dt_T = small[:, 400:912]
        jobs = [("F",)] * 16 + [("T", 512, 2)] * 4 + [("F",)]
        outs = [("act" if j % 2 == 0 else "dve", "copy", qT[:, j, :], 0.125) for j in range(8)]
        outs += [("act" if j % 2 == 0 else "dve", "copy", kT[:, j, :], 1.0) for j in range(8)]
        for tok, what in ((v_tok, "copy"), (z_tok, "silu")):
            for c in range(2):
                for t in range(NT):
                    who = "act" if what == "silu" or t % 2 == 0 else "dve"
                    outs.append((who, what, tok[:, t, c * 512:(c + 1) * 512], 1.0))
        outs += [("dve", "copy", dt_T[:, :], 1.0)]
        norm_a = Norm("norm_a", x, NT, EPS_A, "norm_a", part(G, [NT, D]), lambda t: (x_tile[t], 16), True)
        run(Setup(), norm_a, Projection("in_a", "in_a", jobs, outs, norm=norm_a), Lambda())

        y_a = x
        conv_chain = sem("conv_chain")
        outs = [("dve", "conv", xbc[:, j, :], (4 * j, j, conv_chain)) for j in range(12)]
        outs += [("act", "copy", gT[:, j, :], 1.0) for j in range(8)]
        fill_a = Projection("in_a2", "in_a2", [("F",)] * 20, outs, banks=(6, 7), low="pool")
        units = []
        for h in range(DA_H):
            for t in range(NT):
                w = (t + 1) * P
                units.append(dict(q=[token(qT[m * 64:m * 64 + 64, h, :], t) for m in range(2)],
                                  k=[kT[m * 64:m * 64 + 64, h, 0:w] for m in range(2)], w=w,
                                  mask=const("alibi")[:, S - w:S], slope=2.0 ** -(h + 1),
                                  v=[v_tok[:, b, h * P:(h + 1) * P] for b in range(t + 1)], dv=P,
                                  out=y_a[:, t, h * P:(h + 1) * P]))
        attend("da", units, maps=2, fill=fill_a, squares=lambda i: ss[:, i % NT * 8 + i // NT:i % NT * 8 + i // NT + 1])

        dta = small[:, 400:464]
        dtv = small[:, 464:528]
        decays = small[:, 528:720]
        sl_mean, sl_rooted, sl_scaled, silu_done = (
            sem(m) for m in ("sl_mean", "sl_rooted", "sl_scaled", "silu_done"))
        dt_turned, dt_chain, dt_biased, dt_exp, dt_ln, dta_ready = (
            sem(m) for m in ("dt_turned", "dt_chain", "dt_biased", "dt_exp", "dt_ln", "dta_ready"))
        heads_a = y_a[:, :, :].rearrange("p t (g w) -> p (t g) w", w=P)

        class DtAndScale(Part):

            def pe(self, pe):
                for t in range(NT):
                    last = pe.transpose(ps[:, 7, t * 16:(t + 1) * 16], dt_T[0:16, t * P:(t + 1) * P],
                                        ident[0:16, 0:16])
                last.then_inc(dt_turned, 1)

            def act(self, act):
                nabs = small[:, 784:848]
                act.wait_ge(dt_biased, 1)
                act.activation(nabs, nabs, ACT.Exp).then_inc(dt_exp, 1)
                act.wait_ge(dt_exp, 1)
                act.activation(nabs, nabs, ACT.Ln, bias=1.0).then_inc(dt_ln, 1)
                for j in range(12):
                    act.activation(xbc[:, j, :], xbc[:, j, :], ACT.Silu).then_inc(silu_done, 1)

            def pool(self, pool):
                pool.wait_ge(sl_mean, 1)
                for t in range(NT):
                    pool.tensor_tensor(rs[:, t * 8:t * 8 + 8], ms[:, t * 8:t * 8 + 8], neg_half[:, 0:8], ALU.pow)\
                        .then_inc(sl_rooted, 1)

            def scale(self, eng, t):
                eng.wait_ge(sl_rooted, t + 1)
                ya_t = heads_a[:, t * 8:t * 8 + 8, :]
                eng.tensor_tensor(ya_t, ya_t, rs[:, t * 8:t * 8 + 8].unsqueeze(2).broadcast_to([P, 8, P]),
                                  ALU.mult).then_inc(sl_scaled, 1)

            def dve(self, dve):
                v, nabs, relu = small[:, 720:784], small[:, 784:848], small[:, 848:912]
                dve.tensor_scalar(ms[:, 0:32], ss[:, 0:32], 1.0 / P, EPS_A, ALU.mult, ALU.add).then_inc(sl_mean, 1)
                dve.wait_ge(dt_turned, 1)
                dve.tensor_tensor(v.rearrange("p (t h) -> p t h", t=NT),
                                  ps[:, 7, 0:64].rearrange("p (t h) -> p t h", t=NT),
                                  row("dt_bias").unsqueeze(1).broadcast_to([P, NT, 16]), ALU.add).then_inc(dt_chain, 1)
                dve.wait_ge(dt_chain, 1)
                dve.scalar_tensor_tensor(nabs, v, -1.0, v, ALU.mult, ALU.min).then_inc(dt_biased, 1)
                dve.tensor_scalar(relu, v, 0.0, None, ALU.max).then_inc(dt_chain, 1)
                for t in range(NT):
                    self.scale(dve, t)
                dve.wait_ge(dt_ln, 1)
                dve.wait_ge(dt_chain, 2)
                dve.tensor_tensor(dtv, relu, nabs, ALU.add).then_inc(dt_chain, 1)
                dve.wait_ge(dt_chain, 3)
                dve.tensor_tensor(dta.rearrange("p (t h) -> p t h", t=NT), dtv.rearrange("p (t h) -> p t h", t=NT),
                                  neg_a.unsqueeze(1).broadcast_to([P, NT, 16]), ALU.mult).then_inc(dta_ready, 1)

        gate_a = gT
        turn_a = Turn("ya", lambda t, k: y_a[:, t, k * P:(k + 1) * P], lambda k: (h_hi[:, k, :], h_lo[:, k, :]), 8,
                      lambda k: subln8, lambda k: gate_a[:, k, :])

        class TurnWaits(Part):

            def pe(self, pe):
                pe.wait_ge(sl_scaled, NT)
                pe.wait_ge(xs_out_act, 5)
                pe.wait_ge(xs_out_dve, 5)
                pe.wait_ge(decays_ready, 1)
                pe.wait_ge(cb_masked, 2)

        xs_tok, xdt = part(0, [NT, D]), part(4096, [NT, D])
        TMP = 8192
        x_place = x[:, :, :].rearrange("p t d -> p (t d)")

        def two(v, n):
            return [v[:, 0:n], v[:, n:2 * n]]

        xdd = two(arena[:, 8704:9728], 512)
        dstr = [v.rearrange("p (h l) -> p h l", h=8) for v in (arena[:, 10752:11776], big_row[:, :])]
        exps = [v.rearrange("p (h l) -> p h l", h=8) for v in two(x_place[:, 2048:4096], 1024)]
        b_tok = scr[:, 0:1024].rearrange("p (c n) -> p c n", c=NT)
        cbm = scr[:, 1024:2048].rearrange("p (i l) -> p i l", i=8)
        state = scr[:, 2048:3072].rearrange("p (g d) -> p g d", g=2)
        y_b = part(G, [NT, D])
        xdt_pool = sem("xdt_pool")

        def times_dt(eng, t, done):
            eng.tensor_tensor(xdt[:, t, :].rearrange("p (h d) -> p h d", h=SSD_H),
                              xs_tok[:, t, :].rearrange("p (h d) -> p h d", h=SSD_H),
                              dtv[:, t * 16:(t + 1) * 16].unsqueeze(2).broadcast_to([P, SSD_H, SSD_P]),
                              ALU.mult).then_inc(done, 1)

        def make_dstr(pool, i):
            at_h = i * 8
            pool.tensor_tensor(dstr[i % 2], const("tri_gt").unsqueeze(1).broadcast_to([P, 8, P]),
                               dta[:, at_h:at_h + 8].unsqueeze(2).broadcast_to([P, 8, P]), ALU.mult)\
                .then_inc(dstr_ready, 1)

        dstr_ready = sem("dstr_ready")

        turned_x, xs_out_act, xs_out_dve, decay_sums, decays_ready, cb_done, cb_masked, xdt_ready = (
            sem(m) for m in ("turned_x", "xs_out_act", "xs_out_dve", "decay_sums", "decays_ready", "cb_done",
                             "cb_masked", "xdt_ready"))
        def xs_dst(i):
            if i < 8:
                return xs_tok[:, i // 2, (i % 2) * 512:(i % 2 + 1) * 512]
            return scr[:, (i - 8) * 512:(i - 7) * 512]

        class TokenMajor(Part):

            def pe(self, pe):
                pe.wait_ge(dt_chain, 1)
                for i in range(10):
                    t, half = (i // 2, i % 2) if i < 8 else (2 * (i - 8), 2)
                    b = i % 5
                    pe.wait_ge(silu_done, 4 * half + 4)
                    if i >= 5:
                        pe.wait_ge(xs_out_act if (i - 5) % 2 == 0 else xs_out_dve, (i - 5) // 2 + 1)
                    for j in range(4):
                        if half < 2:
                            src = xbc[:, half * 4 + j, t * P:(t + 1) * P]
                        else:
                            src = xbc[:, 8 + j % 2, (t + j // 2) * P:(t + j // 2 + 1) * P]
                        last = pe.transpose(ps[:, b, j * P:(j + 1) * P], src, ident)
                    last.then_inc(turned_x, 1)
                pe.wait_ge(dta_ready, 1)
                for j, name in enumerate(("tri_le", "tri_gt", "ones")):
                    last = pe.matmul(ps[:, 5, j * 64:(j + 1) * 64], const(name), dta, start=True, stop=True)
                last.then_inc(decay_sums, 1)
                for i in range(8):
                    c, g = i // 2, i % 2
                    last = pe.matmul(ps[:, 6 + i // 4, (i % 4) * P:(i % 4 + 1) * P], xbc[:, 8 + g, c * P:(c + 1) * P],
                                     xbc[:, 10 + g, c * P:(c + 1) * P], start=True, stop=True)
                last.then_inc(cb_done, 1)

            def act(self, act):
                for i in range(0, 10, 2):
                    act.wait_ge(turned_x, i + 1)
                    act.activation(xs_dst(i), ps[:, i % 5, :], ACT.Copy).then_inc(xs_out_act, 1)
                turn_a.silus(act)
                act.wait_ge(decay_sums, 1)
                act.activation(decays, ps[:, 5, 0:192], ACT.Exp).then_inc(decays_ready, 1)

            def dve(self, dve):
                for i in range(1, 10, 2):
                    dve.wait_ge(turned_x, i + 1)
                    dve.tensor_copy(xs_dst(i), ps[:, i % 5, :]).then_inc(xs_out_dve, 1)
                dve.wait_ge(cb_done, 1)
                for i in range(2):
                    dve.tensor_tensor(cbm[:, 4 * i:4 * i + 4, :],
                                      ps[:, 6 + i, :].rearrange("p (i l) -> p i l", i=4),
                                      const("tri_le").unsqueeze(1).broadcast_to([P, 4, P]), ALU.mult)\
                       .then_inc(cb_masked, 1)
                dve.wait_ge(xs_out_act, 4)
                dve.wait_ge(xs_out_dve, 4)
                for t in range(NT - 1):
                    times_dt(dve, t, xdt_ready)

            def pool(self, pool):
                pool.wait_ge(dta_ready, 1)
                make_dstr(pool, 0)
                make_dstr(pool, 1)
                pool.wait_ge(xs_out_act, 4)
                pool.wait_ge(xs_out_dve, 4)
                times_dt(pool, NT - 1, xdt_pool)

        off_read, z_scaled, sd_squared = sem("off_read"), sem("z_scaled"), sem("sd_squared")
        xdd_ready, skip_ready, segs_done, segs_exp, mixed_s, y_done, st_done, st_out, y_out, ssd_chain = (
            sem(m) for m in ("xdd_ready", "skip_ready", "segs_done", "segs_exp", "mixed_s", "y_done",
                             "st_done", "st_out", "y_out", "ssd_chain"))

        def per_head(a):
            return a.unsqueeze(2).broadcast_to([P, 8, SSD_P])

        def heads(a):
            return a.rearrange("p (h d) -> p h d", h=8)

        def squares_of(act, i):
            c, g = i // 2, i % 2
            act.wait_ge(z_scaled, i + 1)
            if i >= 2:
                act.wait_ge(sd_squared, i - 1)
            act.activation(arena[:, 9728 + (i % 2) * 512:10240 + (i % 2) * 512],
                           y_b[:, c, g * 512:(g + 1) * 512], ACT.Square, accum_out=ss[:, i:i + 1])\
               .then_inc(sd_squared, 1)

        class Chunks(Part):

            def pe(self, pe):
                def segs(i):
                    pe.wait_ge(dstr_ready, i + 1)
                    if i >= 2:
                        pe.wait_ge(segs_exp, 2 * i - 2)
                    for j in range(8):
                        last = pe.matmul(ps[:, 2 * (i % 2) + j // 4, (j % 4) * P:(j % 4 + 1) * P],
                                         dstr[i % 2][:, j, :], const("tri_le"), start=True, stop=True)
                        if j % 4 == 3:
                            last.then_inc(segs_done, 1)

                pe.wait_ge(turn_a.gated, 8)
                segs(0)
                for i in range(8):
                    c, g = i // 2, i % 2
                    if i < 7:
                        segs(i + 1)
                    if c > 0:
                        if c > 1 or g:
                            pe.wait_ge(off_read, i - 2)
                        pe.wait_ge(st_out, i - 1)
                        pe.matmul(ps[:, 5, :], xbc[:, 10 + g, c * P:(c + 1) * P], state[:, g, :],
                                  start=True, stop=True)
                    pe.wait_ge(mixed_s, i + 1)
                    if i == 0:
                        pe.wait_ge(xdt_ready, 3)
                    if i == 6:
                        pe.wait_ge(xdt_pool, 1)
                    if i >= 2:
                        pe.wait_ge(y_out, i - 1)
                    for j in range(8):
                        h = g * 8 + j
                        last = pe.matmul(ps[:, 4 + 3 * (i % 2), j * 64:(j + 1) * 64], exps[i % 2][:, j, :],
                                         xdt[:, c, h * 64:(h + 1) * 64], start=True, stop=True)
                    last.then_inc(y_done, 1)
                    pe.wait_ge(xdd_ready, i + 1)
                    if i:
                        pe.wait_ge(st_out, i)
                    pe.matmul(ps[:, 6, :], b_tok[:, c, g * P:(g + 1) * P], xdd[i % 2], start=True, stop=True)\
                      .then_inc(st_done, 1)

            def act(self, act):
                for i in range(8):
                    for half in range(2):
                        act.wait_ge(segs_done, 2 * i + half + 1)
                        if i >= 2 and half == 0:
                            act.wait_ge(y_done, i - 1)
                        act.activation(exps[i % 2][:, 4 * half:4 * half + 4, :],
                                       ps[:, 2 * (i % 2) + half, :].rearrange("p (i l) -> p i l", i=4), ACT.Exp)\
                           .then_inc(segs_exp, 1)
                    if i >= 2:
                        squares_of(act, i - 2)
                squares_of(act, 6)
                squares_of(act, 7)

            def pool(self, pool):
                pool.wait_ge(decays_ready, 1)
                pool.wait_ge(xdt_ready, 3)
                pool.wait_ge(turn_a.out_lo, 8)
                pool.wait_ge(turn_a.out_hi, 8)
                for i in range(8):
                    c, g = i // 2, i % 2
                    hs = slice(c * 16 + g * 8, c * 16 + g * 8 + 8)
                    if 1 <= i < 7:
                        pool.wait_ge(segs_done, 2 * i)
                        make_dstr(pool, i + 1)
                    if i >= 2:
                        pool.wait_ge(st_done, i - 1)
                    pool.tensor_tensor(heads(xdd[i % 2]), heads(xdt[:, c, g * 512:(g + 1) * 512]),
                                       per_head(decays[:, 64 + hs.start:64 + hs.stop]), ALU.mult)\
                        .then_inc(xdd_ready, 1)
                    pool.tensor_tensor(heads(y_b[:, c, g * 512:(g + 1) * 512]),
                                       heads(xs_tok[:, c, g * 512:(g + 1) * 512]),
                                       per_head(row("d_skip")[:, g * 8:(g + 1) * 8]), ALU.mult)\
                        .then_inc(skip_ready, 1)

            def dve(self, dve):
                links = [0]

                def link(ins):
                    links[0] += 1
                    ins.then_inc(ssd_chain, 1)
                    dve.wait_ge(ssd_chain, links[0])

                def mix(i):
                    dve.wait_ge(segs_exp, 2 * i + 2)
                    dve.tensor_tensor(exps[i % 2], exps[i % 2], cbm[:, i:i + 1, :].broadcast_to([P, 8, P]), ALU.mult)\
                       .then_inc(mixed_s, 1)

                dve.wait_ge(decays_ready, 1)
                dve.wait_ge(cb_masked, 2)
                mix(0)
                for i in range(8):
                    c, g = i // 2, i % 2
                    hs = slice(c * 16 + g * 8, c * 16 + g * 8 + 8)
                    if i < 7:
                        mix(i + 1)
                    y = y_b[:, c, g * 512:(g + 1) * 512]
                    tmp = arena[:, TMP:TMP + 512]
                    if c > 0:
                        dve.wait_ge(y_done, i + 1)
                        dve.tensor_tensor(heads(tmp), heads(ps[:, 5, :]), per_head(decays[:, hs]), ALU.mult)\
                           .then_inc(off_read, 1)
                        dve.wait_ge(off_read, i - 1)
                        dve.wait_ge(skip_ready, i + 1)
                        link(dve.tensor_tensor(y, y, tmp, ALU.add))
                    dve.wait_ge(skip_ready, i + 1)
                    dve.wait_ge(y_done, i + 1)
                    dve.tensor_tensor(y, ps[:, 4 + 3 * (i % 2), :], y, ALU.add).then_inc(y_out, 1)
                    if c > 0:
                        link(dve.tensor_tensor(heads(state[:, g, :]), heads(state[:, g, :]),
                                               per_head(decays[:, 128 + hs.start:128 + hs.stop]), ALU.mult))
                        dve.wait_ge(st_done, i + 1)
                        dve.tensor_tensor(state[:, g, :], ps[:, 6, :], state[:, g, :], ALU.add).then_inc(st_out, 1)
                    else:
                        dve.wait_ge(st_done, i + 1)
                        dve.tensor_copy(state[:, g, :], ps[:, 6, :]).then_inc(st_out, 1)
                    dve.wait_ge(y_out, i + 1)
                    dve.tensor_tensor(y, y, z_tok[:, c, g * 512:(g + 1) * 512], ALU.mult).then_inc(z_scaled, 1)

        gs_mean, gs_rooted, gs_scaled, gs_scaled_act = (
            sem(m) for m in ("gs_mean", "gs_rooted", "gs_scaled", "gs_scaled_act"))
        groups_b = y_b[:, :, :].rearrange("p t (g w) -> p (t g) w", w=512)

        class GroupScale(Part):

            def sync(self, sp):
                sp.wait_ge(y_done, 8)
                sp.dma_start(x[:, :, :], x_dram.rearrange("(t p) d -> p t d", p=P)).then_inc(x_loaded, 16)
                sp.dma_start(big_row[:, :], big_dram[0, :].partition_broadcast(P)).then_inc(big_loaded, 16)

            def pool(self, pool):
                pool.wait_ge(gs_mean, 1)
                pool.tensor_tensor(rs[:, 0:8], ms[:, 0:8], neg_half[:, 0:8], ALU.pow).then_inc(gs_rooted, 1)

            def dve(self, dve):
                dve.wait_ge(sd_squared, 8)
                dve.tensor_scalar(ms[:, 0:8], ss[:, 0:8], 1.0 / 512, EPS_A, ALU.mult, ALU.add).then_inc(gs_mean, 1)
                dve.wait_ge(gs_rooted, 1)
                for i in range(5):
                    dve.tensor_scalar(groups_b[:, i, :], groups_b[:, i, :], rs[:, i:i + 1], None, ALU.mult)\
                       .then_inc(gs_scaled, 1)

            def act(self, act):
                act.wait_ge(gs_rooted, 1)
                for i in range(5, 8):
                    act.activation(groups_b[:, i, :], groups_b[:, i, :], ACT.Copy, scale=rs[:, i:i + 1])\
                       .then_inc(gs_scaled_act, 1)

            def pe(self, pe):
                pe.wait_ge(gs_scaled, 5)
                pe.wait_ge(gs_scaled_act, 3)
                pe.wait_ge(y_out, 8)
                pe.wait_ge(st_out, 8)

        yb = halves("yb", ARENA, ARENA + 4096, 8)
        turn_b = Turn("yb", lambda t, k: y_b[:, t, k * P:(k + 1) * P], lambda k: (yb[0][:, k, :], yb[1][:, k, :]), 8,
                      lambda k: col("ssd_norm", k))
        out_a = Combine("out_a", "out_a", lambda k: (h_hi[:, k, :], h_lo[:, k, :]) if k < 8
                        else (yb[0][:, k - 8, :], yb[1][:, k - 8, :]), 16, x_back=16, before=turn_b)

        norm_c = Norm("norm_c", x, NT, EPS_A, "norm_c", part(12288, [NT, D]), out_a.ready)
        qT, kT, v_tok = part(0, [8, S]), part(4096, [2, S]), part(5120, [NT, P])
        gT, o_tok = part(5632, [8, S]), part(9728, [NT, D])
        jobs = [("F",)] * 10 + [("T", 128, 8)]
        outs = [("dve", "bias", qT[:, j, :], (col("bq", j), 0.125)) for j in range(8)]
        outs += [("dve", "bias", kT[:, j, :], (col("bk", j), 1.0)) for j in range(2)]
        outs += [("dve", "add_row", v_tok[:, t, :], row("bv")) for t in range(NT)]
        run(DtAndScale(), TokenMajor(), TurnWaits(), turn_a, Chunks(), GroupScale(), turn_b, out_a, norm_c,
            Projection("in_c", "in_c", jobs, outs, norm=norm_c))
        fill_c = Projection("in_c2", "in_c2", [("F",)] * 8,
                            [("dve", "bias", gT[:, j, :], (col("bg", j), 1.0)) for j in range(8)],
                            banks=(6, 7), low="pool")
        units = []
        for h in range(SW_H):
            kv, hp = h // 8, (h % 2) * 64
            for t in range(NT):
                lo = max(t - 1, 0) * P
                w = (t + 1) * P - lo
                units.append(dict(q=[token(qT[hp:hp + 64, h // 2, :], t)], k=[kT[hp:hp + 64, kv, lo:lo + w]], w=w,
                                  mask=const("sw")[:, 2 * P - w:], slope=2.0 ** (-8.0 * (h + 1) / SW_H),
                                  v=[v_tok[:, lo // P + b, kv * 64:kv * 64 + 64] for b in range(w // P)], dv=64,
                                  out=o_tok[:, t, h * 64:(h + 1) * 64], sink=row("sinks")[:, h:h + 1],
                                  neg_sink=neg_sink[:, h:h + 1]))
        attend("sw", units, fill=fill_c)
        recycle()
        turn_c = Turn("oc", lambda t, k: o_tok[:, t, k * P:(k + 1) * P], lambda k: (h_hi[:, k, :], h_lo[:, k, :]), 8,
                      gate=lambda k: gT[:, k, :])
        out_c = Combine("out_c", "out_c", lambda k: (h_hi[:, k, :], h_lo[:, k, :]), 8, before=turn_c)

        class RowNorm(Part):

            def __init__(self, tag, eps, ready, store=False):
                self.squared, self.mean, self.rooted, self.scaled = (
                    sem(tag + m) for m in ("_squared", "_mean", "_rooted", "_scaled"))
                self.eps, self.x_ready, self.storing = eps, ready, store

            def ready(self, t):
                return self.scaled, t + 1

            def act(self, act):
                for t in range(NT):
                    act.wait_ge(*self.x_ready(t))
                    act.activation(scr[:, t * D:(t + 1) * D], x[:, t, :], ACT.Square, accum_out=ss[:, 32 + t:33 + t])\
                       .then_inc(self.squared, 1)

            def pool(self, pool):
                for t in range(NT):
                    pool.wait_ge(self.mean, t + 1)
                    pool.tensor_tensor(rs[:, 32 + t:33 + t], ms[:, 32 + t:33 + t], neg_half[:, 0:1], ALU.pow)\
                        .then_inc(self.rooted, 1)

            def dve(self, dve):
                dve.wait_ge(big_loaded, 32 if self.storing else 16)
                for t in range(NT + 1):
                    if t < NT:
                        dve.wait_ge(self.squared, t + 1)
                        dve.tensor_scalar(ms[:, 32 + t:33 + t], ss[:, 32 + t:33 + t], 1.0 / D, self.eps,
                                          ALU.mult, ALU.add).then_inc(self.mean, 1)
                    if t:
                        dve.wait_ge(self.rooted, t)
                        dve.scalar_tensor_tensor(x[:, t - 1, :], x[:, t - 1, :], rs[:, 31 + t:32 + t], big_row[:, :],
                                                 ALU.mult, ALU.mult).then_inc(self.scaled, 1)

            def store(self, sp):
                if self.storing:
                    for t in range(NT):
                        sp.wait_ge(self.scaled, t + 1)
                        sp.dma_start(out_dram[t * P:(t + 1) * P, :], x[:, t, :]).then_inc(stored, 16)
                    sp.wait_ge(stored, 16 * NT)

        norm_x = RowNorm("final_a", EPS_A, out_c.ready)
        norm_m = Norm("norm_m", x, NT, EPS_B, "norm_mix", part(12288, [NT, D]), norm_x.ready)
        ft = part(0, [15, S])
        tv = part(7680, [NT, 512])
        gm = part(9728, [24, S])
        o_abc = part(22016, [NT, 768])
        jobs = [("F",)] * 15 + [("T", 512, 2)]
        outs = []
        for j in range(15):
            scale = 0.125 if j in (0, 1, 4, 5, 11, 12) else 1.0
            outs.append(("act" if j % 2 == 0 else "dve", "copy", ft[:, j, :], scale))
        outs += [("dve", "copy", tv[:, t, :], 1.0) for t in range(NT)]
        run(turn_c, out_c, norm_x, norm_m, Projection("in_m", "in_m", jobs, outs, norm=norm_m))

        swapped, sin_done, cos_done, rope_done, gates_done, widx_done = (
            sem(m) for m in ("swapped", "sin_done", "cos_done", "rope_done", "gates_done", "widx_done"))
        sa_names = ["sb_z", "sb_nabs", "sb_exp", "sb_ln", "sb_sp", "sb_mask", "sb_sum", "sb_w", "sb_o", "sb_out"]
        sb_z, sb_nabs, sb_exp, sb_ln, sb_sp, sb_mask, sb_sum, sb_w, sb_o, sb_out = (sem(m) for m in sa_names)

        def z_bank(first, b):
            if b == 3:
                return ps[:, first + 1, 384:512]
            return ps[:, first + b, 0:S - b * P]

        def sb_out_bank(t):
            return ps[:, 5, 256 + t * 64:256 + (t + 1) * 64]

        fill_m2 = Projection("in_m2", "in_m2", [("F",)] * 10,
                             [("dve", "copy", gm[:, j, :], 1.0) for j in range(10)], banks=(6, 7), low="pool")
        FREE = 9728 + 10 * S
        nab = scr[:, 0:2048].rearrange("p (b q) -> p b q", b=NT)
        sb_p = part(FREE, [NT, S])
        spls = [scr[:, 2048:4096].rearrange("p (b q) -> p b q", b=NT), part(FREE + 2048, [NT, S])]
        rope_tmp = part(FREE + 4096, [4, S])
        with nc.Block() as block:
            @block.sync
            def _(sp):
                stream(sp, fill_m2.n)

            @block.gpsimd
            def _(pool):
                for j in range(11):
                    hp = P if j < 10 else 64
                    pool.wait_ge(swapped, j + 1)
                    pool.tensor_tensor(ft[0:hp, j, :], ft[0:hp, j, :], const("cos")[0:hp, :], ALU.mult)\
                        .then_inc(cos_done, 1)
                    if j == 2:
                        cut_low(pool, fill_m2.u0 + 1)
                for f in range(2, fill_m2.n + 1):
                    cut_low(pool, fill_m2.u0 + f)

            @block.tensor
            def _(pe):
                filler = fill_m2.pe(pe)

                def fill_unit():
                    for _ in range(KD):
                        next(filler)

                def logits(h):
                    qh, kh = (ft[h % 2 * 64:h % 2 * 64 + 64, a + h // 2, :] for a in (11, 13))
                    for b in range(NT):
                        pe.matmul(z_bank(0, b), kh[:, b * P:(b + 1) * P], qh[:, b * P:S], start=True, stop=True)\
                          .then_inc(sb_z, 1)

                logits(0)
                for j in range(11):
                    if j >= 3:
                        next(filler)
                        pe.wait_ge(sin_done, j - 2)
                    pe.matmul(ps[:, 3 + j % 3, :], const("perm"), ft[:, j, :], start=True, stop=True)\
                      .then_inc(swapped, 1)
                fill_unit()
                for h in range(4):
                    qh, kh = (ft[h % 2 * 64:h % 2 * 64 + 64, a + h // 2, :] for a in (11, 13))
                    pe.wait_ge(sb_mask, 4 * (h + 1))
                    if h < 3:
                        logits(h + 1)
                    if h:
                        pe.wait_ge(sb_out, 4 * h)
                    else:
                        pe.wait_ge(sin_done, 11)
                    spl = spls[h % 2]
                    for b in range(NT):
                        bank = z_bank(3, b)
                        pe.matmul(bank, kh[:, b * P:(b + 1) * P], qh[:, b * P:S], start=True, stop=False)
                        pe.matmul(bank, const("neg_ge"), spl[:, b, b * P:S], start=False, stop=False)
                        for later in range(b + 1, NT):
                            pe.matmul(bank[:, (later - b) * P:], const("neg_ones"), spl[:, later, later * P:S],
                                      start=False, stop=False)
                        pe.matmul(bank[:, 0:P], ident, const("strict_neg"), start=False, stop=True)\
                          .then_inc(sb_sum, 1)
                    fill_unit()
                    fill_unit()
                    pe.wait_ge(sb_w, 4 * (h + 1))
                    for t in range(NT):
                        for b in range(t + 1):
                            last = pe.matmul(sb_out_bank(t), sb_p[:, b, t * P:(t + 1) * P],
                                             tv[:, b, h * 64:(h + 1) * 64], start=b == 0, stop=b == t)
                        last.then_inc(sb_o, 1)

            @block.scalar
            def _(act):
                filler = fill_m2.act(act)

                def log_term(h):
                    for b in range(NT):
                        act.wait_ge(sb_z, 4 * h + 4)
                        act.activation(nab[:, b, b * P:S], z_bank(0, b), ACT.Abs).then_inc(sb_nabs, 1)
                    for b in range(NT):
                        act.wait_ge(sb_nabs, 4 * h + b + 1)
                        act.activation(nab[:, b, b * P:S], nab[:, b, b * P:S], ACT.Exp, scale=-1.0).then_inc(sb_exp, 1)
                    for b in range(NT):
                        act.wait_ge(sb_exp, 4 * h + b + 1)
                        act.activation(nab[:, b, b * P:S], nab[:, b, b * P:S], ACT.Ln, bias=1.0).then_inc(sb_ln, 1)

                next(filler)
                log_term(0)
                next(filler)
                for h in range(4):
                    if h < 3:
                        log_term(h + 1)
                    next(filler)
                    for b in range(NT):
                        act.wait_ge(sb_sum, 4 * h + 4)
                        if h and b == 0:
                            act.wait_ge(sb_o, 4 * h)
                        act.activation(sb_p[:, b, b * P:S], z_bank(3, b), ACT.Exp).then_inc(sb_w, 1)
                    next(filler)
                for _ in filler:
                    pass

            @block.vector
            def _(dve):
                filler = fill_m2.dve(dve)

                def softplus(h):
                    spl = spls[h % 2]
                    for b in range(NT):
                        dve.wait_ge(sb_ln, 4 * h + b + 1)
                        if h >= 2 and b == 0:
                            dve.wait_ge(sb_sum, 4 * (h - 1))
                        dve.scalar_tensor_tensor(spl[:, b, b * P:S], z_bank(0, b), 0.0, nab[:, b, b * P:S],
                                                 ALU.max, ALU.add).then_inc(sb_sp, 1)
                        dve.wait_ge(sb_sp, 4 * h + b + 1)
                        dve.tensor_tensor(spl[:, b, b * P:(b + 1) * P], spl[:, b, b * P:(b + 1) * P],
                                          const("strict01"), ALU.mult).then_inc(sb_mask, 1)

                for j in range(11):
                    hp = P if j < 10 else 64
                    tmp = rope_tmp[0:hp, j % 4, :]
                    dve.wait_ge(swapped, j + 1)
                    dve.tensor_tensor(tmp, ps[0:hp, 3 + j % 3, :], const("sin")[0:hp, :], ALU.mult)\
                       .then_inc(sin_done, 1)
                    dve.wait_ge(sin_done, j + 1)
                    dve.wait_ge(cos_done, j + 1)
                    dve.tensor_tensor(ft[0:hp, j, :], ft[0:hp, j, :], tmp, ALU.add).then_inc(rope_done, 1)
                softplus(0)
                for t in range(NT):
                    dve.tensor_scalar(tv[:, t, 448:452], tv[:, t, 448:452], 1.0 / 16, None, ALU.mult)\
                       .then_inc(widx_done, 1)
                next(filler)
                next(filler)
                for h in range(4):
                    if h < 3:
                        softplus(h + 1)
                    next(filler)
                    next(filler)
                    for t in range(NT):
                        dve.wait_ge(sb_o, 4 * h + 4)
                        dve.tensor_copy(o_abc[:, t, h * 64:(h + 1) * 64], sb_out_bank(t)).then_inc(sb_out, 1)
                for _ in filler:
                    pass
        end_stage(fill_m2.n)

        sel = arena[:, 25088:26624]
        sel_at = (None, 0, 256, 640)
        relu_at = ((), (0, 256, 512, 768), (1024, 1408, 1792, 2176), (2560, 3072, 3584, 0))
        ix_scored, ix_relu, ix_sum, ix_top, ix_sel, gate_m2 = (
            sem(m) for m in ("ix_scored", "ix_relu", "ix_sum", "ix_top", "ix_sel", "gate_m2"))
        fill_m3 = Projection("in_m3", "in_m3", [("F",)] * 14,
                             [("act", "sigmoid", gm[:, 10 + j, :], 1.0) for j in range(14)], banks=(6, 7), low="pool")

        def selected(t):
            return sel[:, sel_at[t]:sel_at[t] + (t + 1) * P]

        def relu_of(t, h):
            return scr[:, relu_at[t][h]:relu_at[t][h] + (t + 1) * P]

        blocks = part(1024, [32, 32])
        block_hi = at("block_hi", [P, 32, 32], F32R, H_PLACE)
        block_lo = at("block_lo", [P, 32, 32], F32R, HL_PLACE)
        hid_k = small[:, 0:32]
        hid_v4 = small[:, 400:528]
        kc_T = small[:, 528:560]
        vc_diag = small[:, 560:816]
        gelued = at("gelued", [32, 256], F32, H_PLACE + 2048)[:, :]
        cm_zero, cm_diag, cm_blocks, cm_hi, cm_lo, cm_hid, cm_gelu, cm_turned, cm_hidden, cm_two, cm_out = (
            sem(m) for m in ("cm_zero", "cm_diag", "cm_blocks", "cm_hi", "cm_lo", "cm_hid", "cm_gelu", "cm_turned",
                             "cm_hidden", "cm_two", "cm_out"))

        def make_blocks(pool):
            pool.wait_ge(ix_scored, 12)
            pool.memset(blocks, 0.0).then_inc(cm_zero, 1)
            pool.wait_ge(cm_zero, 1)
            src = ft[:, 10, :].rearrange("p (n j) -> p j n", j=16)
            for half in range(2):
                pool.tensor_tensor(blocks[:, half * 16:half * 16 + 16, 0:N_CMP], src[:, :, half:half + N_CMP],
                                   col("pos", half * 16, 16).unsqueeze(2).broadcast_to([P, 16, N_CMP]),
                                   ALU.add).then_inc(cm_blocks, 1)

        mem_x = part(5632, [2, D])
        mem_loaded = sem("mem_loaded")
        with nc.Block() as block:
            @block.sync
            def _(sp):
                sp.dma_start(mem_x, mem_dram.rearrange("(t p) d -> p t d", p=P)).then_inc(mem_loaded, 16)
                sp.dma_start(big_row[:, :], big_dram[1, :].partition_broadcast(P)).then_inc(big_loaded, 16)
                stream(sp, fill_m3.n)

            @block.gpsimd
            def _(pool):
                for f in range(1, fill_m3.n + 1):
                    cut_low(pool, fill_m3.u0 + f)
                    if f == 7:
                        make_blocks(pool)

            @block.tensor
            def _(pe):
                for t in range(1, NT):
                    w = (t + 1) * P
                    for h in range(4):
                        i = 4 * (t - 1) + h
                        hp = (h % 2) * 64
                        if i >= 6:
                            pe.wait_ge(ix_relu, i - 5)
                        pe.matmul(ps[:, i % 6, 0:w], ft[hp:hp + 64, 2 + h // 2, t * P:(t + 1) * P],
                                  ft[hp:hp + 64, 7, 0:w], start=True, stop=True).then_inc(ix_scored, 1)
                for _ in fill_m3.pe(pe):
                    pass

            @block.scalar
            def _(act):
                filler = fill_m3.act(act)
                next(filler)
                for i in range(12):
                    t, h = 1 + i // 4, i % 4
                    act.wait_ge(ix_scored, i + 1)
                    if i == 11:
                        act.wait_ge(ix_sum, 4)
                    act.activation(relu_of(t, h), ps[:, i % 6, 0:(t + 1) * P], ACT.Relu).then_inc(ix_relu, 1)
                for t in range(NT):
                    act.activation(tv[:, t, 452:464], tv[:, t, 452:464], ACT.Sigmoid).then_inc(gates_done, 1)
                next(filler)
                for j in range(10):
                    act.activation(gm[:, j, :], gm[:, j, :], ACT.Sigmoid).then_inc(gate_m2, 1)
                for _ in filler:
                    pass

            @block.vector
            def _(dve):
                sums = tops = 0
                for t in range(1, NT):
                    w = (t + 1) * P
                    score = selected(t)
                    acc = const("causal")[:, S - w:S]
                    for h in range(4):
                        dve.wait_ge(ix_relu, 4 * (t - 1) + h + 1)
                        if sums % 4:
                            dve.wait_ge(ix_sum, sums)
                        dve.scalar_tensor_tensor(score, relu_of(t, h), tv[:, t, 448 + h:449 + h], acc,
                                                 ALU.mult, ALU.add).then_inc(ix_sum, 1)
                        sums += 1
                        acc = score
                    dve.wait_ge(ix_sum, sums)
                    for r in range(P // 8):
                        top = small[:, 912 + 8 * (r % 2):920 + 8 * (r % 2)]
                        dve.max(top, score).then_inc(ix_top, 1)
                        dve.wait_ge(ix_top, tops + 1)
                        dve.match_replace(score, top, score, -3.0e38).then_inc(ix_top, 1)
                        dve.wait_ge(ix_top, tops + 2)
                        tops += 2
                    dve.tensor_scalar(score, score, -2.0e38, NEG, ALU.is_gt, ALU.mult).then_inc(ix_sel, 1)

        end_stage(fill_m3.n)

        class Compression(Part):
            n = cuts = 4
            pe_turns, starts = 32, range(0, 32, 8)
            u0 = START["cmp"]

            def pe(self, pe):
                pe.wait_ge(cm_lo, 1)
                for q in range(4):
                    w = unit(pe, self.u0 + q)
                    for l in range(8):
                        for j in range(2):
                            rows_j = slice(j * 64, j * 64 + 64)
                            a, z = product(pe, ps[0:32, 6 + j, 0:P],
                                           (block_hi[rows_j, q * 8 + l, :], block_lo[rows_j, q * 8 + l, :]),
                                           [v[rows_j, l * P:(l + 1) * P] for v in w], q + l == 0, q * 8 + l == 31)
                            if l + j == 0:
                                a.then_inc(weights_used, 1)
                        if q * 8 + l == 31:
                            z.then_inc(cm_hid, 1)
                        yield
                pe.wait_ge(cm_gelu, 2)
                for j in range(2):
                    pe.transpose(ps[:, 6 + j, P:P + 32], gelued[:, j * P:(j + 1) * P], ident[0:32, 0:32])\
                      .then_inc(cm_turned, 1)
                pe.wait_ge(cm_hidden, 2)
                pe.matmul(ps[:, 6, 0:32], col("w2", 0, P), hid_k, start=True, stop=True)
                pe.matmul(ps[:, 7, 0:64], hid_v4, col("w2", P, 64), start=True, stop=True).then_inc(cm_two, 1)

            def act(self, act):
                act.activation(block_hi[:, :, :], blocks, ACT.Copy).then_inc(cm_hi, 1)
                for q in range(1, 5):
                    cut_high(act, self.u0 + q)
                    yield
                act.wait_ge(cm_hid, 1)
                for j in range(2):
                    act.activation(gelued[:, j * P:(j + 1) * P], ps[0:32, 6 + j, 0:P], ACT.Gelu_apprx_tanh)\
                       .then_inc(cm_gelu, 1)

            def prepare(self, dve):
                dve.memset(vc_diag, 0.0).then_inc(cm_diag, 1)
                dve.wait_ge(cm_hi, 1)
                dve.tensor_tensor(block_lo[:, :, :], blocks, block_hi[:, :, :].bitcast(F32), ALU.subtract)\
                   .then_inc(cm_lo, 1)

            def dve(self, dve):
                for _ in range(4):
                    yield
                dve.wait_ge(cm_turned, 2)
                dve.tensor_copy(hid_k, ps[:, 6, P:P + 32]).then_inc(cm_hidden, 1)
                dve.tensor_copy(hid_v4.rearrange("p (h n) -> p h n", h=4),
                                ps[:, 7, P:P + 32].unsqueeze(1).broadcast_to([P, 4, 32])).then_inc(cm_hidden, 1)
                dve.wait_ge(cm_two, 1)
                dve.tensor_copy(kc_T, ps[:, 6, 0:32]).then_inc(cm_out, 1)
                dve.wait_ge(cm_diag, 1)
                for h in range(4):
                    rows_h = slice(32 * h, 32 * h + 32)
                    dve.tensor_copy(vc_diag[rows_h, h * 64:(h + 1) * 64], ps[rows_h, 7, 0:64]).then_inc(cm_out, 1)

            def pool(self, pool):
                for q in range(1, 5):
                    cut_low(pool, self.u0 + q)

        units = []
        for t in range(NT):
            w = (t + 1) * P
            for h in range(4):
                hp = (h % 2) * 64
                units.append(dict(q=[ft[hp:hp + 64, h // 2, t * P:(t + 1) * P]], k=[ft[hp:hp + 64, 6, 0:w]], w=w,
                                  mask=selected(t) if t else const("causal")[:, S - w:S], slope=1.0,
                                  v=[tv[:, b, 256:320] for b in range(t + 1)], dv=64,
                                  out=o_abc[:, t, 256 + h * 64:256 + (h + 1) * 64]))
        attend("dsa", units, fill=Compression())

        cs_names = ["cs_scored", "cs_chain", "cs_shifted", "cs_exp", "cs_prob", "cs_turned", "cs_pT", "cs_valued",
                    "cs_out"]
        cs_scored, cs_chain, cs_shifted, cs_exp, cs_prob, cs_turned, cs_pT, cs_valued, cs_out = (
            sem(m) for m in cs_names)
        cs_flat, cs_turned_p = scr[:, 0:512], scr[:, 512:1024]
        cs_p = cs_flat.rearrange("p (i n) -> p i n", n=32)
        cs_p4 = cs_flat.rearrange("p (t h n) -> p t h n", t=NT, h=4)
        cs_max, cs_den = small[:, 816:832], small[:, 832:848]

        def per_row(a):
            return a.unsqueeze(2).broadcast_to([P, 16, 32])

        def per_tile(name):
            return const(name).rearrange("p (t n) -> p t n", t=NT).unsqueeze(2).broadcast_to([P, NT, 4, 32])

        norm_kv = Norm("norm_kv", mem_x, 2, EPS_B, "norm_mem_kv", scr[:, 1024:3072].rearrange("p (t d) -> p t d", t=2),
                       lambda t: (mem_loaded, 16))
        mem_kT, mem_v = part(25088, [2, 256]), part(25600, [2, 256])
        with nc.Block() as block:
            @block.tensor
            def _(pe):
                for i in range(16):
                    t, h = i // 4, i % 4
                    hp = (h % 2) * 64
                    at_s = (2 * t + h // 2) * 32
                    last = pe.matmul(ps[:, h % 2, at_s:at_s + 32], ft[hp:hp + 64, 4 + h // 2, t * P:(t + 1) * P],
                                     kc_T[hp:hp + 64, :], start=True, stop=True)
                last.then_inc(cs_scored, 1)
                pe.wait_ge(cs_shifted, 1)
                norm_kv.pe(pe)
                pe.wait_ge(cs_prob, 1)
                pe.wait_ge(norm_kv.out_lo, 5)
                for t in range(NT):
                    last = pe.transpose(ps[:, 4, t * P:(t + 1) * P], cs_flat[:, t * P:(t + 1) * P], ident)
                last.then_inc(cs_turned, 1)
                pe.wait_ge(cs_pT, 1)
                for t in range(NT):
                    last = pe.matmul(ps[:, 2 + t // 2, t % 2 * 256:(t % 2 + 1) * 256],
                                     cs_turned_p[:, t * P:(t + 1) * P], vc_diag, start=True, stop=True)
                    if t % 2:
                        last.then_inc(cs_valued, 1)

            @block.scalar
            def _(act):
                norm = norm_kv.act(act)
                next(norm)
                act.wait_ge(cs_shifted, 1)
                act.activation(cs_flat, cs_flat, ACT.Exp).then_inc(cs_exp, 1)
                for _ in norm:
                    pass
                act.wait_ge(cs_turned, 1)
                act.activation(cs_turned_p, ps[:, 4, :], ACT.Copy).then_inc(cs_pT, 1)

            @block.gpsimd
            def _(pool):
                norm_kv.pool(pool)

            @block.vector
            def _(dve):
                links = [0]

                def link(ins):
                    links[0] += 1
                    ins.then_inc(cs_chain, 1)
                    dve.wait_ge(cs_chain, links[0])

                dve.wait_ge(cs_scored, 1)
                for odd in range(2):
                    link(dve.tensor_tensor(cs_p4[:, :, odd::2, :],
                                           ps[:, odd, 0:256].rearrange("p (t h n) -> p t h n", t=NT, h=2),
                                           per_tile("cmp_neg")[:, :, 0:2, :], ALU.add))
                link(dve.tensor_reduce(cs_max, cs_p, AXX, ALU.max))
                dve.tensor_tensor(cs_p, cs_p, per_row(cs_max), ALU.subtract).then_inc(cs_shifted, 1)
                norm = norm_kv.dve(dve)
                next(norm)
                dve.wait_ge(cs_exp, 1)
                link(dve.tensor_tensor(cs_p4, cs_p4, per_tile("cmp01"), ALU.mult))
                link(dve.tensor_reduce(cs_den, cs_p, AXX, ALU.add))
                link(dve.tensor_scalar(cs_den, cs_den, 1e-30, None, ALU.max))
                link(dve.reciprocal(cs_den, cs_den))
                gate = tv[:, :, 452:464].rearrange("p t (h g) -> p t h g", g=3)[:, :, :, 0]
                den4 = cs_den.rearrange("p (t h) -> p t h", t=NT)
                link(dve.tensor_tensor(den4, den4, gate, ALU.mult))
                dve.tensor_tensor(cs_p, cs_p, per_row(cs_den), ALU.mult).then_inc(cs_prob, 1)
                for _ in norm:
                    pass
                for i in range(2):
                    dve.wait_ge(cs_valued, i + 1)
                    dve.tensor_copy(o_abc[:, 2 * i:2 * i + 2, 512:768],
                                    ps[:, 2 + i, :].rearrange("p (t d) -> p t d", t=2)).then_inc(cs_out, 1)

        units = []
        for j, (kt, vo) in enumerate(((8, 320), (9, 384))):
            for t in range(NT):
                w = (t + 1) * P
                for h in range(4):
                    hp = (h % 2) * 64
                    units.append(dict(q=[ft[hp:hp + 64, 4 + h // 2, t * P:(t + 1) * P]], k=[ft[hp:hp + 64, kt, 0:w]],
                                      w=w, mask=const("causal")[:, S - w:S], slope=1.0,
                                      v=[tv[:, b, vo:vo + 64] for b in range(t + 1)], dv=64,
                                      out=o_abc[:, t, 512 + h * 64:512 + (h + 1) * 64],
                                      gate=tv[:, t, 453 + j + 3 * h:454 + j + 3 * h], add=True))
        attend("swa", units, fill=Projection(
            "mem_kv", "mem_kv", [("F",)] * 2 + [("T", 256, 4)],
            [("act", "copy", mem_kT[:, 0, :], 1.0), ("dve", "copy", mem_kT[:, 1, :], 1.0),
             ("act", "copy", mem_v[:, 0, :], 1.0), ("dve", "copy", mem_v[:, 1, :], 1.0)],
            nt=2, banks=(6, 7), low="pool"))

        o_parts = halves("o_abc", ARENA, ARENA + 3072, 6)
        recycle()
        turn_o = Turn("om", lambda t, k: o_abc[:, t, k * P:(k + 1) * P],
                      lambda k: (o_parts[0][:, k, :], o_parts[1][:, k, :]), 6)
        up_done, up_gated, up_added, merged_hi, merged_lo = (
            sem(m) for m in ("up_done", "up_gated", "up_added", "merged_hi", "merged_lo"))
        m_sum = scr[:, 0:4096].rearrange("p (j s) -> p j s", j=8)
        m_new = part(6144, [4, S])
        class Up(Part):

            cuts, nk = 6, 8
            u0 = START["up"]
            out_lo = merged_lo

            def banks_read(self):
                return up_gated, 24

            def pe(self, pe):
                pe.wait_ge(turn_o.out_lo, 6)
                for i in range(24):
                    half, br, j = i // 12, i // 4 % 3, i % 4
                    if j == 0:
                        w = unit(pe, self.u0 + i // 4)
                    if i >= 8:
                        pe.wait_ge(up_gated, i - 7)
                    for k in range(2):
                        at_w = (2 * j + k) * P
                        a, z = product(pe, ps[:, i % 8, :], [v[:, at_w:at_w + P] for v in w],
                                       [v[:, 2 * br + k, :] for v in o_parts], k == 0, k == 1)
                        if j + k == 0:
                            a.then_inc(weights_used, 1)
                    z.then_inc(up_done, 1)

            def act(self, act):
                for f in range(1, 6):
                    cut_high(act, self.u0 + f)
                    if f == 4:
                        for j in range(4):
                            act.wait_ge(up_added, 5 + j)
                            act.activation(h_hi[:, j, :], m_sum[:, j, :], ACT.Copy).then_inc(merged_hi, 1)
                cut_high(act, self.u0 + 6)
                for j in range(4, 8):
                    act.wait_ge(up_added, 9 + j)
                    act.activation(h_hi[:, j, :], m_sum[:, j, :], ACT.Copy).then_inc(merged_hi, 1)

            def dve(self, dve):
                for i in range(24):
                    half, br, j = i // 12, i // 4 % 3, i % 4
                    tile = 4 * half + j
                    if j == 0 and i < 20:
                        cut_low(dve, self.u0 + i // 4 + 1)
                    dve.wait_ge(up_done, i + 1)
                    if i >= 8 and br:
                        dve.wait_ge(up_added, 8 * half + 4 * br - 8 + j + 1 if br == 2 else 8 * half - 4 + j + 1)
                    dve.tensor_tensor(m_new[:, j, :] if br else m_sum[:, tile, :], ps[:, i % 8, :],
                                      gm[:, 8 * br + tile, :], ALU.mult).then_inc(up_gated, 1)
                    if i >= 20:
                        self.low(dve, i - 20)
                cut_low(dve, self.u0 + 6)
                for j in range(4, 8):
                    self.low(dve, j)

            def low(self, dve, j):
                dve.wait_ge(merged_hi, j + 1)
                dve.tensor_tensor(h_lo[:, j, :], m_sum[:, j, :], h_hi[:, j, :].bitcast(F32), ALU.subtract)\
                   .then_inc(merged_lo, 1)

            def pool(self, pool):
                added = 0
                for i in range(24):
                    half, br, j = i // 12, i // 4 % 3, i % 4
                    if br == 0:
                        continue
                    tile = 4 * half + j
                    pool.wait_ge(up_gated, i + 1)
                    if br == 2:
                        pool.wait_ge(up_added, added - 3)
                    pool.tensor_tensor(m_sum[:, tile, :], m_sum[:, tile, :], m_new[:, j, :], ALU.add)\
                        .then_inc(up_added, 1)
                    added += 1

        up = Up()
        out_m = Combine("out_m", "out_m", lambda k: (h_hi[:, k, :], h_lo[:, k, :]), 8, before=up)

        mem_q, o_mem = part(11264, [2, S]), part(12288, [NT, 256])
        om_parts = halves("o_mem", ARENA + 13312, ARENA + 14336, 2)
        norm_q = Norm("norm_q", x, NT, EPS_B, "norm_mem_q", part(0, [NT, D]), out_m.ready)
        run(turn_o, up, out_m, norm_q, Projection("mem_q", "mem_q", [("F",)] * 2,
                [("act", "copy", mem_q[:, 0, :], 0.125), ("dve", "copy", mem_q[:, 1, :], 0.125)], norm=norm_q))
        units = []
        for h in range(4):
            hp = (h % 2) * 64
            for t in range(NT):
                units.append(dict(q=[mem_q[hp:hp + 64, h // 2, t * P:(t + 1) * P]], k=[mem_kT[hp:hp + 64, h // 2, :]],
                                  w=256, mask=None, slope=1.0, v=[mem_v[:, b, h * 64:(h + 1) * 64] for b in range(2)],
                                  dv=64, out=o_mem[:, t, h * 64:(h + 1) * 64]))
        attend("mem", units)
        turn_m = Turn("omem", lambda t, k: o_mem[:, t, k * P:(k + 1) * P],
                      lambda k: (om_parts[0][:, k, :], om_parts[1][:, k, :]), 2)
        mem_out = Combine("mem_out", "mem_out", lambda k: (om_parts[0][:, k, :], om_parts[1][:, k, :]), 2,
                          before=turn_m)

        norm_f = Norm("norm_f", x, NT, EPS_B, "norm_ffn", part(0, [NT, D]), mem_out.ready)
        ff = halves("ff", ARENA, ARENA + NFF * S, NFF)
        silu_of = scr[:, 0:1536].rearrange("p (i s) -> p i s", i=3)
        prod_of = scr[:, 1536:3072].rearrange("p (i s) -> p i s", i=3)

        class FeedForward(Part):
            done, silu, prod, hi, lo = (sem(m) for m in ("ff_done", "ff_silu", "ff_prod", "ff_hi", "ff_lo"))
            cuts = 2 * NFF
            u0 = START["ffn_in"]

            def pe(self, pe):
                for i in range(2 * NFF):
                    if i >= 8:
                        pe.wait_ge(self.silu if i % 2 == 0 else self.prod, (i - 8) // 2 + 1)
                    w = unit(pe, self.u0 + i)
                    for k in range(KD):
                        if i == 0:
                            pe.wait_ge(norm_f.out_lo, k + 1)
                        a, z = product(pe, ps[:, i % 8, :], [v[:, k * P:(k + 1) * P] for v in w],
                                       (h_hi[:, k, :], h_lo[:, k, :]), k == 0, k == KD - 1)
                        if k == 0:
                            a.then_inc(weights_used, 1)
                    z.then_inc(self.done, 1)

            def act(self, act):
                for j in range(NFF + 1):
                    if j < NFF:
                        cut_high(act, self.u0 + 2 * j + 1)
                        act.wait_ge(self.done, 2 * j + 1)
                        if j >= 3:
                            act.wait_ge(self.prod, j - 2)
                        act.activation(silu_of[:, j % 3, :], ps[:, 2 * j % 8, :], ACT.Silu).then_inc(self.silu, 1)
                        cut_high(act, self.u0 + 2 * j + 2)
                    if j:
                        act.wait_ge(self.prod, j)
                        act.activation(ff[0][:, j - 1, :], prod_of[:, (j - 1) % 3, :], ACT.Copy).then_inc(self.hi, 1)

            def dve(self, dve):
                for j in range(NFF + 1):
                    if j < NFF:
                        cut_low(dve, self.u0 + 2 * j + 1)
                        cut_low(dve, self.u0 + 2 * j + 2)
                        dve.wait_ge(self.done, 2 * j + 2)
                        dve.wait_ge(self.silu, j + 1)
                        if j >= 3:
                            dve.wait_ge(self.lo, j - 2)
                        dve.tensor_tensor(prod_of[:, j % 3, :], ps[:, (2 * j + 1) % 8, :], silu_of[:, j % 3, :],
                                          ALU.mult).then_inc(self.prod, 1)
                    if j:
                        dve.wait_ge(self.hi, j)
                        dve.tensor_tensor(ff[1][:, j - 1, :], prod_of[:, (j - 1) % 3, :],
                                          ff[0][:, j - 1, :].bitcast(F32), ALU.subtract).then_inc(self.lo, 1)

        run(turn_m, mem_out, norm_f, FeedForward())
        recycle()
        ffn_out = Combine("ffn_out", "ffn_out", lambda k: (ff[0][:, k, :], ff[1][:, k, :]), NFF)
        run(ffn_out, RowNorm("final_b", EPS_B, ffn_out.ready, store=True))


def tables():
    c = np.zeros((P, N_CONST), np.float32)
    i, j = np.arange(P)[:, None], np.arange(P)[None, :]

    def put(name, value):
        a, w = CONSTS[name]
        c[:, a:a + w] = value

    put("ident", i == j)
    put("tri_le", i <= j)
    put("tri_gt", i > j)
    put("neg_ge", -1.0 * (i >= j))
    put("neg_ones", -1.0)
    put("ones", 1.0)
    put("strict_neg", np.where(i < j, 0.0, NEG))
    put("strict01", i < j)
    u = np.arange(S)[None, :] - (S - P)
    put("alibi", np.where(u <= i, u - i, NEG))
    put("causal", np.where(u <= i, 0.0, NEG))
    d = i + P - np.arange(2 * P)[None, :]
    put("sw", np.where((d >= 0) & (d < P), -d, NEG))
    inv = np.float32(10000.0) ** (-np.arange(0, 64, 2, dtype=np.float32) / np.float32(64))
    ang = np.arange(S, dtype=np.float32)[None, :] * inv.astype(np.float32)[:, None]
    put("cos", np.tile(np.cos(ang), (4, 1)))
    put("sin", np.concatenate([-np.sin(ang), np.sin(ang)] * 2, 0))
    put("perm", (i // 32 ^ 1) * 32 + i % 32 == j)
    n = np.arange(32)[None, :]
    for t in range(NT):
        ok = (n < N_CMP) & (n * 16 + 31 <= t * P + i)
        a = CONSTS["cmp_neg"][0] + t * 32
        c[:, a:a + 32] = np.where(ok, 0.0, NEG)
        a = CONSTS["cmp01"][0] + t * 32
        c[:, a:a + 32] = ok
    return c


def kernel(**inputs):
    import concourse.bacc as bacc
    from concourse.bass_utils import run_bass_kernel_spmd

    a = {k: np.asarray(v, np.float32) for k, v in inputs.items()}

    stream = []

    def feature(w):
        for j in range(w.shape[1] // P):
            stream.append(w[:, j * P:(j + 1) * P].reshape(KD, P, P).transpose(1, 0, 2).reshape(P, UNIT))

    def chunk(w, n, bk):
        for j in range(w.shape[1] // n):
            for b in range(KD // bk):
                v = w[b * bk * P:(b + 1) * bk * P, j * n:(j + 1) * n].reshape(bk, P, n).transpose(1, 0, 2)
                stream.append(padded(v.reshape(P, bk * n)))

    def rows_of(w):
        for k in range(w.shape[0] // P):
            stream.append(w[k * P:(k + 1) * P, :])

    def padded(v):
        return v if v.shape[1] == UNIT else np.concatenate([v, np.zeros((P, UNIT - v.shape[1]), np.float32)], 1)

    w = a["w_in_a"][0]
    feature(w[:, 0:2048])
    chunk(w[:, 2048:3072], 512, 2)
    chunk(w[:, 4096:5120], 512, 2)
    feature(np.concatenate([w[:, 6656:6672], np.zeros((D, P - 16), np.float32)], 1))
    feature(w[:, 5120:6656])
    feature(w[:, 3072:4096])
    rows_of(a["w_out_a"][0])
    w = a["w_in_c"][0]
    feature(w[:, 0:1024])
    feature(np.concatenate([w[:, 1024:1088]] * 2 + [w[:, 1088:1152]] * 2, 1))
    chunk(w[:, 1152:1280], 128, 8)
    feature(w[:, 1280:2304])
    rows_of(a["w_out_c"][0])
    w = a["w_in_2"][0]
    names = ["q_a", 256, "k_a", 256, "v_a", 256, "q_b", 256, "k_b", 64, "v_b", 64, "q_idx", 256, "k_idx", 64,
             "w_idx", 4, "q_c", 256, "k_cmp", 64, "v_cmp", 64, "k_sel", 64, "v_sel", 64, "k_win", 64, "v_win", 64,
             "g_c", 12, "g_merge", 3072]
    p, at = {}, 0
    for name, n in zip(names[::2], names[1::2]):
        p[name] = w[:, at:at + n]
        at += n
    feature(np.concatenate([p["q_b"], p["q_idx"], p["q_c"]] + [p[n] for n in ("k_b", "k_idx", "k_sel", "k_win")
                                                              for _ in range(2)]
                           + [p["k_cmp"], p["v_cmp"], p["q_a"], p["k_a"]], 1))
    chunk(np.concatenate([p["v_a"], p["v_b"], p["v_sel"], p["v_win"], p["w_idx"], p["g_c"],
                          np.zeros((D, 48), np.float32)], 1), 512, 2)
    feature(p["g_merge"])
    w1 = [a[n][0].reshape(4, 8, 64, P).transpose(0, 2, 1, 3).reshape(4, 64, UNIT) for n in ("cmp_w1_k_2", "cmp_w1_v_2")]
    for q in range(4):
        stream.append(np.concatenate([w1[0][q], w1[1][q]], 0))
    kv = a["w_mem_kv_2"][0]
    feature(kv[:, 0:256])
    chunk(kv[:, 256:512], 256, 4)
    for half in range(2):
        for br in range(3):
            v = a["w_up_2"][0, br][:, half * 512:(half + 1) * 512].reshape(2, P, 4, P)
            stream.append(v.transpose(1, 2, 0, 3).reshape(P, UNIT))
    rows_of(a["w_out_2"][0])
    feature(a["w_mem_q_2"][0])
    rows_of(a["w_mem_o_2"][0])
    w = a["w_ffn_in_2"][0]
    for j in range(NFF):
        feature(w[:, j * P:(j + 1) * P])
        feature(w[:, FF + j * P:FF + (j + 1) * P])
    rows_of(a["w_ffn_out_2"][0])
    assert len(stream) == N_UNITS
    weights = np.ascontiguousarray(np.stack(stream))

    def tiles(v):
        return v.reshape(-1, P).T

    pos = np.concatenate([a["cmp_pos_k_2"][0].T, a["cmp_pos_v_2"][0].T], 0)
    conv_w = a["conv_w_a"][0].reshape(4, 12, P).transpose(2, 1, 0).reshape(P, 48)
    bc = a["b_in_c"][0]
    cols = np.ascontiguousarray(np.concatenate(
        [tiles(a["norm_a"][0]), tiles(a["norm_c"][0]), tiles(a["norm_mix_2"][0]), tiles(a["norm_mem_q_2"][0]),
         tiles(a["norm_mem_kv_2"][0]), tiles(a["norm_ffn_2"][0]), tiles(a["ssd_norm_a"][0]), tiles(a["subln_a"][0]),
         conv_w, tiles(a["conv_b_a"][0]), tiles(bc[0:1024]),
         tiles(np.concatenate([bc[1024:1088]] * 2 + [bc[1088:1152]] * 2)), pos,
         tiles(bc[1280:2304]), a["cmp_w2_k_2"][0], a["cmp_w2_k_2"][0], a["cmp_w2_v_2"][0]], 1))
    rows = np.ascontiguousarray(np.concatenate(
        [a["dt_bias_a"][0], a["a_log_a"][0], a["d_skip_a"][0], a["sinks_c"][0], a["lambda_q1_a"][0],
         a["lambda_k1_a"][0], a["lambda_q2_a"][0], a["lambda_k2_a"][0], bc[1152:1280]]))
    big = np.ascontiguousarray(np.stack([a["final_norm"], a["norm_final_2"]]))

    nc = bacc.Bacc("TRN2", target_bir_lowering=False, num_devices=1,
                   dynamic_dma_scratch_size=1024)
    arrays = {"weights": weights, "x_in": np.ascontiguousarray(a["x"][0]),
              "mem_in": np.ascontiguousarray(a["mem_2"][0]), "tables": tables(), "cols_in": cols, "rows_in": rows,
              "big_in": big}
    args = [nc.dram_tensor(n, v.shape, F32, kind="ExternalInput").ap() for n, v in arrays.items()]
    out = nc.dram_tensor("out", (S, D), F32, kind="ExternalOutput").ap()
    build(nc, *args, out)
    got = run_bass_kernel_spmd(nc, [arrays], core_ids=[0])
    return got.results[0]["out"].reshape(1, S, D)
```
